# Optimizing a Trainium2 kernel written in Bass

```python
import jax, jax.numpy as jnp
from jax import lax
import numpy as np

D_MODEL = 1024
BATCH = 1
SEQ = 128
DEPTH = 2
DEC_BATCH = 1
DEC_SEQ = 256
PAST_LEN = 128

GRID_W = 64
HEAD_DIM = 64
N_Q_HEADS = 8
N_KV_HEADS = 2
GROUP = N_Q_HEADS // N_KV_HEADS
ATT_W = N_Q_HEADS * HEAD_DIM
KV_W = N_KV_HEADS * HEAD_DIM
N_FREQ = HEAD_DIM // 4
ROPE_THETA = 10000.0
CONV_W = 512
POOL_W = 512
POOL_SIZES = (2, 4, 8, 16)
POOL_GROUPS = 4
POOL_GC = POOL_W // POOL_GROUPS
N_BRANCH = 4
BRANCH_W = 512
D_FF = -(-(8 * D_MODEL) // (3 * 256)) * 256
BLOCK = 128
WINDOW = 128
EPS = 1e-6
NEG = -1e30

kernel_name = "hybrid_diffusion_prefix_trunk_step"

def _rmsnorm(x, g):
    xf = x.astype(jnp.float32)
    y = xf * lax.rsqrt(jnp.mean(xf * xf, axis=-1, keepdims=True) + EPS)
    return (y * g.astype(jnp.float32)).astype(x.dtype)

def _rope_tables(T):
    rows = T // GRID_W
    row = jnp.repeat(jnp.arange(rows, dtype=jnp.float32), GRID_W)
    col = jnp.tile(jnp.arange(GRID_W, dtype=jnp.float32), rows)
    inv = 1.0 / (ROPE_THETA ** (jnp.arange(N_FREQ, dtype=jnp.float32) / N_FREQ))
    ang = jnp.stack([row[:, None] * inv, col[:, None] * inv], axis=1)
    return jnp.cos(ang)[:, None], jnp.sin(ang)[:, None]

def _rope(x, cos, sin):
    B, T, H, _ = x.shape
    xr = x.astype(jnp.float32).reshape(B, T, H, 2, 2, N_FREQ)
    x1, x2 = xr[..., 0, :], xr[..., 1, :]
    out = jnp.stack([x1 * cos - x2 * sin, x2 * cos + x1 * sin], axis=-2)
    return out.reshape(B, T, H, HEAD_DIM).astype(x.dtype)

def _attend(q, k, v, mask=None, sink=None):
    B, Tq = q.shape[:2]
    qg = q.reshape(B, Tq, N_KV_HEADS, GROUP, HEAD_DIM)
    s = jnp.einsum('bqkgd,bskd->bkgqs', qg, k, preferred_element_type=jnp.float32) * (HEAD_DIM ** -0.5)
    if mask is not None:
        s = jnp.where(mask, s, NEG)
    if sink is not None:
        sk = jnp.broadcast_to(sink.astype(jnp.float32).reshape(1, N_KV_HEADS, GROUP, 1, 1), s.shape[:-1] + (1,))
        p = jax.nn.softmax(jnp.concatenate([s, sk], axis=-1), axis=-1)[..., :-1]
    else:
        p = jax.nn.softmax(s, axis=-1)
    o = jnp.einsum('bkgqs,bskd->bqkgd', p.astype(v.dtype), v)
    return o.reshape(B, Tq, N_Q_HEADS * HEAD_DIM)

def _blocked(q, fn):
    B, T = q.shape[:2]
    nb = T // BLOCK
    qb = q.reshape((B, nb, BLOCK) + q.shape[2:]).swapaxes(0, 1)
    out = lax.map(lambda a: fn(a[0], a[1]), (jnp.arange(nb), qb))
    return out.swapaxes(0, 1).reshape(B, T, -1)

def _windowed(q, k, v, ck, cv, sink):
    B, T = q.shape[:2]
    S_c = ck.shape[1]
    pad = ((0, 0), (BLOCK, BLOCK), (0, 0), (0, 0))
    kp, vp = jnp.pad(k, pad), jnp.pad(v, pad)
    offs = jnp.arange(3 * BLOCK) - BLOCK
    qoff = jnp.arange(BLOCK)
    ctx_ok = jnp.ones((BLOCK, S_c), dtype=bool)

    def blk(i, qb):
        kb = lax.dynamic_slice_in_dim(kp, i * BLOCK, 3 * BLOCK, axis=1)
        vb = lax.dynamic_slice_in_dim(vp, i * BLOCK, 3 * BLOCK, axis=1)
        qpos = i * BLOCK + qoff
        kpos = i * BLOCK + offs
        band = (jnp.abs(qpos[:, None] - kpos[None, :]) <= WINDOW) & ((kpos >= 0) & (kpos < T))[None, :]
        mask = jnp.concatenate([ctx_ok, band], axis=1)
        return _attend(qb, jnp.concatenate([ck, kb], axis=1), jnp.concatenate([cv, vb], axis=1), mask, sink)

    return _blocked(q, blk)

def _short_conv(u, gb, gc, conv_w):
    z = gc * u
    T = z.shape[1]
    zp = jnp.pad(z, ((0, 0), (1, 1), (0, 0)))
    y = zp[:, :T] * conv_w[0] + zp[:, 1:T + 1] * conv_w[1] + zp[:, 2:] * conv_w[2]
    return gb * y

def _pool_mix(p, pool_w, pool_scale):
    B, T, _ = p.shape
    pf = p.astype(jnp.float32).reshape(B, T, POOL_GROUPS, POOL_GC)
    cs = jnp.concatenate([jnp.zeros((B, 1, POOL_GROUPS, POOL_GC), jnp.float32), jnp.cumsum(pf, axis=1)], axis=1)
    t = jnp.arange(T)
    means = []
    for g, w in enumerate(POOL_SIZES):
        lo = jnp.clip(t - w // 2, 0, T)
        hi = jnp.clip(t + w - w // 2, 0, T)
        means.append((cs[:, hi, g] - cs[:, lo, g]) / (hi - lo).astype(jnp.float32)[None, :, None])
    y = (jnp.stack(means, axis=2) - pf).astype(p.dtype)
    y = jnp.einsum('btgc,gce->btge', y, pool_w).reshape(B, T, POOL_W)
    return y * pool_scale

def _project(h, w_in, gq_a, gk_a, gq_c, gk_c):
    B, T, _ = h.shape
    sizes = [ATT_W, KV_W, KV_W, ATT_W, KV_W, KV_W, CONV_W, CONV_W, CONV_W, POOL_W, N_BRANCH * D_MODEL]
    idx = np.cumsum(sizes)[:-1].tolist()
    qa, ka, va, qc, kc, vc, u, gb, gc, pv, gl = jnp.split(h @ w_in, idx, axis=-1)
    heads = lambda t, n: t.reshape(B, T, n, HEAD_DIM)
    qa = _rmsnorm(heads(qa, N_Q_HEADS), gq_a)
    ka = _rmsnorm(heads(ka, N_KV_HEADS), gk_a)
    qc = _rmsnorm(heads(qc, N_Q_HEADS), gq_c)
    kc = _rmsnorm(heads(kc, N_KV_HEADS), gk_c)
    va = heads(va, N_KV_HEADS)
    vc = heads(vc, N_KV_HEADS)
    gates = jax.nn.sigmoid(gl.reshape(B, T, N_BRANCH, D_MODEL))
    return qa, ka, va, qc, kc, vc, u, gb, gc, pv, gates

def _layer(x, cond, prm, ctx):
    (w_mod, b_mod, g_mix, g_ffn, w_in, gq_a, gk_a, gq_c, gk_c, sink,
     conv_w, pool_w, pool_scale, w_br, w_o, w_gu, w_down) = prm
    T = x.shape[1]
    mod = jax.nn.silu(cond) @ w_mod + b_mod
    sh1, sc1, g1, sh2, sc2, g2 = [m[:, None, :] for m in jnp.split(mod, 6, axis=-1)]
    h = _rmsnorm(x, g_mix) * (1 + sc1) + sh1
    qa, ka, va, qc, kc, vc, u, gb, gc, pv, gates = _project(h, w_in, gq_a, gk_a, gq_c, gk_c)
    if ctx is None:
        new = (ka, va, kc, vc)
        att_a = _blocked(qa, lambda i, qb: _attend(qb, ka, va))
        att_c = _blocked(qc, lambda i, qb: _attend(qb, kc, vc, sink=sink))
    else:
        cka, cva, ckc, cvc = ctx
        cos, sin = _rope_tables(T)
        qa, ka, qc, kc = (_rope(t, cos, sin) for t in (qa, ka, qc, kc))
        k_all = jnp.concatenate([cka, ka], axis=1)
        v_all = jnp.concatenate([cva, va], axis=1)
        att_a = _blocked(qa, lambda i, qb: _attend(qb, k_all, v_all))
        att_c = _windowed(qc, kc, vc, ckc, cvc, sink)
        new = None
    conv = _short_conv(u, gb, gc, conv_w)
    pool = _pool_mix(pv, pool_w, pool_scale)
    br = jnp.stack([att_a, conv, att_c, pool], axis=2)
    proj = jnp.einsum('btkc,kcd->btkd', br, w_br)
    x = x + g1 * (jnp.sum(gates * proj, axis=2) @ w_o)
    h2 = _rmsnorm(x, g_ffn) * (1 + sc2) + sh2
    a, b = jnp.split(h2 @ w_gu, 2, axis=-1)
    x = x + g2 * ((jax.nn.silu(a) * b) @ w_down)
    return x, new

def setup_inputs(seed: int = 0) -> dict:
    key = jax.random.key(seed)
    ks = jax.random.split(key, 32)
    n = lambda k, s, sc: jax.random.normal(k, s, jnp.float32) * sc
    n_in = 2 * ATT_W + 4 * KV_W + 3 * CONV_W + POOL_W + N_BRANCH * D_MODEL
    cshape = (DEC_BATCH, DEPTH, PAST_LEN, N_KV_HEADS, HEAD_DIM)
    return {
        'x_prompt': n(ks[0], (BATCH, SEQ, D_MODEL), 1.0),
        'x_sample': n(ks[1], (DEC_BATCH, DEC_SEQ, D_MODEL), 1.0),
        'cache_k_attn': n(ks[2], cshape, 1.0),
        'cache_v_attn': n(ks[3], cshape, 1.0),
        'cache_k_win': n(ks[4], cshape, 1.0),
        'cache_v_win': n(ks[5], cshape, 1.0),
        'c': n(ks[6], (DEC_BATCH, D_MODEL), 1.0),
        'c_ctx': n(ks[7], (D_MODEL,), 1.0),
        'w_mod': n(ks[8], (DEPTH, D_MODEL, 6 * D_MODEL), 0.5 * D_MODEL ** -0.5),
        'b_mod': n(ks[9], (DEPTH, 6 * D_MODEL), 0.01),
        'g_mix': 1.0 + n(ks[10], (DEPTH, D_MODEL), 0.02),
        'g_ffn': 1.0 + n(ks[11], (DEPTH, D_MODEL), 0.02),
        'w_in': n(ks[12], (DEPTH, D_MODEL, n_in), D_MODEL ** -0.5),
        'gq_attn': 1.0 + n(ks[13], (DEPTH, HEAD_DIM), 0.02),
        'gk_attn': 1.0 + n(ks[14], (DEPTH, HEAD_DIM), 0.02),
        'gq_win': 1.0 + n(ks[15], (DEPTH, HEAD_DIM), 0.02),
        'gk_win': 1.0 + n(ks[16], (DEPTH, HEAD_DIM), 0.02),
        'sink_win': n(ks[17], (DEPTH, N_Q_HEADS), 0.5),
        'conv_w': n(ks[18], (DEPTH, 3, CONV_W), 3 ** -0.5),
        'pool_w': n(ks[19], (DEPTH, POOL_GROUPS, POOL_GC, POOL_GC), POOL_GC ** -0.5),
        'pool_scale': 1.0 + n(ks[20], (DEPTH, POOL_W), 0.1),
        'w_branch': n(ks[21], (DEPTH, N_BRANCH, BRANCH_W, D_MODEL), BRANCH_W ** -0.5),
        'w_out': n(ks[22], (DEPTH, D_MODEL, D_MODEL), D_MODEL ** -0.5),
        'w_gate_up': n(ks[23], (DEPTH, D_MODEL, 2 * D_FF), D_MODEL ** -0.5),
        'w_down': n(ks[24], (DEPTH, D_FF, D_MODEL), D_FF ** -0.5),
    }

def reference(x_prompt, x_sample, cache_k_attn, cache_v_attn, cache_k_win, cache_v_win, c, c_ctx,
              w_mod, b_mod, g_mix, g_ffn, w_in, gq_attn, gk_attn, gq_win, gk_win, sink_win,
              conv_w, pool_w, pool_scale, w_branch, w_out, w_gate_up, w_down):
    cond_ctx = jnp.broadcast_to(c_ctx, (x_prompt.shape[0], c_ctx.shape[0]))
    xp, xs = x_prompt, x_sample
    ka_l, va_l, kc_l, vc_l = [], [], [], []
    for l in range(DEPTH):
        prm = (w_mod[l], b_mod[l], g_mix[l], g_ffn[l], w_in[l], gq_attn[l], gk_attn[l],
               gq_win[l], gk_win[l], sink_win[l], conv_w[l], pool_w[l], pool_scale[l],
               w_branch[l], w_out[l], w_gate_up[l], w_down[l])
        xp, (ka, va, kc, vc) = _layer(xp, cond_ctx, prm, None)
        ka_l.append(ka)
        va_l.append(va)
        kc_l.append(kc)
        vc_l.append(vc)
        ctx = (cache_k_attn[:, l], cache_v_attn[:, l], cache_k_win[:, l], cache_v_win[:, l])
        xs, _ = _layer(xs, c, prm, ctx)
    k_attn = jnp.stack(ka_l, axis=1)
    v_attn = jnp.stack(va_l, axis=1)
    k_win = jnp.stack(kc_l, axis=1)
    v_win = jnp.stack(vc_l, axis=1)
    return (xp, xs, k_attn, v_attn, k_win, v_win)


_drawn_inputs = setup_inputs


def setup_inputs(seed=0):
    import zlib

    import numpy as np

    out = dict(_drawn_inputs(seed))
    spreads = {}
    factors = {'cache_k_attn': 6.536,
     'cache_v_attn': 5.238,
     'cache_k_win': 5.266,
     'cache_v_win': 4.307,
     'b_mod': 3.164,
     'g_mix': 2.835,
     'g_ffn': 7.342,
     'gq_attn': 8.0,
     'gk_attn': 2.848,
     'gq_win': 8.0,
     'gk_win': 2.725,
     'sink_win': 8.0,
     'pool_scale': 2.87}
    for name, (base, spread) in spreads.items():
        noise = np.random.default_rng([zlib.crc32(name.encode()), seed]).standard_normal(out[name].shape)
        drawn = base * np.exp(spread * noise) if base else spread * noise
        out[name] = __import__('jax').numpy.asarray(drawn.astype(out[name].dtype))
    for name, factor in factors.items():
        out[name] = (out[name] * factor).astype(out[name].dtype)
    return out
```

```python
from contextlib import ExitStack

import numpy as np

import concourse.bass as bass
import concourse.mybir as mybir

P = 128
F32 = mybir.dt.float32
F32R = mybir.dt.float32r
ALU = mybir.AluOpType
ACT = mybir.ActivationFunctionType
AXX = mybir.AxisListType.X

DEPTH = 2
D = 1024
DC = D // P
T_LAT, T_CTX = 256, 128
T = T_LAT + T_CTX
TT = T // P
PAST = 128
HD = 64
NQ, NKV = 8, 2
QW, KVW = NQ * HD, NKV * HD
GRID_W = 64
N_FREQ = HD // 4
ROPE_THETA = 10000.0
CW = 512
CC = CW // P
POOL_SIZES = (2, 4, 8, 16)
D_FF = -(-(8 * D) // (3 * 256)) * 256
FC = D_FF // P
EPS = 1e-6
NEG = -1e30
SCALE = HD ** -0.5

C_QA, C_KVA = 0, QW
C_QC, C_KVC = QW + 2 * KVW, 2 * QW + 2 * KVW
C_U = 2 * QW + 4 * KVW
C_GB, C_GC, C_PV = C_U + CW, C_U + 2 * CW, C_U + 3 * CW
C_GL = C_U + 4 * CW

LOOKAHEAD = 3
RING = 4
SLAB = 2048
LAT, CTX = slice(0, T_LAT), slice(T_LAT, T)

V_BMOD, V_GMIX, V_GFFN, V_CONV, V_PSC, V_GAIN = 0, 48, 56, 64, 76, 80
NV = 84
NVX = NV + 4
M_SH1, M_SC1, M_G1, M_SH2, M_SC2, M_G2 = range(0, 48, 8)

K_ID, K_PERM, K_MASK, K_COS, K_SIN = 0, 128, 256, 512, 768
K_HEAD, K_SEL, K_MEAN, K_EDGE = 1024, 1026, 1028, 1029
NK = 1029 + 128


def constants():
    k = np.zeros((P, NK), np.float32)
    p = np.arange(P)
    k[p, K_ID + p] = 1.0
    k[p, K_PERM + (p ^ N_FREQ)] = 1.0
    a, b = np.meshgrid(p, p, indexing="ij")
    k[:, K_MASK:K_MASK + P] = np.where(b <= a, 0.0, NEG)
    k[:, K_MASK + P:K_MASK + 2 * P] = np.where(a <= b, 0.0, NEG)
    t = np.arange(T_LAT)
    pos = np.stack([t // GRID_W, t % GRID_W]).astype(np.float32)
    inv = (1.0 / (np.float32(ROPE_THETA) ** (np.arange(N_FREQ, dtype=np.float32) / N_FREQ))).astype(np.float32)
    ang = (pos[(p % HD) // 32] * inv[p % N_FREQ][:, None]).astype(np.float32)
    sign = np.where((p // N_FREQ) % 2 == 0, -1.0, 1.0)[:, None]
    k[:, K_COS:K_COS + T_LAT] = np.cos(ang)
    k[:, K_SIN:K_SIN + T_LAT] = np.sin(ang) * sign
    k[p, K_HEAD + p // HD] = 1.0 / HD
    for j in range(4):
        for c in range(2):
            k[32 * j + c, K_SEL + c] = 1.0
    k[:, K_MEAN] = 1.0 / D
    edge = np.ones((4, 4, 8), np.float32)
    for g, w in enumerate(POOL_SIZES):
        for s, n in enumerate((T_LAT, T_CTX)):
            for e, first in enumerate((0, n - 8)):
                i = np.arange(first, first + 8)
                cnt = np.clip(i + w - w // 2, 0, n) - np.clip(i - w // 2, 0, n)
                edge[g, 2 * s + e] = w / cnt
    k[:, K_EDGE:K_EDGE + 128] = edge.reshape(1, 128)
    return k


def plan():
    units, slab_of = [], []

    def add(kind, indices, K, slab):
        slab_of.append(slab)
        for j, i in enumerate(indices):
            units.append(dict(kind=kind[j] if isinstance(kind, tuple) else kind, i=i, K=K,
                              part=j, slab=len(slab_of) - 1, shape=slab[0]))

    for m, c0 in enumerate((C_KVA, C_KVC)):
        add(("norm", "v"), (m, m), DC, ("in", c0))
    for m, c0 in enumerate((C_QA, C_QC)):
        for s in range(2):
            add("norm", (2 + 4 * m + 2 * s, 3 + 4 * m + 2 * s), DC, ("pair", c0 + P * s))
    for s in range(2):
        for kind, c0 in (("u", C_U), ("gb", C_GB), ("gc", C_GC), ("pv", C_PV)):
            add(kind, (2 * s, 2 * s + 1), DC, ("in", c0 + 2 * P * s))
    for b, branch in enumerate((1, 3, 0, 2)):
        for half in range(2):
            for s in (2 * half, 2 * half + 1):
                add("gate", (8 * b + 2 * s, 8 * b + 2 * s + 1), DC, ("in", C_GL + branch * D + 2 * P * s))
            for d in (4 * half, 4 * half + 2):
                add("proj", (8 * b + d, 8 * b + d + 1), 4, ("heads" if b > 1 else "branch", branch, P * d))
    for s in range(4):
        add("out", (2 * s, 2 * s + 1), DC, ("out", s))
    for s in range(FC // 2):
        add("a", (2 * s, 2 * s + 1), DC, ("gu", 2 * P * s))
        add("b", (2 * s, 2 * s + 1), DC, ("gu", D_FF + 2 * P * s))
    for s in range(4):
        k0 = 0
        for q, K in enumerate((6, 6, 5, 5)):
            add("down", (2 * s, 2 * s + 1), K, ("down", s, k0, K))
            for u in units[-2:]:
                u.update(k0=k0, first=q == 0, last=q == 3)
            k0 += K
    base = {}
    for n, u in enumerate(units):
        base.setdefault(u["kind"], n)
    U = len(units)

    hooks = [[] for _ in range(U)]
    for n, u in enumerate(units[:12]):
        if u["kind"] == "norm":
            hooks[n + 2].append(("rnorm", u["i"]))
            hooks[n + 1].append(("stat", u["i"]))
        else:
            hooks[n + 1].append(("vt", u["i"]))
    hooks[4].append(("kout", 0))
    hooks[6].append(("kout", 1))
    hooks[7].append(("cache", 0))
    hooks[9].append(("cache", 1))
    P0, G0 = base["u"], base["gate"]
    for n in range(P0, G0):
        if units[n]["kind"] == "gc":
            hooks[n + 1].append(("conv", units[n]["i"]))
        if units[n]["kind"] == "pv":
            hooks[n + 1].append(("pool", units[n]["i"]))
            hooks[n + 2].append(("poolsplit", units[n]["i"]))
    steps = []
    for k in range(50):
        now = []
        if k % 2 == 0:
            j = k // 2
            now += [("probsT", j - 1)] if 0 < j <= 24 else []
            now += [("scores", j)] if j < 24 else []
        else:
            j = (k - 1) // 2
            now += [("attn", j - 1)] if j >= 1 else []
            now += [("scale", j)] if j < 24 else []
        steps.append(now)
    n_attn = range(P0, base["gate"] + 32)
    weight = sum(units[n]["K"] for n in n_attn)
    done = k = 0
    for n in n_attn:
        done += units[n]["K"]
        while k < len(steps) and (k + 0.5) * weight / len(steps) <= done:
            hooks[n].extend(steps[k])
            k += 1
    assert k == len(steps)
    AC = G0 + 32
    for x, at in enumerate((3, 5, 8, 10, 12, 14)):
        hooks[AC + at - 2].insert(0, ("load", x))
        hooks[AC + at].append(("mod", x))
        hooks[AC + at + 1].insert(0, ("sel", x))
    F = base["a"] + 4
    hooks[F] += [("load", 12), ("load_next", 0)]
    hooks[F + 3] += [("mod", 12), ("mod_next", 0), ("load_next", 1)]
    hooks[F + 5] += [("sel", 12), ("sel_next", 0), ("mod_next", 1)]
    hooks[F + 7] += [("sel_next", 1)]
    last_unit = {}
    for n, u in enumerate(units):
        last_unit[u["slab"]] = n
    return units, slab_of, hooks, base, last_unit


UNITS, SLABS, HOOKS, BASE, LAST_UNIT = plan()
U, S = len(UNITS), len(SLABS)
N_Q, N_P, N_G = 0, BASE["u"], BASE["gate"]
N_AC, N_O = N_G + 32, BASE["out"]
N_F, N_D = BASE["a"], BASE["down"]
assert U % RING == 0 and S % RING == 0


class Signal:

    def __init__(self, sem, per_layer, before=0, step=1):
        self.sem, self.per_layer, self.before, self.step = sem, per_layer, before, step

    def __call__(self, l, k):
        return self.sem, (l * self.per_layer + (k + self.before + 1)) * self.step


class Steps:

    def __init__(self, sem, sizes, name):
        self.sem, self.sizes, self.name = sem, sizes, name
        self.offset, self.n, self.marks = 0, 0, []

    def made(self, instruction):
        instruction.then_inc(self.sem, 1)
        self.n += 1
        return self.sem, self.offset + self.n

    def enter(self, what, i):
        self.marks.append((what, self.n, self.offset))
        self.offset = self.offset + i * self.sizes.get((self.name, what), 1)

    def leave(self, times):
        what, n, offset = self.marks.pop()
        size = self.n - n
        self.sizes[(self.name, what)] = size
        self.offset, self.n = offset, n + size * times


def program(nc, io, sizes):
    with ExitStack() as ctx:
        base = (nc.sbuf_base + 63) // 64 * 64
        top = base

        def place(name, shape, dt=F32, at=None):
            nonlocal top
            size = 4 * int(np.prod(shape[1:]))
            size = (size + 31) // 32 * 32
            if at is None:
                at, top = top, top + size
            place.end = at + size
            return nc.alloc_sbuf_tensor_at(name, shape, dt, offset=at)

        raw = place("raw", [P, RING, SLAB])
        w_hi = place("w_hi", [P, RING, DC * P], F32R)
        w_lo = place("w_lo", [P, RING, DC * P], F32R)
        x = place("x", [P, DC, T])
        h_hi = place("h_hi", [P, DC, T], F32R)
        h_lo = place("h_lo", [P, DC, T], F32R)
        G = top
        f_hi = place("f_hi", [P, FC, T], F32R)
        f_lo = place("f_lo", [P, FC, T], F32R)
        br_hi = place("br_hi", [P, 16, T], F32R, at=G)
        br_lo = place("br_lo", [P, 16, T], F32R, at=G + 16 * T * 4)
        Z = G + 2 * 16 * T * 4
        merged = place("merged", [P, DC, T], at=Z)
        gate_t = place("gate_t", [P, 4, T], at=Z + DC * T * 4)
        assert place.end <= top
        Q1, Q2 = G + 8 * T * 4, G + 24 * T * 4
        q_sq = place("q_sq", [P, 2, T], at=Q1)
        q_raw = place("q_raw", [P, 3, T], at=place.end)
        q_rot = place("q_rot", [P, T_LAT], at=place.end)
        pw = place("pw", [P, CC, P], at=place.end)
        assert place.end <= Q1 + 8 * T * 4
        v_t = place("v_t", [P, 2, T], at=Q2)
        q_mix = place("q_mix", [P, 2, T], at=place.end)
        k_past = place("k_past", [P, 2, KVW], at=place.end)
        k_out = place("k_out", [P, 2, KVW], at=place.end)
        assert place.end <= Q2 + 8 * T * 4
        ZL = 1 + T_LAT + 1 + T_CTX + 1
        PL = 16 + T_LAT + 16 + T_CTX + 16
        cu = place("cu", [P, 2, T], at=Z)
        cgb = place("cgb", [P, 2, T], at=place.end)
        cz = place("cz", [P, ZL], at=place.end)
        cy = place("cy", [P, 2, ZL - 1], at=place.end)
        pin = place("pin", [P, 2, PL], at=place.end)
        ps_a = place("ps_a", [P, PL], at=place.end)
        ps_b = place("ps_b", [P, PL], at=place.end)
        assert place.end <= top, (place.end, top)
        nx = place("nx", [P, 4, T], at=Z)
        nf = place("nf", [P, 4, T], at=place.end)
        tok = place("tok", [P, TT, D], at=G)
        vec_raw = place("vec_raw", [NV, DEPTH, P], at=G + TT * D * 4)
        c_raw = place("c_raw", [2 * DC, P], at=place.end)
        start_w = place("start_w", [P, 4, SLAB], at=place.end)
        assert place.end <= Z
        q_at = top
        q = place("q", [P, 8, T])
        x_sq = place("x_sq", [P, 2, T], at=q_at)
        x_acc = place("x_acc", [P, T], at=place.end)
        keys = place("keys", [P, 2, PAST + T])
        vals = place("vals", [P, 2, 1 + TT, KVW])
        A0 = top
        prob = place("prob", [P, 2, 2, PAST + T_LAT])
        prob_t = place("prob_t", [P, 2, 2, 3, P])
        mod_w = place("mod_w", [P, 2, SLAB], at=q_at + 3 * T * 4)
        next_row = place("next_row", [P, 2, 2 * P], at=place.end)
        ff_t = place("ff_t", [P, 2, T], at=place.end)
        ff_s = place("ff_s", [P, 2, T], at=place.end)
        ff_f = place("ff_f", [P, 2, T], at=place.end)
        assert place.end <= top
        const = place("const", [P, NK])
        cond = place("cond", [P, DC, 32])
        cond_t = place("cond_t", [P, 2, 2 * DC], at=A0 + 4096)
        vec_all = place("vec_all", [P, DEPTH, NVX])
        vec = place("vec", [P, NVX])
        modc = place("modc", [P, 48, 2])
        gain = place("gain", [P, 2, DC, 2])
        mod_row = place("mod_row", [P, 2, 2 * P])
        sink = place("sink", [P, DEPTH, NQ])
        nsink = place("nsink", [P, NQ])
        st = place("st", [P, 64])
        exponent = place("exponent", [P, 1])
        assert top <= nc.sbuf_usable_end, (top, nc.sbuf_usable_end)
        x_ms, x_rs = st[:, 0:3], st[:, 4:7]
        q_ms, q_rs = [st[:, 8 + 8 * i:14 + 8 * i] for i in range(2)], [st[:, 24 + 8 * i:30 + 8 * i] for i in range(2)]
        s_max, s_nm, s_sum = st[:, 40:42], [st[:, 42 + 2 * i:44 + 2 * i] for i in range(2)], [st[:, 46 + 2 * i:48 + 2 * i] for i in range(2)]
        s_sd, s_se, s_r = st[:, 50:52], st[:, 52:54], st[:, 54:56]
        ident = const[:, K_ID:K_ID + P]

        def psum(name, shape):
            return ctx.enter_context(nc.psum_tensor(name, shape, F32))

        bank = psum("bank", [P, RING, 512])
        sc = psum("sc", [P, 2, 512])
        tr = psum("tr", [P, 2, 512])

        def signal(name, per_layer, before=0, step=1):
            return Signal(ctx.enter_context(nc.semaphore(name)), per_layer, before, step)

        slab_in = [signal(f"slab_in{s}", S // RING, step=32) for s in range(RING)]
        start_in = [signal(f"start_in{s}", 0, step=32) for s in range(6)]
        mod_in = [signal(f"mod_in{s}", (10, 6)[s], step=32) for s in range(2)]
        next_in = signal("next_in", 8, step=32)
        unit_done = signal("unit_done", U, before=RING)
        x_stat = signal("x_stat", 2)
        x_bcast = signal("x_bcast", 2)
        q_stat = signal("q_stat", 10)
        q_bcast = signal("q_bcast", 10)
        v_turned = signal("v_turned", 2)
        k_turned = signal("k_turned", 2)
        past_turned = signal("past_turned", 2)
        scores = signal("scores", 24)
        probs_turned = signal("probs_turned", 24)
        attn_out = signal("attn_out", 24)
        mod_sum = signal("mod_sum", 16)
        mod_col = signal("mod_col", 16)
        next_sum = signal("next_sum", 8, before=8)
        next_col = signal("next_col", 8, before=8)
        pooled = signal("pooled", 4)
        turned = signal("turned", 0)
        hi_ready = signal("hi_ready", U)
        h_full = signal("h_full", 16)
        h_hi_ready = signal("h_hi_ready", 16)
        q_copied = signal("q_copied", 10)
        v_copied = signal("v_copied", 2)
        k_out_ready = signal("k_out_ready", 2)
        past_ready = signal("past_ready", 2)
        exps = signal("exps", 24)
        sink_exp = signal("sink_exp", 12)
        probs_t_ready = signal("probs_t_ready", 24)
        attn_hi = signal("attn_hi", 24)
        mod_row_ready = signal("mod_row_ready", 16)
        next_row_ready = signal("next_row_ready", 8, before=8)
        conv_in = signal("conv_in", 8)
        pool_in = signal("pool_in", 4)
        conv_hi = signal("conv_hi", 4)
        pool_hi = signal("pool_hi", 4)
        gate_ready = signal("gate_ready", 32)
        merged_hi = signal("merged_hi", 8)
        x_squared = signal("x_squared", 16, before=8)
        ff_tanh = signal("ff_tanh", FC)
        ff_hi = signal("ff_hi", FC)
        cond_tanh = signal("cond_tanh", 0)
        lo_ready = signal("lo_ready", U, before=8)
        vec_ready = signal("vec_ready", 1)
        x_ms_ready = signal("x_ms_ready", 2)
        x_normed = signal("x_normed", 16)
        h_ready = signal("h_ready", 16)
        q_ms_ready = signal("q_ms_ready", 10)
        q_mixed = signal("q_mixed", 10)
        qk_ready = signal("qk_ready", 10)
        v_ready = signal("v_ready", 2)
        max_ready = signal("max_ready", 24)
        probs_ready = signal("probs_ready", 24)
        attn_ready = signal("attn_ready", 24)
        mod_ready = signal("mod_ready", 16)
        next_ready = signal("next_ready", 8, before=8)
        gain_ready = signal("gain_ready", 2)
        conv_ready = signal("conv_ready", 4)
        conv_split = signal("conv_split", 4)
        pool_ready = signal("pool_ready", 4)
        pool_split = signal("pool_split", 4)
        merge_done = signal("merge_done", 32)
        merged_split = signal("merged_split", 8)
        x_ready = signal("x_ready", 16, before=8)
        ff_prod = signal("ff_prod", FC)
        ff_split = signal("ff_split", FC)
        evicted = signal("evicted", 0)
        cond_ready = signal("cond_ready", 0)
        dve_step = ctx.enter_context(nc.semaphore("dve_step"))
        x_rs_ready = signal("x_rs_ready", 2)
        q_rs_ready = signal("q_rs_ready", 10)
        x_summed = signal("x_summed", 16, before=8)
        pads_zeroed = signal("pads_zeroed", 2)
        pool_step = ctx.enter_context(nc.semaphore("pool_step"))
        loaded = signal("loaded", 0, step=16)
        vectors_in = signal("vectors_in", 0, step=16)
        tok_in = signal("tok_in", 0, step=16)
        past_in = signal("past_in", 1, step=16 * 2)
        vals_in = signal("vals_in", 1, step=16 * 2)
        pw_in = signal("pw_in", 1, step=16)
        kv_stored = signal("kv_stored", 1, step=16 * 4)
        y_stored = signal("y_stored", 0, step=16)

        block = ctx.enter_context(nc.Block())

        def load_vector(engine, k):
            rows = [
                (V_BMOD, 48, io["b_mod"]), (V_GMIX, 8, io["g_mix"]), (V_GFFN, 8, io["g_ffn"]),
                (V_CONV, 12, io["conv_w"]), (V_PSC, 4, io["pool_scale"]),
            ]
            if k < 5:
                r, n, src = rows[k]
                src = src.rearrange("l a (k p) -> (a k) l p", p=P) if k == 3 else src.rearrange("l (k p) -> k l p", p=P)
                engine.dma_start(vec_raw[r:r + n, :, :], src).then_inc(vectors_in.sem, 16)
            elif k < 9:
                g = k - 5
                src = io[("gq_attn", "gk_attn", "gq_win", "gk_win")[g]].unsqueeze(1).unsqueeze(0)
                engine.dma_start(vec_raw[V_GAIN + g:V_GAIN + g + 1, :, :].rearrange("a l (r c) -> a l r c", r=2),
                                 src.broadcast_to([1, DEPTH, 2, HD])).then_inc(vectors_in.sem, 16)
            else:
                src = io["sink_win"].rearrange("l h -> (l h)").unsqueeze(0)
                engine.dma_start(sink[:, :, :].rearrange("p l h -> p (l h)"), src.broadcast_to([P, DEPTH * NQ]))\
                    .then_inc(vectors_in.sem, 16)

        next_bank = [sc[:, 1, :], tr[:, 1, :]]
        start_bank = [tr[:, 0, :], tr[:, 1, :], sc[:, 0, :], sc[:, 1, :]]

        def mod_index(i, it):
            return i + it * 6 if i < 12 else 12 + it

        def mod_load_index(i, it):
            return i // 2 + it * 3 if i < 12 else 6 + it

        def run_hooks(engine, l, n, it, hook, takes):
            hooks = HOOKS[n]
            for what, i in hooks:
                if not what.endswith("_next"):
                    hook(l, what, i, it)
            following = [h for h in hooks if h[0] in takes]
            if following:
                with engine.If(l < DEPTH - 1):
                    for what, i in following:
                        hook(l, what, i, it)

        def load_mod(engine, w, l, columns, done):
            src = io["w_mod"][l].rearrange("(k p) c -> p k c", p=P)
            to = w.rearrange("p (k c) -> p k c", k=DC)
            for k in (slice(4, 8), slice(0, 4)):
                engine.dma_start(to[:, k, :], src[:, k, columns]).then_inc(done, 16)

        def weights_of(n, to):
            u = UNITS[n]
            K, j, slot = u["K"], u["part"], u["slab"] % RING
            if u["shape"] == "pair":
                dst = to[:, n % RING, :].rearrange("p (k g c) -> p k g c", k=DC, g=2)
                return dst, raw[:, slot, :].rearrange("p (k g i c) -> p k g i c", k=DC, g=2, i=2)[:, :, :, j, :]
            dst = to[:, n % RING, 0:K * P].rearrange("p (k c) -> p k c", k=K)
            return dst, raw[:, slot, 0:K * 2 * P].rearrange("p (k c) -> p k c", k=K)[:, :, P * j:P * j + P]

        @block.sync
        def _(sp):
            def slab(l, s, it=0, per=0):
                slot = s % RING
                before, wrap = (s - RING) % S, U if s < RING else 0
                sp.wait_ge(*lo_ready(l, LAST_UNIT[before] - wrap + it * (2 * per)))
                dst, done = raw[:, slot, :], slab_in[slot].sem

                def load(to, rows):
                    sp.dma_start(to, rows).then_inc(done, 16)

                def columns(w, c0, n=256, K=DC, r0=0):
                    to = dst[:, 0:K * n].rearrange("p (k c) -> p k c", k=K)
                    a = w.rearrange("(k p) c -> p k c", p=P)[:, r0:r0 + K, c0 if isinstance(c0, slice) else slice(c0, c0 + n)]
                    load(to[:, 0:K // 2, :], a[:, 0:K // 2, :])
                    load(to[:, K // 2:K, :], a[:, K // 2:K, :])

                what = SLABS[s]
                if what[0] == "in":
                    c0 = bass.ds(what[1] + it * (2 * D), 256) if per else what[1]
                    w = io["w_in"][l].rearrange("(k p) c -> p k c", p=P)
                    to = dst.rearrange("p (k c) -> p k c", k=DC)
                    c = c0 if per else slice(c0, c0 + 256)
                    load(to[:, 0:4, :], w[:, 0:4, c])
                    load(to[:, 4:8, :], w[:, 4:8, c])
                elif what[0] == "pair":
                    w = io["w_in"][l].rearrange("(k p) c -> p k c", p=P)
                    to = dst.rearrange("p (k g c) -> p k g c", k=DC, g=2)
                    for g in (1, 0):
                        load(to[:, :, g, :], w[:, :, what[1] + 256 * g:what[1] + 256 * g + P])
                elif what[0] in ("branch", "heads"):
                    _, branch, c0 = what
                    to = dst[:, 0:4 * 256].rearrange("p (k c) -> p k c", k=4)
                    c = slice(c0, c0 + 256)
                    if what[0] == "branch":
                        w = io["w_branch"][l, branch].rearrange("(k p) c -> p k c", p=P)
                        load(to[:, 0:2, :], w[:, 0:2, c])
                        load(to[:, 2:4, :], w[:, 2:4, c])
                    else:
                        w = io["w_branch"][l, 2 * it].rearrange("(g i p) c -> g p i c", g=2, i=4)
                        for g in range(2):
                            load(to[64 * g:64 * g + 64, :, :], w[g, :, :, c])
                elif what[0] == "out":
                    columns(io["w_out"][l], 256 * what[1])
                elif what[0] == "gu":
                    w = io["w_gate_up"][l].rearrange("(k p) c -> p k c", p=P)
                    to = dst.rearrange("p (k c) -> p k c", k=DC)
                    c = bass.ds(what[1] + it * 512, 256) if per else slice(what[1], what[1] + 256)
                    load(to[:, 0:4, :], w[:, 0:4, c])
                    load(to[:, 4:8, :], w[:, 4:8, c])
                else:
                    _, s4, k0, K = what
                    columns(io["w_down"][l], 256 * s4, K=K, r0=k0)

            sp.dma_start(const[:, :], io["const"]).then_inc(loaded.sem, 16)
            sp.dma_start(c_raw[0:DC, :], io["c"].rearrange("a (k p) -> (a k) p", p=P)).then_inc(loaded.sem, 16)
            sp.dma_start(c_raw[DC:2 * DC, :], io["c_ctx"].rearrange("(k p) -> k p", p=P)).then_inc(loaded.sem, 16)
            for g in range(8):
                if g >= 6:
                    sp.wait_ge(*next_sum(0, g - 6 - 8))
                w = start_w[:, g % 6, :] if g % 6 < 4 else mod_w[:, g % 6 - 4, :]
                load_mod(sp, w, 0, slice(256 * g, 256 * g + 256), start_in[g % 6].sem)
            a0, a1 = UNITS[N_AC]["slab"], UNITS[N_O]["slab"]
            f1, d0 = UNITS[N_F + 4]["slab"], UNITS[N_D]["slab"]
            assert (a1 - a0) == 16 and (d0 - f1) == 20
            stores = UNITS[N_P + 4]["slab"]
            with sp.Fori(0, DEPTH) as l:
                for s in range(0, a0):
                    if s == stores:
                        for m, name in enumerate(("attn", "win")):
                            sp.wait_ge(*k_out_ready(l, m))
                            sp.dma_start(io["k_" + name][0, l].rearrange("t h c -> t (h c)"), k_out[:, m, :]).then_inc(kv_stored.sem, 16)
                            sp.wait_ge(*v_ready(l, m))
                            sp.dma_start(io["v_" + name][0, l].rearrange("t h c -> t (h c)"), vals[:, m, TT, :]).then_inc(kv_stored.sem, 16)
                    slab(l, s)
                with sp.Fori(0, 2) as it:
                    for s in range(a0, a0 + 8):
                        slab(l, s, it, 8)
                for s in range(a1, f1):
                    slab(l, s)
                with sp.Fori(0, 5) as it:
                    for s in range(f1, f1 + 4):
                        slab(l, s, it, 4)
                for s in range(d0, S):
                    slab(l, s)
            for t in range(TT):
                sp.wait_ge(*evicted(0, 2 * DEPTH + 2 * t + 1))
                to = io["y_sample"][0, P * t:P * t + P, :] if t < 2 else io["y_prompt"][0]
                sp.dma_start(to, tok[:, t, :]).then_inc(y_stored.sem, 16)
            sp.wait_ge(*kv_stored(DEPTH - 1, 0))
            sp.wait_ge(*y_stored(0, TT - 1))

        @block.tensor
        def _(pe):
            def parts(n, k):
                K = UNITS[n]["K"]
                a = slice(k * P, k * P + P)
                return w_hi[:, n % RING, a], w_lo[:, n % RING, a]

            def product(out, w, r, start, stop):
                pe.matmul(out, w[1], r[0], start=start, stop=False)
                pe.matmul(out, w[0], r[1], start=False, stop=False)
                return pe.matmul(out, w[0], r[0], start=False, stop=stop)

            def right_operand(n, k, it):
                u = UNITS[n]
                kind = u["kind"]
                if kind == "proj":
                    if n >= N_AC:
                        c = bass.ds(8 + k + it * 4, 1)
                        return [v[:, c, :].rearrange("p a t -> p (a t)") for v in (br_hi, br_lo)]
                    c = (n - N_G) // 16 * 4 + k
                    return br_hi[:, c, :], br_lo[:, c, :]
                if kind == "out":
                    return br_hi[:, k, :], br_lo[:, k, :]
                if kind == "down":
                    return f_hi[:, u["k0"] + k, :], f_lo[:, u["k0"] + k, :]
                return h_hi[:, k, :], h_lo[:, k, :]

            def out_bank(n):
                u = UNITS[n]
                b = (u["i"] % 4) if u["kind"] == "down" else n % RING
                return bank[:, b, 0:T]

            def unit(l, n, it=0, per=0):
                u = UNITS[n]
                pe.wait_ge(*lo_ready(l, n + it * per))
                first, last = u.get("first", True), u.get("last", True)
                for k in range(u["K"]):
                    ins = product(out_bank(n), parts(n, k), right_operand(n, k, it),
                                  first and k == 0, last and k == u["K"] - 1)
                ins.then_inc(unit_done.sem, 1)

            def three_units(l, n, chunk_ready):
                for m in range(n, n + 3):
                    pe.wait_ge(*lo_ready(l, m))
                for k in range(DC):
                    pe.wait_ge(*chunk_ready(k))
                    for m in range(n, n + 3):
                        ins = product(out_bank(m), parts(m, k), right_operand(m, k, 0), k == 0, k == DC - 1)
                        if k == DC - 1:
                            ins.then_inc(unit_done.sem, 1)

            def statistics(l, which):
                pe.wait_ge(*x_summed(l, -1 if which == 0 else 7))
                for t in range(TT):
                    ins = pe.matmul(tr[:, 0, t:t + 1], x_acc[:, P * t:P * t + P], const[:, K_MEAN:K_MEAN + 1],
                                    start=True, stop=True)
                ins.then_inc(x_stat.sem, 1)

            def broadcast(l, which):
                pe.wait_ge(*x_rs_ready(l, which))
                for t in range(TT):
                    ins = pe.matmul(tr[:, 0, P * t:P * t + P], x_rs[:, t:t + 1].broadcast_to([P, P]), ident,
                                    start=True, stop=True)
                ins.then_inc(x_bcast.sem, 1)

            def mod_matmul(out, w, done):
                w = w.rearrange("p (k c) -> p k c", k=DC)
                for k in range(DC):
                    j = k % 4
                    ins = pe.matmul(out[32 * j:32 * j + 32, 0:2 * P], cond[:, k, :], w[:, k, :], start=k < 4, stop=k >= 4)
                ins.then_inc(done, 1)

            def mod_select(out, row, done):
                for y in range(2):
                    ins = pe.matmul(out[:, 2 * y:2 * y + 2], row[:, P * y:P * y + P], const[:, K_SEL:K_SEL + 2],
                                    start=True, stop=True)
                ins.then_inc(done, 1)

            reader = {}

            def claim(b):
                if reader.get(b):
                    pe.wait_ge(*reader[b])

            def hook(l, what, i, it):
                if what == "mod":
                    f, slot = mod_index(i, it), i % 2
                    pe.wait_ge(*mod_in[slot](l, mod_load_index(i, it)))
                    if i >= 12:
                        pe.wait_ge(*mod_ready(l, f - 1))
                    elif i >= 2:
                        pe.wait_ge(*mod_ready(l, f - 2))
                    mod_matmul(sc[:, slot, :], mod_w[:, slot, :], mod_sum.sem)
                elif what == "sel":
                    pe.wait_ge(*mod_row_ready(l, mod_index(i, it)))
                    mod_select(sc[:, i % 2, :], mod_row[:, i % 2, :], mod_col.sem)
                elif what == "mod_next":
                    pe.wait_ge(*next_in(l, i + 2 * it))
                    pe.wait_ge(*next_ready(l, i + 2 * it - 2))
                    mod_matmul(next_bank[i], mod_w[:, 1, :], next_sum.sem)
                elif what == "sel_next":
                    pe.wait_ge(*next_row_ready(l, i + 2 * it))
                    mod_select(next_bank[i], next_row[:, i, :], next_col.sem)
                elif what == "stat":
                    pe.wait_ge(*q_copied(l, i))
                    claim(1)
                    pe.matmul(tr[:, 1, 0:T_LAT], const[:, K_PERM:K_PERM + P], q_raw[:, i % 3, LAT], start=True, stop=True)
                    for t in range(TT):
                        ins = pe.matmul(tr[:, 1, T_LAT + 2 * t:T_LAT + 2 * t + 2], q_sq[:, i % 2, P * t:P * t + P],
                                        const[:, K_HEAD:K_HEAD + 2], start=True, stop=True)
                    ins.then_inc(q_stat.sem, 1)
                    reader[1] = q_mixed(l, i)
                elif what == "rnorm":
                    pe.wait_ge(*q_rs_ready(l, i))
                    claim(0)
                    for t in range(TT):
                        for g in range(2):
                            c = 2 * t + g
                            ins = pe.matmul(tr[64 * g:64 * g + 64, 0, P * t:P * t + P],
                                            q_rs[i % 2][:, c:c + 1].broadcast_to([P, 64]), ident, start=True, stop=True)
                    ins.then_inc(q_bcast.sem, 1)
                    reader[0] = qk_ready(l, i)
                elif what == "vt":
                    pe.wait_ge(*v_copied(l, i))
                    claim(0)
                    for t in range(TT):
                        ins = pe.transpose(tr[:, 0, P * t:P * t + P], v_t[:, i, P * t:P * t + P], ident)
                    ins.then_inc(v_turned.sem, 1)
                    reader[0] = v_ready(l, i)
                elif what == "kout":
                    pe.wait_ge(*qk_ready(l, i))
                    claim(1)
                    pe.transpose(tr[:, 1, 0:P], keys[:, i, PAST + T_LAT:PAST + T], ident).then_inc(k_turned.sem, 1)
                    reader[1] = k_out_ready(l, i)
                elif what == "cache":
                    pe.wait_ge(*past_in(l, 0))
                    claim(1)
                    pe.transpose(tr[:, 1, 0:P], k_past[:, i, :], ident).then_inc(past_turned.sem, 1)
                    reader[1] = past_ready(l, i)
                elif what == "scores":
                    m, c, t = i // 12, i % 12 // 3, i % 3
                    pe.wait_ge(*qk_ready(l, 2 + 4 * m + c))
                    pe.wait_ge(*past_ready(l, m))
                    if i:
                        pe.wait_ge(*exps(l, i - 1))
                    ks = slice(0, PAST + T_LAT) if t < 2 else slice(PAST + T_LAT, PAST + T)
                    for g in range(2):
                        a = slice(64 * g, 64 * g + 64)
                        ins = pe.matmul(sc[:, g, 0:ks.stop - ks.start], q[a, 4 * m + c, P * t:P * t + P], keys[a, m, ks],
                                        start=True, stop=True)
                    ins.then_inc(scores.sem, 1)
                elif what == "probsT":
                    pe.wait_ge(*probs_ready(l, i))
                    claim(0)
                    claim(1)
                    for g in range(2):
                        for b in range(3 if i % 3 < 2 else 1):
                            ins = pe.transpose(tr[:, g, P * b:P * b + P], prob[:, i % 2, g, P * b:P * b + P], ident)
                    ins.then_inc(probs_turned.sem, 1)
                    reader[0] = reader[1] = probs_t_ready(l, i)
                elif what == "attn":
                    m, t = i // 12, i % 3
                    pe.wait_ge(*probs_t_ready(l, i))
                    pe.wait_ge(*v_ready(l, m))
                    pe.wait_ge(*vals_in(l, 0))
                    claim(0)
                    reader[0] = attn_ready(l, i)
                    tiles = (0, 1, 2) if t < 2 else (3,)
                    for b, v in enumerate(tiles):
                        for g in range(2):
                            ins = pe.matmul(tr[64 * g:64 * g + 64, 0, 384:512], vals[:, m, v, 64 * g:64 * g + 64],
                                            prob_t[:, i % 2, g, b, :], start=b == 0, stop=v == tiles[-1])
                    ins.then_inc(attn_out.sem, 1)
                elif what == "pool":
                    pe.wait_ge(*pool_ready(l, i))
                    pe.wait_ge(*pw_in(l, 0))
                    n = BASE["pv"] + 8 * (i // 2) + i % 2
                    for to, at in ((LAT, 16), (CTX, 32 + T_LAT)):
                        ins = pe.matmul(bank[:, n % RING, to], pw[:, i, :], pin[:, i % 2, at:at + to.stop - to.start],
                                        start=True, stop=True)
                    ins.then_inc(pooled.sem, 1)

            def after(l, n, it=0):
                run_hooks(pe, l, n, it, hook, ("mod_next", "sel_next"))

            pe.nop().then_inc(unit_done.sem, RING)
            pe.wait_ge(*loaded(0, 2))
            pe.transpose(tr[:, 1, 0:2 * DC], c_raw[:, :], const[0:2 * DC, K_ID:K_ID + 2 * DC]).then_inc(turned.sem, 1)
            pe.wait_ge(*tok_in(0, TT - 1))
            for k in range(DC):
                if k >= RING:
                    pe.wait_ge(*x_ready(0, k - RING - 8))
                for t in range(TT):
                    ins = pe.transpose(bank[:, k % RING, P * t:P * t + P], tok[:, t, P * k:P * k + P], ident)
                ins.then_inc(turned.sem, 1)
            pe.wait_ge(*vectors_in(0, 9))
            for l in range(DEPTH):
                if l:
                    pe.wait_ge(*evicted(0, 2 * l - 1))
                pe.transpose(tr[:, 0, P * l:P * l + NV], vec_raw[:, l, :], const[0:NV, K_ID:K_ID + NV]).then_inc(turned.sem, 1)
                pe.wait_ge(*evicted(0, 2 * l))
                pe.matmul(tr[:, 0, 256 + 4 * l:256 + 4 * l + 4], const[:, K_PERM:K_PERM + P],
                          vec_all[:, l, V_GAIN:V_GAIN + 4], start=True, stop=True).then_inc(turned.sem, 1)
            pe.wait_ge(*evicted(0, 2 * DEPTH - 1))
            pe.wait_ge(*cond_ready(0, 1))
            for g in range(10):
                if g < 8:
                    pe.wait_ge(*start_in[g % 6](0, g // 6))
                    if g >= 4:
                        pe.wait_ge(*next_ready(0, g - 4 - 8))
                    w = start_w[:, g % 6, :] if g % 6 < 4 else mod_w[:, g % 6 - 4, :]
                    mod_matmul(start_bank[g % 4], w, next_sum.sem)
                if g >= 2:
                    pe.wait_ge(*next_row_ready(0, g - 2 - 8))
                    mod_select(start_bank[(g - 2) % 4], next_row[:, g % 2, :], next_col.sem)

            with pe.Fori(0, DEPTH) as l:
                reader.clear()
                pe.wait_ge(*next_ready(l, -4))
                statistics(l, 0)
                broadcast(l, 0)
                three_units(l, N_Q, lambda k: h_ready(l, k))
                for n in range(0, 3):
                    after(l, n)
                for n in range(3, N_AC):
                    if n == N_G + 4:
                        pe.wait_ge(*conv_split(l, CC - 1))
                    if n == N_G + 16 + 4:
                        pe.wait_ge(*pool_split(l, CC - 1))
                    if UNITS[n - 4]["kind"] == "pv" and n >= 4:
                        pe.wait_ge(*pool_split(l, UNITS[n - 4]["i"]))
                    unit(l, n)
                    after(l, n)
                with pe.Fori(0, 2) as it:
                    for n in range(N_AC, N_AC + 16):
                        if n == N_AC + 4:
                            pe.wait_ge(*attn_ready(l, 11 + it * 12))
                        unit(l, n, it, 16)
                        after(l, n, it)
                three_units(l, N_O, lambda k: merged_split(l, k))
                for n in range(N_O + 3, N_F):
                    unit(l, n)
                statistics(l, 1)
                broadcast(l, 1)
                three_units(l, N_F, lambda k: h_ready(l, 8 + k))
                unit(l, N_F + 3)
                with pe.Fori(0, 4) as it:
                    for n in range(N_F + 4, N_F + 12):
                        unit(l, n, it, 8)
                        after(l, n, it)
                for n in range(N_F + 36, N_D):
                    unit(l, n)
                for n in range(N_D, U):
                    if n < N_D + 8 and n % 2 == 0:
                        pe.wait_ge(*ff_split(l, UNITS[n]["k0"] + UNITS[n]["K"] - 1))
                    unit(l, n)

            pe.wait_ge(*x_ready(DEPTH - 1, 15))
            for k in range(2 * TT):
                if k >= RING:
                    pe.wait_ge(*evicted(0, 2 * DEPTH + (k - RING)))
                for c in range(4):
                    ins = pe.transpose(bank[:, k % RING, P * c:P * c + P],
                                       x[:, 4 * (k % 2) + c, P * (k // 2):P * (k // 2) + P], ident)
                ins.then_inc(turned.sem, 1)

        @block.scalar
        def _(act):
            def split(l, n, it=0, per=0, spi=0):
                u = UNITS[n]
                s = u["slab"]
                act.wait_ge(*slab_in[s % RING](l, s // RING + it * (spi // RING)))
                act.wait_ge(*unit_done(l, n - RING + it * per))
                to, src = weights_of(n, w_hi)
                act.copy(to, src).then_inc(hi_ready.sem, 1)

            def post(l, n, it=0, per=0):
                u = UNITS[n]
                kind, i = u["kind"], u["i"]
                ps = bank[:, n % RING, 0:T]
                if kind in ("out", "proj", "b", "gc"):
                    if kind == "b":
                        k = i + it * 4
                        act.wait_ge(*ff_prod(l, k))
                        c = bass.ds(k, 1) if per else slice(i, i + 1)
                        act.mul(f_hi[:, c, :].rearrange("p a t -> p (a t)"), ff_f[:, i % 2, :], 0.5).then_inc(ff_hi.sem, 1)
                    if kind == "out":
                        square(l, i)
                    return
                if kind == "down":
                    if u["last"]:
                        square(l, 8 + i)
                    return
                act.wait_ge(*unit_done(l, n + it * per))
                if kind == "norm":
                    if i >= 2:
                        act.wait_ge(*q_stat(l, i - 2))
                    act.activation(q_sq[:, i % 2, :], ps, ACT.Square)
                    if i >= 3:
                        act.wait_ge(*q_mixed(l, i - 3))
                    act.copy(q_raw[:, i % 3, :], ps).then_inc(q_copied.sem, 1)
                elif kind == "v":
                    act.copy(v_t[:, i, :], ps).then_inc(v_copied.sem, 1)
                elif kind == "u":
                    act.copy(cu[:, i % 2, :], ps).then_inc(conv_in.sem, 1)
                elif kind == "gb":
                    act.copy(cgb[:, i % 2, :], ps).then_inc(conv_in.sem, 1)
                elif kind == "pv":
                    if i == 0:
                        act.wait_ge(*pads_zeroed(l, 1))
                    if i >= 2:
                        act.wait_ge(*pooled(l, i - 2))
                    act.copy(pin[:, i % 2, 16:16 + T_LAT], ps[:, LAT])
                    act.copy(pin[:, i % 2, 32 + T_LAT:32 + T], ps[:, CTX]).then_inc(pool_in.sem, 1)
                elif kind == "gate":
                    if n == N_G:
                        act.wait_ge(*pooled(l, CC - 1))
                    act.activation(gate_t[:, i % 4, :], ps, ACT.Tanh, scale=0.5).then_inc(gate_ready.sem, 1)
                elif kind == "a":
                    act.activation(ff_t[:, i % 2, :], ps, ACT.Tanh, scale=0.5).then_inc(ff_tanh.sem, 1)

            def square(l, k):
                act.wait_ge(*x_ready(l, k))
                act.wait_ge(*x_summed(l, k - 2))
                act.activation(x_sq[:, k % 2, :], x[:, k % 8, :], ACT.Square).then_inc(x_squared.sem, 1)

            def hook(l, what, i, it):
                if what == "load":
                    f, slot = mod_index(i, it), i % 2
                    if i < 2:
                        act.wait_ge(*attn_ready(l, 23))
                    if i >= 2:
                        act.wait_ge(*mod_sum(l, f - (2 if i < 12 else 1)))
                    columns = bass.ds(256 * (8 + i) + it * (6 * 256), 256) if i < 12 else bass.ds(256 * 20 + it * 256, 256)
                    load_mod(act, mod_w[:, slot, :], l, columns, mod_in[slot].sem)
                elif what == "mod":
                    f = mod_index(i, it)
                    act.wait_ge(*mod_sum(l, f))
                    if i >= 2:
                        act.wait_ge(*mod_col(l, f - (2 if i < 12 else 1)))
                    act.copy(mod_row[:, i % 2, :], sc[:, i % 2, 0:2 * P]).then_inc(mod_row_ready.sem, 1)
                elif what == "load_next":
                    k = i + 2 * it
                    if i:
                        act.wait_ge(*next_sum(l, k - 1))
                    else:
                        act.wait_ge(*mod_sum(l, 11))
                    load_mod(act, mod_w[:, 1, :], (l + 1) % DEPTH, bass.ds(256 * i + it * 512, 256), next_in.sem)
                elif what == "mod_next":
                    act.wait_ge(*next_sum(l, i + 2 * it))
                    act.wait_ge(*next_col(l, i + 2 * it - 2))
                    act.copy(next_row[:, i, :], next_bank[i][:, 0:2 * P]).then_inc(next_row_ready.sem, 1)
                elif what == "kout":
                    act.wait_ge(*k_turned(l, i))
                    act.copy(k_out[:, i, :], tr[:, 1, 0:P]).then_inc(k_out_ready.sem, 1)
                elif what == "cache":
                    act.wait_ge(*past_turned(l, i))
                    act.copy(keys[:, i, 0:PAST], tr[:, 1, 0:P]).then_inc(past_ready.sem, 1)
                elif what == "scores":
                    act.wait_ge(*max_ready(l, i))
                    if i >= 2:
                        act.wait_ge(*probs_turned(l, i - 2))
                    nk = PAST + T_LAT if i % 3 < 2 else T_CTX
                    for g in range(2):
                        ins = act.activation(prob[:, i % 2, g, 0:nk], sc[:, g, 0:nk], ACT.Exp, scale=SCALE,
                                             bias=s_nm[i % 2][:, g:g + 1], accum_out=s_sum[i % 2][:, g:g + 1])
                    ins.then_inc(exps.sem, 1)
                    if i >= 12:
                        act.activation(s_se, s_sd, ACT.Exp).then_inc(sink_exp.sem, 1)
                elif what == "probsT":
                    act.wait_ge(*probs_turned(l, i))
                    if i >= 2:
                        act.wait_ge(*attn_out(l, i - 2))
                    nb = 3 if i % 3 < 2 else 1
                    act.copy(prob_t[:, i % 2, :, 0:nb, :], tr[:, :, 0:P * nb].rearrange("p g (b q) -> p g b q", b=nb))\
                        .then_inc(probs_t_ready.sem, 1)
                elif what == "attn":
                    m, c, t = i // 12, i % 12 // 3, i % 3
                    act.wait_ge(*attn_out(l, i))
                    act.copy(br_hi[:, 8 + 4 * m + c, P * t:P * t + P], tr[:, 0, 384:512]).then_inc(attn_hi.sem, 1)
                elif what == "conv":
                    act.wait_ge(*conv_ready(l, i))
                    act.copy(br_hi[:, i, LAT], cy[:, i % 2, 0:T_LAT])
                    act.copy(br_hi[:, i, CTX], cy[:, i % 2, T_LAT + 1:T + 1]).then_inc(conv_hi.sem, 1)
                elif what == "poolsplit":
                    act.wait_ge(*pooled(l, i))
                    n = BASE["pv"] + 8 * (i // 2) + i % 2
                    act.activation(br_hi[:, 4 + i, :], bank[:, n % RING, 0:T], ACT.Identity,
                                   scale=vec[:, V_PSC + i:V_PSC + i + 1]).then_inc(pool_hi.sem, 1)

            def norm(l, which):
                shift = (M_SH1, M_SH2)[which]

                def round_chunk(d):
                    act.wait_ge(*h_full(l, 8 * which + d))
                    act.copy(h_hi[:, d, :], nf[:, d % 4, :]).then_inc(h_hi_ready.sem, 1)

                act.wait_ge(*gain_ready(l, which))
                for d in range(DC):
                    act.wait_ge(*x_normed(l, 8 * which + d))
                    if d >= 4:
                        act.wait_ge(*h_ready(l, 8 * which + d - 4))
                    for c, part in enumerate((LAT, CTX)):
                        ins = act.activation(nf[:, d % 4, part], nx[:, d % 4, part], ACT.Identity,
                                             scale=gain[:, which, d, c:c + 1], bias=modc[:, shift + d, c:c + 1])
                    ins.then_inc(h_full.sem, 1)
                    if d:
                        round_chunk(d - 1)
                round_chunk(DC - 1)

            def slot(l, n, it=0, per=0, spi=0, ahead=True):
                run_hooks(act, l, n, it, hook, ("load_next", "mod_next"))
                if ahead:
                    split(l, n + LOOKAHEAD, it, per, spi)
                post(l, n, it, per)

            for t in range(TT):
                rows = io["x_sample"][0, P * t:P * t + P, :] if t < 2 else io["x_prompt"][0]
                act.dma_start(tok[:, t, :], rows).then_inc(tok_in.sem, 16)
            act.wait_ge(*turned(0, 0))
            act.activation(cond_t[:, 0, :], tr[:, 1, 0:2 * DC], ACT.Tanh, scale=0.5).then_inc(cond_tanh.sem, 1)
            act.copy(cond_t[:, 1, :], tr[:, 1, 0:2 * DC]).then_inc(cond_tanh.sem, 1)
            for k in range(DC):
                act.wait_ge(*x_ready(0, k - 8))
                if k >= 2:
                    act.wait_ge(*x_summed(0, k - 2 - 8))
                act.activation(x_sq[:, k % 2, :], x[:, k, :], ACT.Square).then_inc(x_squared.sem, 1)

            for g in range(8):
                act.wait_ge(*next_sum(0, g - 8))
                if g >= 2:
                    act.wait_ge(*next_col(0, g - 2 - 8))
                act.copy(next_row[:, g % 2, :], start_bank[g % 4][:, 0:2 * P]).then_inc(next_row_ready.sem, 1)

            with act.Fori(0, DEPTH) as l:
                for n in range(LOOKAHEAD):
                    split(l, n)
                norm(l, 0)
                for n in range(0, N_AC):
                    slot(l, n)
                with act.Fori(0, 2) as it:
                    for n in range(N_AC, N_AC + 16):
                        slot(l, n, it, 16, 8)
                for d in range(DC):
                    act.wait_ge(*merge_done(l, 24 + d))
                    act.mul(br_hi[:, d, :], merged[:, d, :], 0.5).then_inc(merged_hi.sem, 1)
                for n in range(N_O, N_F):
                    slot(l, n)
                norm(l, 1)
                for n in range(N_F, N_F + 4):
                    slot(l, n)
                with act.Fori(0, 4) as it:
                    for n in range(N_F + 4, N_F + 12):
                        slot(l, n, it, 8, 4)
                for n in range(N_F + 36, U):
                    slot(l, n, ahead=n + LOOKAHEAD < U)

        @block.vector
        def _(dve):
            chain = Steps(dve_step, sizes, "dve")

            def split(l, n, it=0, per=0):
                dve.wait_ge(*hi_ready(l, n + it * per))
                to, src = weights_of(n, w_lo)
                hi, _ = weights_of(n, w_hi)
                dve.tensor_tensor(to, src, hi.bitcast(F32), ALU.subtract).then_inc(lo_ready.sem, 1)

            def lo_part(to, x_, hi, scale=None):
                if scale is None:
                    return dve.tensor_tensor(to, x_, hi.bitcast(F32), ALU.subtract)
                return dve.scalar_tensor_tensor(to, x_, scale, hi.bitcast(F32), ALU.mult, ALU.subtract)

            def residual(l, n, k):
                u = UNITS[n]
                b = (u["i"] % 4) if u["kind"] == "down" else n % RING
                g = (M_G1 if k < 8 else M_G2) + k % 8
                for c, part in enumerate((LAT, CTX)):
                    xs = x[:, k % 8, part]
                    ins = dve.scalar_tensor_tensor(xs, bank[:, b, part], modc[:, g, c:c + 1], xs, ALU.mult, ALU.add)
                ins.then_inc(x_ready.sem, 1)

            def before_split(l, n, it, per):
                u = UNITS[n]
                kind, i = u["kind"], u["i"]
                ps = bank[:, n % RING, 0:T]
                if kind == "out":
                    dve.wait_ge(*unit_done(l, n))
                    residual(l, n, i)
                elif kind == "down" and u["last"]:
                    dve.wait_ge(*unit_done(l, n))
                    residual(l, n, 8 + i)
                elif kind == "b":
                    dve.wait_ge(*unit_done(l, n + it * per))
                    dve.wait_ge(*ff_made[i % 2])
                    dve.tensor_tensor(ff_f[:, i % 2, :], ff_s[:, i % 2, :], ps, ALU.mult).then_inc(ff_prod.sem, 1)
                elif kind == "gc":
                    dve.wait_ge(*unit_done(l, n))
                    dve.wait_ge(*conv_in(l, 4 * (i // 2) + 3))
                    if i == 0:
                        dve.wait_ge(*pads_zeroed(l, 1))
                    dve.tensor_tensor(cz[:, 1:1 + T_LAT], cu[:, i % 2, LAT], ps[:, LAT], ALU.mult)
                    made["z"] = chain.made(dve.tensor_tensor(cz[:, 2 + T_LAT:2 + T], cu[:, i % 2, CTX], ps[:, CTX], ALU.mult))
                elif kind == "proj":
                    b, d = i // 8, i % 8
                    dve.wait_ge(*unit_done(l, n + it * per))
                    dve.wait_ge(*gate_ready(l, i + it * 8))
                    t = gate_t[:, d % 4, :]
                    if b == 0:
                        dve.scalar_tensor_tensor(merged[:, d, :], t, 1.0, ps, ALU.add, ALU.mult).then_inc(merge_done.sem, 1)
                    else:
                        made["t"] = chain.made(dve.scalar_tensor_tensor(t, t, 1.0, ps, ALU.add, ALU.mult))

            def after_split(l, n, it, per):
                u = UNITS[n]
                kind, i = u["kind"], u["i"]
                ps = bank[:, n % RING, 0:T]
                if kind == "a":
                    dve.wait_ge(*ff_tanh(l, i + it * 4))
                    ff_made[i % 2] = chain.made(dve.scalar_tensor_tensor(
                        ff_s[:, i % 2, :], ff_t[:, i % 2, :], 1.0, ps, ALU.add, ALU.mult))
                elif kind == "b":
                    k = i + it * 4
                    dve.wait_ge(*ff_hi(l, k))
                    c = bass.ds(k, 1) if per else slice(i, i + 1)
                    lo_part(f_lo[:, c, :].rearrange("p a t -> p (a t)"), ff_f[:, i % 2, :],
                            f_hi[:, c, :].rearrange("p a t -> p (a t)"), 0.5).then_inc(ff_split.sem, 1)
                elif kind == "gc":
                    y, n1 = cy[:, i % 2, :], ZL - 2
                    tap = [vec[:, V_CONV + 4 * r + i:V_CONV + 4 * r + i + 1] for r in range(3)]
                    dve.wait_ge(*made["z"])
                    if i >= 2:
                        dve.wait_ge(*conv_split(l, i - 2))
                        dve.wait_ge(*conv_hi(l, i - 2))
                    s = chain.made(dve.tensor_scalar(y[:, 0:n1], cz[:, 1:1 + n1], tap[1], None, ALU.mult))
                    dve.wait_ge(*s)
                    s = chain.made(dve.scalar_tensor_tensor(y[:, 0:n1], cz[:, 0:n1], tap[0], y[:, 0:n1], ALU.mult, ALU.add))
                    dve.wait_ge(*s)
                    s = chain.made(dve.scalar_tensor_tensor(y[:, 0:n1], cz[:, 2:2 + n1], tap[2], y[:, 0:n1], ALU.mult, ALU.add))
                    dve.wait_ge(*s)
                    dve.tensor_tensor(y[:, 0:T_LAT], y[:, 0:T_LAT], cgb[:, i % 2, LAT], ALU.mult)
                    dve.tensor_tensor(y[:, T_LAT + 1:T + 1], y[:, T_LAT + 1:T + 1], cgb[:, i % 2, CTX], ALU.mult)\
                        .then_inc(conv_ready.sem, 1)
                elif kind == "pv":
                    p, w = pin[:, i % 2, :], POOL_SIZES[i]
                    dve.wait_ge(*pool_in(l, i))
                    s = chain.made(dve.tensor_tensor(ps_a[:, 1:PL], p[:, 0:PL - 1], p[:, 1:PL], ALU.add))
                    src, dst, size, lo = ps_a, ps_b, 2, 1
                    while size < w:
                        hf = size // 2
                        dve.wait_ge(*s)
                        a, b = lo + hf, PL - (size - 1)
                        s = chain.made(dve.tensor_tensor(dst[:, a:b], src[:, a - hf:b - hf], src[:, a + hf:b + hf], ALU.add))
                        src, dst, size, lo = dst, src, 2 * size, a
                    dve.wait_ge(*s)
                    edge = const[:, K_EDGE + 32 * i:K_EDGE + 32 * i + 32].rearrange("p (s e) -> p s e", e=8)
                    for sq_, at, step in ((0, 16, T_LAT - 8), (1, 32 + T_LAT, T_CTX - 8)):
                        for e in range(2):
                            v = src[:, at + e * step:at + e * step + 8]
                            s = chain.made(dve.tensor_tensor(v, v, edge[:, 2 * sq_ + e, :], ALU.mult))
                    dve.wait_ge(*s)
                    for at, m in ((16, T_LAT), (32 + T_LAT, T_CTX)):
                        ins = dve.scalar_tensor_tensor(p[:, at:at + m], src[:, at:at + m], 1.0 / w, p[:, at:at + m],
                                                       ALU.mult, ALU.subtract)
                    ins.then_inc(pool_ready.sem, 1)
                elif kind == "proj" and i >= 8:
                    d = i % 8
                    dve.wait_ge(*made["t"])
                    m = merged[:, d, :]
                    dve.tensor_tensor(m, m, gate_t[:, d % 4, :], ALU.add).then_inc(merge_done.sem, 1)

            def mod_columns(c, src, b, done):
                dve.tensor_tensor(modc[:, c, :], src.rearrange("p (y c) -> p y c", c=2),
                                  b.unsqueeze(2).broadcast_to([P, 2, 2]), ALU.add).then_inc(done, 1)

            def hook(l, what, i, it):
                if what == "sel":
                    dve.wait_ge(*mod_col(l, mod_index(i, it)))
                    c = 16 + 2 * i + it * 12 if i < 12 else 40 + it * 2
                    mod_columns(bass.ds(c, 2), sc[:, i % 2, 0:4], vec[:, bass.ds(c, 2)], mod_ready.sem)
                elif what == "sel_next":
                    dve.wait_ge(*next_col(l, i + 2 * it))
                    c = bass.ds(2 * i + it * 4, 2)
                    b = vec_all[:, bass.ds((l + 1) % DEPTH, 1), c].rearrange("p a v -> p (a v)")
                    mod_columns(c, next_bank[i][:, 0:4], b, next_ready.sem)
                elif what == "stat":
                    g = i if i < 2 else (i - 2) // 4
                    gi = V_GAIN + (2 * g + 1 if i < 2 else 2 * g)
                    own, other = vec[:, gi:gi + 1], vec[:, gi + 4:gi + 5]
                    dve.wait_ge(*q_stat(l, i))
                    if i >= 2:
                        dve.wait_ge(*q_rs_ready(l, i - 2))
                    dve.tensor_scalar(q_ms[i % 2], tr[:, 1, T_LAT:T_LAT + 6], EPS, None, ALU.add).then_inc(q_ms_ready.sem, 1)
                    mix = q_mix[:, i % 2, :]
                    s = chain.made(dve.scalar_tensor_tensor(q_rot[:, :], tr[:, 1, 0:T_LAT], other, const[:, K_SIN:K_SIN + T_LAT],
                                                            ALU.mult, ALU.mult))
                    s2 = chain.made(dve.scalar_tensor_tensor(mix[:, LAT], q_raw[:, i % 3, LAT], own,
                                                             const[:, K_COS:K_COS + T_LAT], ALU.mult, ALU.mult))
                    s2 = chain.made(dve.tensor_scalar(mix[:, CTX], q_raw[:, i % 3, CTX], own, None, ALU.mult))
                    dve.wait_ge(*s2)
                    dve.tensor_tensor(mix[:, LAT], mix[:, LAT], q_rot[:, :], ALU.add).then_inc(q_mixed.sem, 1)
                elif what == "rnorm":
                    to = keys[:, i, PAST:PAST + T] if i < 2 else q[:, i - 2, :]
                    dve.wait_ge(*q_bcast(l, i))
                    dve.wait_ge(*q_mixed(l, i))
                    dve.tensor_tensor(to, q_mix[:, i % 2, :], tr[:, 0, 0:T], ALU.mult).then_inc(qk_ready.sem, 1)
                elif what == "vt":
                    dve.wait_ge(*v_turned(l, i))
                    dve.tensor_copy(vals[:, i, 1:1 + TT, :], tr[:, 0, 0:T].rearrange("p (t c) -> p t c", c=P))\
                        .then_inc(v_ready.sem, 1)
                elif what == "scores":
                    m, t = i // 12, i % 3
                    nk = PAST + T_LAT if t < 2 else T_CTX
                    dve.wait_ge(*scores(l, i))
                    if m == 1 and t < 2:
                        at = PAST + P * (1 - t)
                        blk = sc[:, :, at:at + P]
                        mask = const[:, K_MASK + P * t:K_MASK + P * t + P].unsqueeze(1).broadcast_to([P, 2, P])
                        s = chain.made(dve.tensor_tensor(blk, blk, mask, ALU.add))
                        dve.wait_ge(*s)
                    s = chain.made(dve.reduce_max(s_max, sc[:, :, 0:nk], AXX))
                    dve.wait_ge(*s)
                    nm = s_nm[i % 2]
                    if m == 0:
                        dve.tensor_scalar(nm, s_max, -SCALE, None, ALU.mult).then_inc(max_ready.sem, 1)
                    else:
                        c = i % 12 // 3
                        two = nsink[:, c:c + 5:4]
                        s = chain.made(dve.scalar_tensor_tensor(nm, s_max, -SCALE, two, ALU.mult, ALU.min))
                        dve.wait_ge(*s)
                        dve.tensor_tensor(s_sd, nm, two, ALU.subtract).then_inc(max_ready.sem, 1)
                elif what == "scale":
                    nk = PAST + T_LAT if i % 3 < 2 else T_CTX
                    dve.wait_ge(*exps(l, i))
                    total = s_sum[i % 2]
                    if i >= 12:
                        dve.wait_ge(*sink_exp(l, i - 12))
                        s = chain.made(dve.tensor_tensor(total, total, s_se, ALU.add))
                        dve.wait_ge(*s)
                    s = chain.made(dve.reciprocal(s_r, total))
                    dve.wait_ge(*s)
                    for g in range(2):
                        v = prob[:, i % 2, g, 0:nk]
                        ins = dve.tensor_scalar(v, v, s_r[:, g:g + 1], None, ALU.mult)
                    ins.then_inc(probs_ready.sem, 1)
                elif what == "attn":
                    m, c, t = i // 12, i % 12 // 3, i % 3
                    part = slice(P * t, P * t + P)
                    dve.wait_ge(*attn_hi(l, i))
                    if i == 0:
                        dve.wait_ge(*kv_stored(l, 0))
                    lo_part(br_lo[:, 8 + 4 * m + c, part], tr[:, 0, 384:512], br_hi[:, 8 + 4 * m + c, part])\
                        .then_inc(attn_ready.sem, 1)
                elif what == "conv":
                    dve.wait_ge(*conv_hi(l, i))
                    lo_part(br_lo[:, i, LAT], cy[:, i % 2, 0:T_LAT], br_hi[:, i, LAT])
                    lo_part(br_lo[:, i, CTX], cy[:, i % 2, T_LAT + 1:T + 1], br_hi[:, i, CTX]).then_inc(conv_split.sem, 1)
                elif what == "poolsplit":
                    n = BASE["pv"] + 8 * (i // 2) + i % 2
                    dve.wait_ge(*pool_hi(l, i))
                    lo_part(br_lo[:, 4 + i, :], bank[:, n % RING, 0:T], br_hi[:, 4 + i, :],
                            vec[:, V_PSC + i:V_PSC + i + 1]).then_inc(pool_split.sem, 1)

            def mean_square(l, which):
                dve.wait_ge(*x_stat(l, which))
                dve.tensor_scalar(x_ms, tr[:, 0, 0:TT], EPS, None, ALU.add).then_inc(x_ms_ready.sem, 1)

            def norm(l, which):
                sc_, g_ = (M_SC1, M_SC2)[which], (V_GMIX, V_GFFN)[which]
                dve.wait_ge(*(next_ready(l, -1) if which == 0 else mod_ready(l, 11)))
                dve.scalar_tensor_tensor(gain[:, which, :, :], modc[:, sc_:sc_ + 8, :], 1.0,
                                         vec[:, g_:g_ + 8].unsqueeze(2).broadcast_to([P, DC, 2]), ALU.add, ALU.mult)\
                    .then_inc(gain_ready.sem, 1)

                def low(d):
                    dve.wait_ge(*h_hi_ready(l, 8 * which + d))
                    lo_part(h_lo[:, d, :], nf[:, d % 4, :], h_hi[:, d, :]).then_inc(h_ready.sem, 1)

                dve.wait_ge(*x_bcast(l, which))
                for d in range(DC):
                    if d >= 4:
                        dve.wait_ge(*h_full(l, 8 * which + d - 4))
                    dve.tensor_tensor(nx[:, d % 4, :], x[:, d, :], tr[:, 0, 0:T], ALU.mult).then_inc(x_normed.sem, 1)
                    if d >= 2:
                        low(d - 2)
                low(DC - 2)
                low(DC - 1)

            def slot(l, n, it=0, per=0, ahead=True):
                run_hooks(dve, l, n, it, hook, ("sel_next",))
                before_split(l, n, it, per)
                if ahead:
                    split(l, n + LOOKAHEAD, it, per)
                after_split(l, n, it, per)

            made, ff_made = {}, {}

            dve.nop().then_inc(lo_ready.sem, 8)
            s = chain.made(dve.memset(cond[:, :, :], 0.0))
            dve.wait_ge(*cond_tanh(0, 1))
            s = chain.made(dve.scalar_tensor_tensor(cond_t[:, 0, :], cond_t[:, 0, :], 1.0, cond_t[:, 1, :], ALU.add, ALU.mult))
            dve.wait_ge(*s)
            for c in range(2):
                dve.tensor_scalar(cond[:, :, c], cond_t[:, 0, DC * c:DC * c + DC], 0.5, None, ALU.mult)\
                    .then_inc(cond_ready.sem, 1)
            for k in range(DC):
                dve.wait_ge(*turned(0, 1 + k))
                dve.tensor_copy(x[:, k, :], bank[:, k % RING, 0:T]).then_inc(x_ready.sem, 1)
            for l in range(DEPTH):
                dve.wait_ge(*turned(0, 1 + DC + 2 * l))
                dve.tensor_copy(vec_all[:, l, 0:NV], tr[:, 0, P * l:P * l + NV]).then_inc(evicted.sem, 1)
                dve.wait_ge(*turned(0, 2 + DC + 2 * l))
                dve.tensor_copy(vec_all[:, l, NV:NVX], tr[:, 0, 256 + 4 * l:256 + 4 * l + 4]).then_inc(evicted.sem, 1)
            dve.wait_ge(*evicted(0, 2 * DEPTH - 1))
            dve.wait_ge(*vectors_in(0, 9))
            for g in range(8):
                dve.wait_ge(*next_col(0, g - 8))
                mod_columns(slice(2 * g, 2 * g + 2), start_bank[g % 4][:, 0:4], vec_all[:, 0, 2 * g:2 * g + 2], next_ready.sem)

            with dve.Fori(0, DEPTH) as l:
                chain.enter("layer", l)
                dve.tensor_copy(vec[:, :], vec_all[:, bass.ds(l, 1), :].rearrange("p a v -> p (a v)")).then_inc(vec_ready.sem, 1)
                dve.wait_ge(*vec_ready(l, 0))
                s = chain.made(dve.tensor_scalar(nsink[:, :], sink[:, bass.ds(l, 1), :].rearrange("p a v -> p (a v)"),
                                                 -1.0, None, ALU.mult))
                dve.wait_ge(*s)
                mean_square(l, 0)
                for n in range(LOOKAHEAD):
                    split(l, n)
                norm(l, 0)
                for n in range(0, N_AC):
                    slot(l, n)
                with dve.Fori(0, 2) as it:
                    chain.enter("branches", it)
                    for n in range(N_AC, N_AC + 16):
                        slot(l, n, it, 16)
                    chain.leave(2)
                for d in range(DC):
                    dve.wait_ge(*merged_hi(l, d))
                    lo_part(br_lo[:, d, :], merged[:, d, :], br_hi[:, d, :], 0.5).then_inc(merged_split.sem, 1)
                for n in range(N_O, N_F):
                    slot(l, n)
                mean_square(l, 1)
                norm(l, 1)
                for n in range(N_F, N_F + 4):
                    slot(l, n)
                with dve.Fori(0, 4) as it:
                    chain.enter("ffn", it)
                    for n in range(N_F + 4, N_F + 12):
                        slot(l, n, it, 8)
                    chain.leave(4)
                for n in range(N_F + 36, U):
                    slot(l, n, ahead=n + LOOKAHEAD < U)
                chain.leave(DEPTH)

            for k in range(2 * TT):
                dve.wait_ge(*turned(0, 1 + DC + 2 * DEPTH + k))
                ins = dve.tensor_copy(tok[:, k // 2, 512 * (k % 2):512 * (k % 2) + 512], bank[:, k % RING, :])
                ins.then_inc(evicted.sem, 1)

        @block.gpsimd
        def _(pool):
            chain = Steps(pool_step, sizes, "pool")

            def add_square(l, k):
                pool.wait_ge(*x_squared(l, k))
                if k % 8 == 0:
                    return
                if k % 8 == 1:
                    pool.tensor_tensor(x_acc[:, :], x_sq[:, 0, :], x_sq[:, 1, :], ALU.add).then_inc(x_summed.sem, 2)
                    return
                pool.wait_ge(*x_summed(l, k - 1))
                pool.tensor_tensor(x_acc[:, :], x_acc[:, :], x_sq[:, k % 2, :], ALU.add).then_inc(x_summed.sem, 1)

            def rms(l, which):
                pool.wait_ge(*x_ms_ready(l, which))
                pool.tensor_tensor(x_rs, x_ms, exponent[:, 0:1].broadcast_to([P, TT]), ALU.pow).then_inc(x_rs_ready.sem, 1)

            for k in range(10):
                load_vector(pool, k)
            pool.wait_ge(*chain.made(pool.memset(exponent[:, :], -0.5)))
            for k in range(DC):
                add_square(0, k - 8)
            with pool.Fori(0, DEPTH) as l:
                rms(l, 0)
                for m, name in enumerate(("attn", "win")):
                    pool.dma_start(k_past[:, m, :], io["cache_k_" + name][0, l].rearrange("t h c -> t (h c)"))\
                        .then_inc(past_in.sem, 16)
                for m, name in enumerate(("attn", "win")):
                    pool.dma_start(vals[:, m, 0, :], io["cache_v_" + name][0, l].rearrange("t h c -> t (h c)"))\
                        .then_inc(vals_in.sem, 16)
                pool.dma_start(pw[:, :, :], io["pool_w"][l].rearrange("g c e -> c g e")).then_inc(pw_in.sem, 16)
                for i in range(10):
                    pool.wait_ge(*q_ms_ready(l, i))
                    if i >= 2:
                        pool.wait_ge(*q_bcast(l, i - 2))
                    pool.tensor_tensor(q_rs[i % 2], q_ms[i % 2], exponent[:, 0:1].broadcast_to([P, 2 * TT]), ALU.pow)\
                        .then_inc(q_rs_ready.sem, 1)
                    if i == 0:
                        pool.memset(cz[:, :], 0.0).then_inc(pads_zeroed.sem, 1)
                        pool.memset(pin[:, :, :], 0.0).then_inc(pads_zeroed.sem, 1)
                for k in range(8):
                    add_square(l, k)
                rms(l, 1)
                for k in range(8, 16):
                    add_square(l, k)


SHAPES_OUT = {
    "y_prompt": (1, T_CTX, D), "y_sample": (1, T_LAT, D),
    "k_attn": (1, DEPTH, T_CTX, NKV, HD), "v_attn": (1, DEPTH, T_CTX, NKV, HD),
    "k_win": (1, DEPTH, T_CTX, NKV, HD), "v_win": (1, DEPTH, T_CTX, NKV, HD),
}


def build(make, shapes, sizes):
    nc = make()
    io = {n: nc.dram_tensor(f"in_{n}", s, F32, kind="ExternalInput").ap() for n, s in shapes.items()}
    io |= {n: nc.dram_tensor(f"out_{n}", s, F32, kind="ExternalOutput").ap() for n, s in SHAPES_OUT.items()}
    program(nc, io, sizes)
    return nc


def kernel(**inputs):
    import concourse.bacc as bacc
    from concourse.bass_utils import run_bass_kernel_spmd

    arrays = {n: np.ascontiguousarray(a) for n, a in inputs.items()}
    arrays["const"] = constants()
    shapes = {n: a.shape for n, a in arrays.items()}

    def make():
        return bacc.Bacc("TRN2", target_bir_lowering=False, num_devices=1)

    sizes = {}
    build(make, shapes, sizes)
    nc = build(make, shapes, sizes)
    r = run_bass_kernel_spmd(nc, [{f"in_{n}": a for n, a in arrays.items()}], core_ids=[0])
    return tuple(r.results[0][f"out_{n}"] for n in SHAPES_OUT)
```

```python
from contextlib import ExitStack

import numpy as np

import concourse.bass as bass
import concourse.mybir as mybir

P = 128
F32 = mybir.dt.float32
F32R = mybir.dt.float32r
ALU = mybir.AluOpType
ACT = mybir.ActivationFunctionType
AXX = mybir.AxisListType.X

DEPTH = 2
D = 1024
DC = D // P
T_LAT, T_CTX = 256, 128
T = T_LAT + T_CTX
TT = T // P
PAST = 128
HD = 64
NQ, NKV = 8, 2
QW, KVW = NQ * HD, NKV * HD
GRID_W = 64
N_FREQ = HD // 4
ROPE_THETA = 10000.0
CW = 512
CC = CW // P
POOL_SIZES = (2, 4, 8, 16)
D_FF = -(-(8 * D) // (3 * 256)) * 256
FC = D_FF // P
EPS = 1e-6
NEG = -1e30
SCALE = HD ** -0.5

C_QA, C_KVA = 0, QW
C_QC, C_KVC = QW + 2 * KVW, 2 * QW + 2 * KVW
C_U = 2 * QW + 4 * KVW
C_GB, C_GC, C_PV = C_U + CW, C_U + 2 * CW, C_U + 3 * CW
C_GL = C_U + 4 * CW

LOOKAHEAD = 3
RING = 4
SLAB = 2048
LAT, CTX = slice(0, T_LAT), slice(T_LAT, T)

V_BMOD, V_GMIX, V_GFFN, V_CONV, V_PSC, V_GAIN = 0, 48, 56, 64, 76, 80
NV = 84
NVX = NV + 4
M_SH1, M_SC1, M_G1, M_SH2, M_SC2, M_G2 = range(0, 48, 8)

K_ID, K_PERM, K_MASK, K_COS, K_SIN = 0, 128, 256, 512, 768
K_HEAD, K_SEL, K_MEAN, K_EDGE = 1024, 1026, 1028, 1029
NK = 1029 + 128


def constants():
    k = np.zeros((P, NK), np.float32)
    p = np.arange(P)
    k[p, K_ID + p] = 1.0
    k[p, K_PERM + (p ^ N_FREQ)] = 1.0
    a, b = np.meshgrid(p, p, indexing="ij")
    k[:, K_MASK:K_MASK + P] = np.where(b <= a, 0.0, NEG)
    k[:, K_MASK + P:K_MASK + 2 * P] = np.where(a <= b, 0.0, NEG)
    t = np.arange(T_LAT)
    pos = np.stack([t // GRID_W, t % GRID_W]).astype(np.float32)
    inv = (1.0 / (np.float32(ROPE_THETA) ** (np.arange(N_FREQ, dtype=np.float32) / N_FREQ))).astype(np.float32)
    ang = (pos[(p % HD) // 32] * inv[p % N_FREQ][:, None]).astype(np.float32)
    sign = np.where((p // N_FREQ) % 2 == 0, -1.0, 1.0)[:, None]
    k[:, K_COS:K_COS + T_LAT] = np.cos(ang)
    k[:, K_SIN:K_SIN + T_LAT] = np.sin(ang) * sign
    k[p, K_HEAD + p // HD] = 1.0 / HD
    for j in range(4):
        for c in range(2):
            k[32 * j + c, K_SEL + c] = 1.0
    k[:, K_MEAN] = 1.0 / D
    edge = np.ones((4, 4, 8), np.float32)
    for g, w in enumerate(POOL_SIZES):
        for s, n in enumerate((T_LAT, T_CTX)):
            for e, first in enumerate((0, n - 8)):
                i = np.arange(first, first + 8)
                cnt = np.clip(i + w - w // 2, 0, n) - np.clip(i - w // 2, 0, n)
                edge[g, 2 * s + e] = w / cnt
    k[:, K_EDGE:K_EDGE + 128] = edge.reshape(1, 128)
    return k


def plan():
    units, slab_of = [], []

    def add(kind, indices, K, slab):
        slab_of.append(slab)
        for j, i in enumerate(indices):
            units.append(dict(kind=kind[j] if isinstance(kind, tuple) else kind, i=i, K=K,
                              part=j, slab=len(slab_of) - 1, shape=slab[0]))

    for m, c0 in enumerate((C_KVA, C_KVC)):
        add(("norm", "v"), (m, m), DC, ("in", c0))
    for m, c0 in enumerate((C_QA, C_QC)):
        for s in range(2):
            add("norm", (2 + 4 * m + 2 * s, 3 + 4 * m + 2 * s), DC, ("pair", c0 + P * s))
    for s in range(2):
        for kind, c0 in (("u", C_U), ("gb", C_GB), ("gc", C_GC), ("pv", C_PV)):
            add(kind, (2 * s, 2 * s + 1), DC, ("in", c0 + 2 * P * s))
    for b, branch in enumerate((1, 3, 0, 2)):
        for half in range(2):
            for s in (2 * half, 2 * half + 1):
                add("gate", (8 * b + 2 * s, 8 * b + 2 * s + 1), DC, ("in", C_GL + branch * D + 2 * P * s))
            for d in (4 * half, 4 * half + 2):
                add("proj", (8 * b + d, 8 * b + d + 1), 4, ("heads" if b > 1 else "branch", branch, P * d))
    for s in range(4):
        add("out", (2 * s, 2 * s + 1), DC, ("out", s))
    for s in range(FC // 2):
        add("a", (2 * s, 2 * s + 1), DC, ("gu", 2 * P * s))
        add("b", (2 * s, 2 * s + 1), DC, ("gu", D_FF + 2 * P * s))
    for s in range(4):
        k0 = 0
        for q, K in enumerate((6, 6, 5, 5)):
            add("down", (2 * s, 2 * s + 1), K, ("down", s, k0, K))
            for u in units[-2:]:
                u.update(k0=k0, first=q == 0, last=q == 3)
            k0 += K
    base = {}
    for n, u in enumerate(units):
        base.setdefault(u["kind"], n)
    U = len(units)

    hooks = [[] for _ in range(U)]
    for n, u in enumerate(units[:12]):
        if u["kind"] == "norm":
            at = (3, None, 4)[n] if n < 3 else n + 1
            if u["i"] < 2:
                hooks[at + 2].append(("rnorm", u["i"]))
            hooks[at].append(("stat", u["i"]))
        else:
            hooks[(3, 4)[u["i"]]].append(("vt", u["i"]))
    hooks[6].insert(0, ("kout", 0))
    hooks[7].insert(0, ("kout", 1))
    hooks[8].insert(0, ("cache", 0))
    hooks[9].insert(0, ("cache", 1))
    P0, G0 = base["u"], base["gate"]
    for n in range(P0, G0):
        if units[n]["kind"] == "gc":
            hooks[n + 1].append(("conv", units[n]["i"]))
        if units[n]["kind"] == "pv":
            hooks[n + 2].append(("pooldiff", units[n]["i"]))
            hooks[n + 3].append(("pool", units[n]["i"]))
            hooks[n + 4].append(("poolsplit", units[n]["i"]))
    steps = []
    for k in range(51):
        now, j = [], k // 2
        if k % 2 == 0:
            now += [("attn", j - 2)] if j >= 2 else []
            now += [("scores", j)] if j < 24 else []
        else:
            now += [("scale", j)] if j < 24 else []
            now += [("probsT", j - 1)] if j >= 1 else []
        steps.append(now)
    n_attn = range(P0, base["gate"] + 32)
    weight = sum(units[n]["K"] for n in n_attn)
    done = k = 0
    for n in n_attn:
        done += units[n]["K"]
        while k < len(steps) and (k + 0.5) * weight / len(steps) <= done:
            hooks[n].extend(steps[k])
            k += 1
    assert k == len(steps)
    AC = G0 + 32
    for x, at in enumerate((3, 5, 8, 10, 12, 14)):
        hooks[AC + at - 2].insert(0, ("load", x))
        hooks[AC + at].append(("mod", x))
        hooks[AC + at + 1].insert(0, ("sel", x))
    F = base["a"] + 4
    hooks[F] += [("load", 12), ("load_next", 0)]
    hooks[F + 3] += [("mod", 12), ("mod_next", 0), ("load_next", 1)]
    hooks[F + 5] += [("sel", 12), ("sel_next", 0), ("mod_next", 1)]
    hooks[F + 7] += [("sel_next", 1)]
    last_unit = {}
    for n, u in enumerate(units):
        last_unit[u["slab"]] = n
    return units, slab_of, hooks, base, last_unit


UNITS, SLABS, HOOKS, BASE, LAST_UNIT = plan()
U, S = len(UNITS), len(SLABS)
N_Q, N_P, N_G = 0, BASE["u"], BASE["gate"]
N_AC, N_O = N_G + 32, BASE["out"]
N_F, N_D = BASE["a"], BASE["down"]
assert U % RING == 0 and S % RING == 0


class Signal:

    def __init__(self, sem, per_layer, before=0, step=1):
        self.sem, self.per_layer, self.before, self.step = sem, per_layer, before, step

    def __call__(self, l, k):
        return self.sem, (l * self.per_layer + (k + self.before + 1)) * self.step


class Steps:

    def __init__(self, sem, sizes, name):
        self.sem, self.sizes, self.name = sem, sizes, name
        self.offset, self.n, self.marks = 0, 0, []

    def made(self, instruction):
        instruction.then_inc(self.sem, 1)
        self.n += 1
        return self.sem, self.offset + self.n

    def enter(self, what, i):
        self.marks.append((what, self.n, self.offset))
        self.offset = self.offset + i * self.sizes.get((self.name, what), 1)

    def leave(self, times):
        what, n, offset = self.marks.pop()
        size = self.n - n
        self.sizes[(self.name, what)] = size
        self.offset, self.n = offset, n + size * times


def program(nc, io, sizes):
    with ExitStack() as ctx:
        base = (nc.sbuf_base + 63) // 64 * 64
        top = base

        def place(name, shape, dt=F32, at=None):
            nonlocal top
            size = 4 * int(np.prod(shape[1:]))
            size = (size + 31) // 32 * 32
            if at is None:
                at, top = top, top + size
            place.end = at + size
            return nc.alloc_sbuf_tensor_at(name, shape, dt, offset=at)

        raw = place("raw", [P, RING, SLAB])
        w_hi = place("w_hi", [P, RING, DC * P], F32R)
        w_lo = place("w_lo", [P, RING, DC * P], F32R)
        x = place("x", [P, DC, T])
        h_hi = place("h_hi", [P, DC, T], F32R)
        h_lo = place("h_lo", [P, DC, T], F32R)
        G = top
        f_hi = place("f_hi", [P, FC, T], F32R)
        f_lo = place("f_lo", [P, FC, T], F32R)
        br_hi = place("br_hi", [P, 16, T], F32R, at=G)
        br_lo = place("br_lo", [P, 16, T], F32R, at=G + 16 * T * 4)
        Z = G + 2 * 16 * T * 4
        merged = place("merged", [P, DC, T], at=Z)
        gate_t = place("gate_t", [P, 4, T], at=Z + DC * T * 4)
        assert place.end <= top
        Q1, Q2 = G + 8 * T * 4, G + 24 * T * 4
        q_sq = place("q_sq", [P, 2, T], at=Q1)
        q_raw = place("q_raw", [P, 3, T], at=place.end)
        q_rot = place("q_rot", [P, T_LAT], at=place.end)
        pw = place("pw", [P, CC, P], at=place.end)
        assert place.end <= Q1 + 8 * T * 4
        v_t = place("v_t", [P, 2, T], at=Q2)
        q_mix = place("q_mix", [P, 2, T], at=place.end)
        k_past = place("k_past", [P, 2, KVW], at=place.end)
        k_out = place("k_out", [P, 2, KVW], at=place.end)
        assert place.end <= Q2 + 8 * T * 4
        ZL = 1 + T_LAT + 1 + T_CTX + 1
        PL = 16 + T_LAT + 16 + T_CTX + 16
        pin = place("pin", [P, 2, PL], at=Z)
        ps_a = place("ps_a", [P, PL], at=place.end)
        ps_b = place("ps_b", [P, PL], at=place.end)
        cz = place("cz", [P, ZL], at=place.end)
        cy = place("cy", [P, 2, ZL - 1], at=place.end)
        cu = place("cu", [P, 2, T], at=place.end)
        cgb = place("cgb", [P, 2, T], at=place.end)
        assert place.end <= top, (place.end, top)
        nx = place("nx", [P, 4, T], at=Z)
        nf = place("nf", [P, 4, T], at=place.end)
        tok = place("tok", [P, TT, D], at=G)
        vec_raw = place("vec_raw", [NV, DEPTH, P], at=G + TT * D * 4)
        c_raw = place("c_raw", [2 * DC, P], at=place.end)
        start_w = place("start_w", [P, 4, SLAB], at=place.end)
        assert place.end <= Z
        q_at = top
        q = place("q", [P, 8, T])
        x_sq = place("x_sq", [P, 2, T], at=q_at)
        x_acc = place("x_acc", [P, T], at=place.end)
        keys = place("keys", [P, 2, PAST + T])
        vals = place("vals", [P, 2, 1 + TT, KVW])
        A0 = top
        prob = place("prob", [P, 2, 2, PAST + T_LAT])
        prob_t = place("prob_t", [P, 2, 2, 3, P])
        mod_w = place("mod_w", [P, 2, SLAB], at=q_at + 3 * T * 4)
        next_row = place("next_row", [P, 2, 2 * P], at=place.end)
        ff_t = place("ff_t", [P, 2, T], at=place.end)
        ff_s = place("ff_s", [P, 2, T], at=place.end)
        ff_f = place("ff_f", [P, 2, T], at=place.end)
        assert place.end <= top
        const = place("const", [P, NK])
        cond = place("cond", [P, DC, 32])
        cond_t = place("cond_t", [P, 2, 2 * DC], at=A0 + 4096)
        vec_all = place("vec_all", [P, DEPTH, NVX])
        vec = place("vec", [P, NVX])
        modc = place("modc", [P, 48, 2])
        gain = place("gain", [P, 2, DC, 2])
        mod_row = place("mod_row", [P, 2, 2 * P])
        sink = place("sink", [P, DEPTH, NQ])
        nsink = place("nsink", [P, NQ])
        st = place("st", [P, 64])
        exponent = place("exponent", [P, 1])
        mod_t = place("mod_t", [P, 6, 2, 2])
        q_rs = place("q_rs", [P, 10, 2 * TT])
        assert top <= nc.sbuf_usable_end, (top, nc.sbuf_usable_end)
        x_ms, x_rs = st[:, 0:3], st[:, 4:7]
        q_ms = [st[:, 8 + 8 * i:14 + 8 * i] for i in range(2)]
        s_max, s_nm, s_sum = st[:, 40:42], [st[:, 42 + 2 * i:44 + 2 * i] for i in range(2)], [st[:, 46 + 2 * i:48 + 2 * i] for i in range(2)]
        s_sd, s_se, s_r = st[:, 50:52], st[:, 52:54], st[:, 54:56]
        ident = const[:, K_ID:K_ID + P]

        def psum(name, shape):
            return ctx.enter_context(nc.psum_tensor(name, shape, F32))

        bank = psum("bank", [P, RING, 512])
        sc = psum("sc", [P, 2, 512])
        tr = psum("tr", [P, 2, 512])

        def signal(name, per_layer, before=0, step=1):
            return Signal(ctx.enter_context(nc.semaphore(name)), per_layer, before, step)

        slab_in = [signal(f"slab_in{s}", S // RING, step=32) for s in range(RING)]
        start_in = [signal(f"start_in{s}", 0, step=32) for s in range(6)]
        mod_in = [signal(f"mod_in{s}", (10, 6)[s], step=32) for s in range(2)]
        next_in = signal("next_in", 8, step=32)
        unit_done = signal("unit_done", U, before=RING)
        x_stat = signal("x_stat", 2)
        x_bcast = signal("x_bcast", 2)
        q_stat = signal("q_stat", 10)
        q_bcast = signal("q_bcast", 2)
        v_turned = signal("v_turned", 2)
        k_turned = signal("k_turned", 2)
        past_turned = signal("past_turned", 2)
        scores = signal("scores", 24)
        probs_turned = signal("probs_turned", 24)
        attn_out = signal("attn_out", 24)
        mod_sum = signal("mod_sum", 16)
        mod_col = signal("mod_col", 16)
        next_sum = signal("next_sum", 8, before=8)
        next_col = signal("next_col", 8, before=8)
        pooled = signal("pooled", 4)
        turned = signal("turned", 0)
        hi_ready = signal("hi_ready", U)
        h_hi_ready = signal("h_hi_ready", 16)
        q_copied = signal("q_copied", 10)
        v_copied = signal("v_copied", 2)
        k_out_ready = signal("k_out_ready", 2)
        past_ready = signal("past_ready", 2)
        exps = signal("exps", 24)
        sink_exp = signal("sink_exp", 12)
        probs_t_ready = signal("probs_t_ready", 24)
        attn_hi = signal("attn_hi", 24)
        mod_row_ready = signal("mod_row_ready", 16)
        next_row_ready = signal("next_row_ready", 8, before=8)
        conv_in = signal("conv_in", 8)
        pool_in = signal("pool_in", 4)
        conv_hi = signal("conv_hi", 4)
        pool_hi = signal("pool_hi", 4)
        gate_ready = signal("gate_ready", 32)
        merged_hi = signal("merged_hi", 8)
        x_squared = signal("x_squared", 16, before=8)
        ff_tanh = signal("ff_tanh", FC)
        ff_hi = signal("ff_hi", FC)
        cond_tanh = signal("cond_tanh", 0)
        lo_ready = signal("lo_ready", U, before=8)
        vec_ready = signal("vec_ready", 1)
        x_ms_ready = signal("x_ms_ready", 2)
        x_normed = signal("x_normed", 16)
        h_ready = signal("h_ready", 16)
        q_ms_ready = signal("q_ms_ready", 10)
        q_mixed = signal("q_mixed", 10)
        k_ready = signal("k_ready", 2)
        v_ready = signal("v_ready", 2)
        max_ready = signal("max_ready", 24)
        probs_ready = signal("probs_ready", 24)
        attn_ready = signal("attn_ready", 24)
        mod_ready = signal("mod_ready", 16)
        next_ready = signal("next_ready", 8, before=8)
        mod_added = signal("mod_added", 16)
        next_added = signal("next_added", 8, before=8)
        gain_ready = signal("gain_ready", 5)
        conv_ready = signal("conv_ready", 4)
        conv_split = signal("conv_split", 4)
        pool_ready = signal("pool_ready", 4)
        pool_split = signal("pool_split", 4)
        merge_begun = signal("merge_begun", 8)
        merge_product = signal("merge_product", 24)
        merged_split = signal("merged_split", 8)
        x_ready = signal("x_ready", 16, before=8)
        ff_prod = signal("ff_prod", FC)
        ff_split = signal("ff_split", FC)
        evicted = signal("evicted", 0)
        cond_ready = signal("cond_ready", 0)
        dve_step = ctx.enter_context(nc.semaphore("dve_step"))
        x_rs_ready = signal("x_rs_ready", 2)
        q_rs_ready = signal("q_rs_ready", 10)
        x_summed = signal("x_summed", 14, before=7)
        pads_zeroed = signal("pads_zeroed", 2)
        merge_done = signal("merge_done", 24)
        window_sums = signal("window_sums", 4)
        pool_step = ctx.enter_context(nc.semaphore("pool_step"))
        loaded = signal("loaded", 0, step=16)
        vectors_in = signal("vectors_in", 0, step=16)
        tok_in = signal("tok_in", 0, step=16)
        past_in = signal("past_in", 1, step=16 * 2)
        vals_in = signal("vals_in", 1, step=16 * 2)
        pw_in = signal("pw_in", 1, step=16)
        kv_stored = signal("kv_stored", 1, step=16 * 4)
        y_stored = signal("y_stored", 0, step=16)

        block = ctx.enter_context(nc.Block())

        def load_vector(engine, k):
            rows = [
                (V_BMOD, 48, io["b_mod"]), (V_GMIX, 8, io["g_mix"]), (V_GFFN, 8, io["g_ffn"]),
                (V_CONV, 12, io["conv_w"]), (V_PSC, 4, io["pool_scale"]),
            ]
            if k < 5:
                r, n, src = rows[k]
                src = src.rearrange("l a (k p) -> (a k) l p", p=P) if k == 3 else src.rearrange("l (k p) -> k l p", p=P)
                engine.dma_start(vec_raw[r:r + n, :, :], src).then_inc(vectors_in.sem, 16)
            elif k < 9:
                g = k - 5
                src = io[("gq_attn", "gk_attn", "gq_win", "gk_win")[g]].unsqueeze(1).unsqueeze(0)
                engine.dma_start(vec_raw[V_GAIN + g:V_GAIN + g + 1, :, :].rearrange("a l (r c) -> a l r c", r=2),
                                 src.broadcast_to([1, DEPTH, 2, HD])).then_inc(vectors_in.sem, 16)
            else:
                src = io["sink_win"].rearrange("l h -> (l h)").unsqueeze(0)
                engine.dma_start(sink[:, :, :].rearrange("p l h -> p (l h)"), src.broadcast_to([P, DEPTH * NQ]))\
                    .then_inc(vectors_in.sem, 16)

        next_bank = [sc[:, 1, :], tr[:, 1, :]]
        start_bank = [bank[:, 3, :], tr[:, 1, :], sc[:, 0, :], sc[:, 1, :]]

        def next_group(k):
            return k // 2 + 4 * (k % 2)

        def start_slot(k):
            return start_w[:, k % 6, :] if k % 6 < 4 else mod_w[:, k % 6 - 4, :]

        def sums_of(w):
            return (ps_a, ps_b)[(w.bit_length() - 2) % 2]

        def mod_index(i, it):
            return i + it * 6 if i < 12 else 12 + it

        def mod_load_index(i, it):
            return i // 2 + it * 3 if i < 12 else 6 + it

        def run_hooks(engine, l, n, it, hook, takes):
            hooks = HOOKS[n]
            for what, i in hooks:
                if not what.endswith("_next"):
                    hook(l, what, i, it)
            following = [h for h in hooks if h[0] in takes]
            if following:
                with engine.If(l < DEPTH - 1):
                    for what, i in following:
                        hook(l, what, i, it)

        def load_mod(engine, w, l, columns, done):
            src = io["w_mod"][l].rearrange("(k p) c -> p k c", p=P)
            to = w.rearrange("p (k c) -> p k c", k=DC)
            for k in (slice(4, 8), slice(0, 4)):
                engine.dma_start(to[:, k, :], src[:, k, columns]).then_inc(done, 16)

        def weights_of(n, to):
            u = UNITS[n]
            K, j, slot = u["K"], u["part"], u["slab"] % RING
            if u["shape"] == "pair":
                dst = to[:, n % RING, :].rearrange("p (k g c) -> p k g c", k=DC, g=2)
                return dst, raw[:, slot, :].rearrange("p (k g i c) -> p k g i c", k=DC, g=2, i=2)[:, :, :, j, :]
            dst = to[:, n % RING, 0:K * P].rearrange("p (k c) -> p k c", k=K)
            return dst, raw[:, slot, 0:K * 2 * P].rearrange("p (k c) -> p k c", k=K)[:, :, P * j:P * j + P]

        @block.sync
        def _(sp):
            def slab(l, s, it=0, per=0):
                slot = s % RING
                layer = l % DEPTH if s < 2 and not isinstance(l, int) else l
                before, wrap = (s - RING) % S, U if s < RING else 0
                sp.wait_ge(*lo_ready(l, LAST_UNIT[before] - wrap + it * (2 * per)))
                dst, done = raw[:, slot, :], slab_in[slot].sem

                def load(to, rows):
                    sp.dma_start(to, rows).then_inc(done, 16)

                def columns(w, c0, n=256, K=DC, r0=0):
                    to = dst[:, 0:K * n].rearrange("p (k c) -> p k c", k=K)
                    a = w.rearrange("(k p) c -> p k c", p=P)[:, r0:r0 + K, c0 if isinstance(c0, slice) else slice(c0, c0 + n)]
                    load(to[:, 0:K // 2, :], a[:, 0:K // 2, :])
                    load(to[:, K // 2:K, :], a[:, K // 2:K, :])

                what = SLABS[s]
                if what[0] == "in":
                    c0 = bass.ds(what[1] + it * (2 * D), 256) if per else what[1]
                    w = io["w_in"][layer].rearrange("(k p) c -> p k c", p=P)
                    to = dst.rearrange("p (k c) -> p k c", k=DC)
                    c = c0 if per else slice(c0, c0 + 256)
                    load(to[:, 0:4, :], w[:, 0:4, c])
                    load(to[:, 4:8, :], w[:, 4:8, c])
                elif what[0] == "pair":
                    w = io["w_in"][layer].rearrange("(k p) c -> p k c", p=P)
                    to = dst.rearrange("p (k g c) -> p k g c", k=DC, g=2)
                    for g in (1, 0):
                        load(to[:, :, g, :], w[:, :, what[1] + 256 * g:what[1] + 256 * g + P])
                elif what[0] in ("branch", "heads"):
                    _, branch, c0 = what
                    to = dst[:, 0:4 * 256].rearrange("p (k c) -> p k c", k=4)
                    c = slice(c0, c0 + 256)
                    if what[0] == "branch":
                        w = io["w_branch"][l, branch].rearrange("(k p) c -> p k c", p=P)
                        load(to[:, 0:2, :], w[:, 0:2, c])
                        load(to[:, 2:4, :], w[:, 2:4, c])
                    else:
                        w = io["w_branch"][l, 2 * it].rearrange("(g i p) c -> g p i c", g=2, i=4)
                        for g in range(2):
                            load(to[64 * g:64 * g + 64, :, :], w[g, :, :, c])
                elif what[0] == "out":
                    columns(io["w_out"][l], 256 * what[1])
                elif what[0] == "gu":
                    w = io["w_gate_up"][l].rearrange("(k p) c -> p k c", p=P)
                    to = dst.rearrange("p (k c) -> p k c", k=DC)
                    c = bass.ds(what[1] + it * 512, 256) if per else slice(what[1], what[1] + 256)
                    load(to[:, 0:4, :], w[:, 0:4, c])
                    load(to[:, 4:8, :], w[:, 4:8, c])
                else:
                    _, s4, k0, K = what
                    columns(io["w_down"][l], 256 * s4, K=K, r0=k0)

            sp.dma_start(const[:, :], io["const"]).then_inc(loaded.sem, 16)
            sp.dma_start(c_raw[0:DC, :], io["c"].rearrange("a (k p) -> (a k) p", p=P)).then_inc(loaded.sem, 16)
            sp.dma_start(c_raw[DC:2 * DC, :], io["c_ctx"].rearrange("(k p) -> k p", p=P)).then_inc(loaded.sem, 16)
            for k in range(10):
                load_vector(sp, k)
            for k in range(8):
                if k == 2:
                    slab(0, 0)
                    slab(0, 1)
                if k >= 6:
                    sp.wait_ge(*next_sum(0, k - 6 - 8))
                g = next_group(k)
                load_mod(sp, start_slot(k), 0, slice(256 * g, 256 * g + 256), start_in[k % 6].sem)
            a0, a1 = UNITS[N_AC]["slab"], UNITS[N_O]["slab"]
            f1, d0 = UNITS[N_F + 4]["slab"], UNITS[N_D]["slab"]
            assert (a1 - a0) == 16 and (d0 - f1) == 20
            stores = UNITS[N_P + 8]["slab"]
            with sp.Fori(0, DEPTH) as l:
                for s in range(2, a0):
                    if s == stores:
                        for m, name in enumerate(("attn", "win")):
                            sp.wait_ge(*k_out_ready(l, m))
                            sp.dma_start(io["k_" + name][0, l].rearrange("t h c -> t (h c)"), k_out[:, m, :]).then_inc(kv_stored.sem, 16)
                            sp.wait_ge(*v_ready(l, m))
                            sp.dma_start(io["v_" + name][0, l].rearrange("t h c -> t (h c)"), vals[:, m, TT, :]).then_inc(kv_stored.sem, 16)
                    slab(l, s)
                with sp.Fori(0, 2) as it:
                    for s in range(a0, a0 + 8):
                        slab(l, s, it, 8)
                for s in range(a1, f1):
                    slab(l, s)
                with sp.Fori(0, 5) as it:
                    for s in range(f1, f1 + 4):
                        slab(l, s, it, 4)
                for s in range(d0, S):
                    slab(l, s)
                with sp.If(l < DEPTH - 1):
                    slab(l + 1, 0)
                    slab(l + 1, 1)
            for t in range(TT):
                sp.wait_ge(*evicted(0, 2 * DEPTH + 2 * t + 1))
                to = io["y_sample"][0, P * t:P * t + P, :] if t < 2 else io["y_prompt"][0]
                sp.dma_start(to, tok[:, t, :]).then_inc(y_stored.sem, 16)
            sp.wait_ge(*kv_stored(DEPTH - 1, 0))
            sp.wait_ge(*y_stored(0, TT - 1))

        @block.tensor
        def _(pe):
            def parts(n, k):
                K = UNITS[n]["K"]
                a = slice(k * P, k * P + P)
                return w_hi[:, n % RING, a], w_lo[:, n % RING, a]

            def product(out, w, r, start, stop):
                pe.matmul(out, w[1], r[0], start=start, stop=False)
                pe.matmul(out, w[0], r[1], start=False, stop=False)
                return pe.matmul(out, w[0], r[0], start=False, stop=stop)

            def right_operand(n, k, it):
                u = UNITS[n]
                kind = u["kind"]
                if kind == "proj":
                    if n >= N_AC:
                        c = bass.ds(8 + k + it * 4, 1)
                        return [v[:, c, :].rearrange("p a t -> p (a t)") for v in (br_hi, br_lo)]
                    c = (n - N_G) // 16 * 4 + k
                    return br_hi[:, c, :], br_lo[:, c, :]
                if kind == "out":
                    return br_hi[:, k, :], br_lo[:, k, :]
                if kind == "down":
                    return f_hi[:, u["k0"] + k, :], f_lo[:, u["k0"] + k, :]
                return h_hi[:, k, :], h_lo[:, k, :]

            def out_bank(n):
                u = UNITS[n]
                b = (u["i"] % 4) if u["kind"] == "down" else n % RING
                return bank[:, b, 0:T]

            def unit(l, n, it=0, per=0):
                u = UNITS[n]
                pe.wait_ge(*lo_ready(l, n + it * per))
                first, last = u.get("first", True), u.get("last", True)
                for k in range(u["K"]):
                    ins = product(out_bank(n), parts(n, k), right_operand(n, k, it),
                                  first and k == 0, last and k == u["K"] - 1)
                ins.then_inc(unit_done.sem, 1)

            def three_units(l, n, chunk_ready, chunks=range(DC)):
                if chunks[0] == 0:
                    for m in range(n, n + 3):
                        pe.wait_ge(*lo_ready(l, m))
                for k in chunks:
                    pe.wait_ge(*chunk_ready(k))
                    for m in range(n, n + 3):
                        ins = product(out_bank(m), parts(m, k), right_operand(m, k, 0), k == 0, k == DC - 1)
                        if k == DC - 1:
                            ins.then_inc(unit_done.sem, 1)

            def statistics(l, which):
                pe.wait_ge(*x_summed(l, 7 * which - 1))
                pe.wait_ge(*x_squared(l, 8 * which - 1))
                for t in range(TT):
                    part = slice(P * t, P * t + P)
                    pe.matmul(tr[:, 0, t:t + 1], x_acc[:, part], const[:, K_MEAN:K_MEAN + 1], start=True, stop=False)
                    ins = pe.matmul(tr[:, 0, t:t + 1], x_sq[:, 1, part], const[:, K_MEAN:K_MEAN + 1], start=False, stop=True)
                ins.then_inc(x_stat.sem, 1)

            def broadcast(l, which):
                pe.wait_ge(*x_rs_ready(l, which))
                for t in range(TT):
                    ins = pe.transpose(tr[:, 0, P * t:P * t + P], x_rs[:, t:t + 1].broadcast_to([P, P]), ident)
                ins.then_inc(x_bcast.sem, 1)

            def mod_matmul(out, w, done):
                w = w.rearrange("p (k c) -> p k c", k=DC)
                for k in range(DC):
                    j = k % 4
                    ins = pe.matmul(out[32 * j:32 * j + 32, 0:2 * P], cond[:, k, :], w[:, k, :], start=k < 4, stop=k >= 4)
                ins.then_inc(done, 1)

            def mod_turn(out, row, done):
                for y in range(2):
                    ins = pe.transpose(out[:, P * y:P * y + P], row[:, P * y:P * y + P], ident)
                ins.then_inc(done, 1)

            reader = {}

            def claim(b):
                if reader.get(b):
                    pe.wait_ge(*reader[b])

            def hook(l, what, i, it):
                if what == "mod":
                    f, slot = mod_index(i, it), i % 2
                    pe.wait_ge(*mod_in[slot](l, mod_load_index(i, it)))
                    if i >= 12:
                        pe.wait_ge(*mod_ready(l, f - 1))
                    elif i >= 2:
                        pe.wait_ge(*mod_ready(l, f - 2))
                    mod_matmul(sc[:, slot, :], mod_w[:, slot, :], mod_sum.sem)
                elif what == "sel":
                    pe.wait_ge(*mod_row_ready(l, mod_index(i, it)))
                    mod_turn(sc[:, i % 2, :], mod_row[:, i % 2, :], mod_col.sem)
                elif what == "mod_next":
                    pe.wait_ge(*next_in(l, i + 2 * it))
                    pe.wait_ge(*next_ready(l, i + 2 * it - 2))
                    mod_matmul(next_bank[i], mod_w[:, 1, :], next_sum.sem)
                elif what == "sel_next":
                    pe.wait_ge(*next_row_ready(l, i + 2 * it))
                    mod_turn(next_bank[i], next_row[:, i, :], next_col.sem)
                elif what == "stat":
                    pe.wait_ge(*q_copied(l, i))
                    claim(1)
                    pe.matmul(tr[:, 1, 0:T_LAT], const[:, K_PERM:K_PERM + P], q_raw[:, i % 3, LAT], start=True, stop=True)
                    for t in range(TT):
                        ins = pe.matmul(tr[:, 1, T_LAT + 2 * t:T_LAT + 2 * t + 2], q_sq[:, i % 2, P * t:P * t + P],
                                        const[:, K_HEAD:K_HEAD + 2], start=True, stop=True)
                    ins.then_inc(q_stat.sem, 1)
                    reader[1] = q_mixed(l, i)
                elif what == "rnorm":
                    pe.wait_ge(*q_rs_ready(l, i))
                    claim(0)
                    for t in range(TT):
                        for g in range(2):
                            c = 2 * t + g
                            ins = pe.matmul(tr[64 * g:64 * g + 64, 0, P * t:P * t + P],
                                            q_rs[:, i, c:c + 1].broadcast_to([P, 64]), ident, start=True, stop=True)
                    ins.then_inc(q_bcast.sem, 1)
                    reader[0] = k_ready(l, i)
                elif what == "vt":
                    pe.wait_ge(*v_copied(l, i))
                    claim(0)
                    for t in range(TT):
                        ins = pe.transpose(tr[:, 0, P * t:P * t + P], v_t[:, i, P * t:P * t + P], ident)
                    ins.then_inc(v_turned.sem, 1)
                    reader[0] = v_ready(l, i)
                elif what == "kout":
                    pe.wait_ge(*k_ready(l, i))
                    claim(1)
                    pe.transpose(tr[:, 1, 0:P], keys[:, i, PAST + T_LAT:PAST + T], ident).then_inc(k_turned.sem, 1)
                    reader[1] = k_out_ready(l, i)
                elif what == "cache":
                    pe.wait_ge(*past_in(l, 0))
                    claim(1)
                    pe.transpose(tr[:, 1, 0:P], k_past[:, i, :], ident).then_inc(past_turned.sem, 1)
                    reader[1] = past_ready(l, i)
                elif what == "scores":
                    m, c, t = i // 12, i % 12 // 3, i % 3
                    pe.wait_ge(*q_mixed(l, 2 + 4 * m + c))
                    pe.wait_ge(*k_ready(l, m))
                    pe.wait_ge(*past_ready(l, m))
                    if i:
                        pe.wait_ge(*exps(l, i - 1))
                    ks = slice(0, PAST + T_LAT) if t < 2 else slice(PAST + T_LAT, PAST + T)
                    for g in range(2):
                        a = slice(64 * g, 64 * g + 64)
                        ins = pe.matmul(sc[:, g, 0:ks.stop - ks.start], q[a, 4 * m + c, P * t:P * t + P], keys[a, m, ks],
                                        start=True, stop=True)
                    ins.then_inc(scores.sem, 1)
                elif what == "probsT":
                    pe.wait_ge(*probs_ready(l, i))
                    claim(0)
                    claim(1)
                    for g in range(2):
                        for b in range(3 if i % 3 < 2 else 1):
                            ins = pe.transpose(tr[:, g, P * b:P * b + P], prob[:, i % 2, g, P * b:P * b + P], ident)
                    ins.then_inc(probs_turned.sem, 1)
                    reader[0] = reader[1] = probs_t_ready(l, i)
                elif what == "attn":
                    m, t = i // 12, i % 3
                    pe.wait_ge(*probs_t_ready(l, i))
                    pe.wait_ge(*v_ready(l, m))
                    pe.wait_ge(*vals_in(l, 0))
                    claim(0)
                    reader[0] = attn_ready(l, i)
                    tiles = (0, 1, 2) if t < 2 else (3,)
                    for b, v in enumerate(tiles):
                        for g in range(2):
                            ins = pe.matmul(tr[64 * g:64 * g + 64, 0, 384:512], vals[:, m, v, 64 * g:64 * g + 64],
                                            prob_t[:, i % 2, g, b, :], start=b == 0, stop=v == tiles[-1])
                    ins.then_inc(attn_out.sem, 1)
                elif what == "pool":
                    pe.wait_ge(*pool_ready(l, i))
                    pe.wait_ge(*pw_in(l, 0))
                    n = BASE["pv"] + 8 * (i // 2) + i % 2 + 1
                    pe.wait_ge(*lo_ready(l, n + 4))
                    for to, at in ((LAT, 16), (CTX, 32 + T_LAT)):
                        ins = pe.matmul(bank[:, n % RING, to], pw[:, i, :], pin[:, i % 2, at:at + to.stop - to.start],
                                        start=True, stop=True)
                    ins.then_inc(pooled.sem, 1)

            def after(l, n, it=0):
                run_hooks(pe, l, n, it, hook, ("mod_next", "sel_next"))

            pe.nop().then_inc(unit_done.sem, RING)
            pe.wait_ge(*loaded(0, 2))
            pe.wait_ge(*tok_in(0, TT - 1))
            for k in range(DC):
                if k >= RING:
                    pe.wait_ge(*x_ready(0, k - RING - 8))
                for t in range(TT):
                    ins = pe.transpose(bank[:, k % RING, P * t:P * t + P], tok[:, t, P * k:P * k + P], ident)
                ins.then_inc(turned.sem, 1)
            pe.transpose(tr[:, 1, 0:2 * DC], c_raw[:, :], const[0:2 * DC, K_ID:K_ID + 2 * DC]).then_inc(turned.sem, 1)
            pe.wait_ge(*vectors_in(0, 9))
            for l in range(DEPTH):
                if l:
                    pe.wait_ge(*evicted(0, 2 * l - 1))
                pe.transpose(tr[:, 0, P * l:P * l + NV], vec_raw[:, l, :], const[0:NV, K_ID:K_ID + NV]).then_inc(turned.sem, 1)
                pe.wait_ge(*evicted(0, 2 * l))
                pe.matmul(tr[:, 0, 256 + 4 * l:256 + 4 * l + 4], const[:, K_PERM:K_PERM + P],
                          vec_all[:, l, V_GAIN:V_GAIN + 4], start=True, stop=True).then_inc(turned.sem, 1)
            pe.wait_ge(*evicted(0, 2 * DEPTH - 1))
            pe.wait_ge(*cond_ready(0, 1))
            for j in range(4):
                for k in (2 * j, 2 * j + 1):
                    pe.wait_ge(*start_in[k % 6](0, k // 6))
                    if k >= 4:
                        pe.wait_ge(*next_ready(0, k - 4 - 8))
                    mod_matmul(start_bank[k % 4], start_slot(k), next_sum.sem)
                for k in (2 * j, 2 * j + 1):
                    pe.wait_ge(*next_row_ready(0, k - 8))
                    mod_turn(start_bank[k % 4], next_row[:, k % 2, :], next_col.sem)
                if j == 0:
                    statistics(0, 0)
                    broadcast(0, 0)
                    three_units(0, N_Q, lambda k: h_ready(0, k), range(2))
                if j > 1:
                    three_units(0, N_Q, lambda k: h_ready(0, k), range(2 * j - 2, 2 * j))
            three_units(0, N_Q, lambda k: h_ready(0, k), range(6, 8))

            with pe.Fori(0, DEPTH) as l:
                reader.clear()
                for n in range(0, 3):
                    after(l, n)
                for n in range(3, N_AC):
                    if n == N_G + 4:
                        pe.wait_ge(*conv_split(l, CC - 1))
                    if n == N_G + 16 + 4:
                        pe.wait_ge(*pool_split(l, CC - 1))
                    if n >= 5 and UNITS[n - 5]["kind"] == "pv":
                        pe.wait_ge(*pool_split(l, UNITS[n - 5]["i"]))
                    unit(l, n)
                    after(l, n)
                with pe.Fori(0, 2) as it:
                    for n in range(N_AC, N_AC + 16):
                        if n == N_AC + 4:
                            pe.wait_ge(*attn_ready(l, 11 + it * 12))
                        unit(l, n, it, 16)
                        after(l, n, it)
                three_units(l, N_O, lambda k: merged_split(l, k))
                for n in range(N_O + 3, N_F):
                    unit(l, n)
                statistics(l, 1)
                broadcast(l, 1)
                three_units(l, N_F, lambda k: h_ready(l, 8 + k))
                unit(l, N_F + 3)
                with pe.Fori(0, 4) as it:
                    for n in range(N_F + 4, N_F + 12):
                        unit(l, n, it, 8)
                        after(l, n, it)
                for n in range(N_F + 36, N_D):
                    unit(l, n)
                for n in range(N_D, U):
                    if n < N_D + 8 and n % 2 == 0:
                        pe.wait_ge(*ff_split(l, UNITS[n]["k0"] + UNITS[n]["K"] - 1))
                    unit(l, n)
                with pe.If(l < DEPTH - 1):
                    statistics(l + 1, 0)
                    broadcast(l + 1, 0)
                    three_units(l + 1, N_Q, lambda k: h_ready(l + 1, k))

            pe.wait_ge(*x_ready(DEPTH - 1, 15))
            for k in range(2 * TT):
                if k >= RING:
                    pe.wait_ge(*evicted(0, 2 * DEPTH + (k - RING)))
                for c in range(4):
                    ins = pe.transpose(bank[:, k % RING, P * c:P * c + P],
                                       x[:, 4 * (k % 2) + c, P * (k // 2):P * (k // 2) + P], ident)
                ins.then_inc(turned.sem, 1)

        @block.scalar
        def _(act):
            def split(l, n, it=0, per=0, spi=0):
                u = UNITS[n]
                s = u["slab"]
                act.wait_ge(*slab_in[s % RING](l, s // RING + it * (spi // RING)))
                act.wait_ge(*unit_done(l, n - RING + it * per))
                to, src = weights_of(n, w_hi)
                act.copy(to, src).then_inc(hi_ready.sem, 1)

            def post(l, n, it=0, per=0):
                u = UNITS[n]
                kind, i = u["kind"], u["i"]
                ps = bank[:, n % RING, 0:T]
                if kind in ("out", "proj", "b", "gc"):
                    if kind == "b":
                        k = i + it * 4
                        act.wait_ge(*ff_prod(l, k))
                        c = bass.ds(k, 1) if per else slice(i, i + 1)
                        act.mul(f_hi[:, c, :].rearrange("p a t -> p (a t)"), ff_f[:, i % 2, :], 0.5).then_inc(ff_hi.sem, 1)
                    if kind == "out":
                        square(l, i)
                    return
                if kind == "down":
                    if u["last"]:
                        square(l, 8 + i)
                    return
                act.wait_ge(*unit_done(l, n + it * per))
                if kind == "norm":
                    if i >= 2:
                        act.wait_ge(*q_stat(l, i - 2))
                    act.activation(q_sq[:, i % 2, :], ps, ACT.Square)
                    if i >= 3:
                        act.wait_ge(*q_mixed(l, i - 3))
                    act.copy(q_raw[:, i % 3, :], ps).then_inc(q_copied.sem, 1)
                elif kind == "v":
                    act.copy(v_t[:, i, :], ps).then_inc(v_copied.sem, 1)
                elif kind == "u":
                    act.copy(cu[:, i % 2, :], ps).then_inc(conv_in.sem, 1)
                elif kind == "gb":
                    act.copy(cgb[:, i % 2, :], ps).then_inc(conv_in.sem, 1)
                elif kind == "pv":
                    if i == 0:
                        act.wait_ge(*pads_zeroed(l, 1))
                    if i >= 2:
                        act.wait_ge(*pooled(l, i - 2))
                    act.copy(pin[:, i % 2, 16:16 + T_LAT], ps[:, LAT])
                    act.copy(pin[:, i % 2, 32 + T_LAT:32 + T], ps[:, CTX]).then_inc(pool_in.sem, 1)
                elif kind == "gate":
                    if n == N_G:
                        act.wait_ge(*conv_ready(l, CC - 1))
                    if i >= 12:
                        act.wait_ge(*merge_done(l, i - 12 + it * 8))
                    elif i >= 4:
                        act.wait_ge(*merge_begun(l, i - 4))
                    act.activation(gate_t[:, i % 4, :], ps, ACT.Tanh, scale=0.5).then_inc(gate_ready.sem, 1)
                elif kind == "a":
                    act.activation(ff_t[:, i % 2, :], ps, ACT.Tanh, scale=0.5).then_inc(ff_tanh.sem, 1)

            def square(l, k):
                act.wait_ge(*x_ready(l, k))
                if k % 8 == 1:
                    act.wait_ge(*x_stat(l, k // 8))
                else:
                    act.wait_ge(*x_summed(l, (k - 2) // 8 * 7 + (k - 2) % 8))
                act.activation(x_sq[:, k % 2, :], x[:, k % 8, :], ACT.Square).then_inc(x_squared.sem, 1)

            def hook(l, what, i, it):
                if what == "load":
                    f, slot = mod_index(i, it), i % 2
                    if i < 2:
                        act.wait_ge(*attn_ready(l, 23))
                    if i >= 2:
                        act.wait_ge(*mod_sum(l, f - (2 if i < 12 else 1)))
                    columns = bass.ds(256 * (8 + i) + it * (6 * 256), 256) if i < 12 else bass.ds(256 * 20 + it * 256, 256)
                    load_mod(act, mod_w[:, slot, :], l, columns, mod_in[slot].sem)
                elif what == "mod":
                    f = mod_index(i, it)
                    act.wait_ge(*mod_sum(l, f))
                    if i >= 2:
                        act.wait_ge(*mod_col(l, f - (2 if i < 12 else 1)))
                    act.copy(mod_row[:, i % 2, :], sc[:, i % 2, 0:2 * P]).then_inc(mod_row_ready.sem, 1)
                elif what == "load_next":
                    k = i + 2 * it
                    if i:
                        act.wait_ge(*next_sum(l, k - 1))
                    else:
                        act.wait_ge(*mod_sum(l, 11))
                    load_mod(act, mod_w[:, 1, :], (l + 1) % DEPTH, bass.ds(256 * next_group(i) + it * 256, 256), next_in.sem)
                elif what == "mod_next":
                    act.wait_ge(*next_sum(l, i + 2 * it))
                    act.wait_ge(*next_col(l, i + 2 * it - 2))
                    act.copy(next_row[:, i, :], next_bank[i][:, 0:2 * P]).then_inc(next_row_ready.sem, 1)
                elif what == "kout":
                    act.wait_ge(*k_turned(l, i))
                    act.copy(k_out[:, i, :], tr[:, 1, 0:P]).then_inc(k_out_ready.sem, 1)
                elif what == "cache":
                    act.wait_ge(*past_turned(l, i))
                    act.copy(keys[:, i, 0:PAST], tr[:, 1, 0:P]).then_inc(past_ready.sem, 1)
                elif what == "scores":
                    act.wait_ge(*max_ready(l, i))
                    if i >= 2:
                        act.wait_ge(*probs_turned(l, i - 2))
                    nk = PAST + T_LAT if i % 3 < 2 else T_CTX
                    c = 2 + 4 * (i // 12) + i % 12 // 3
                    for g in range(2):
                        r = 2 * (i % 3) + g
                        ins = act.activation(prob[:, i % 2, g, 0:nk], sc[:, g, 0:nk], ACT.Exp, scale=q_rs[:, c, r:r + 1],
                                             bias=s_nm[i % 2][:, g:g + 1], accum_out=s_sum[i % 2][:, g:g + 1])
                    ins.then_inc(exps.sem, 1)
                    if i >= 12:
                        act.activation(s_se, s_sd, ACT.Exp).then_inc(sink_exp.sem, 1)
                elif what == "probsT":
                    act.wait_ge(*probs_turned(l, i))
                    if i >= 2:
                        act.wait_ge(*attn_out(l, i - 2))
                    nb = 3 if i % 3 < 2 else 1
                    act.copy(prob_t[:, i % 2, :, 0:nb, :], tr[:, :, 0:P * nb].rearrange("p g (b q) -> p g b q", b=nb))\
                        .then_inc(probs_t_ready.sem, 1)
                elif what == "attn":
                    m, c, t = i // 12, i % 12 // 3, i % 3
                    act.wait_ge(*attn_out(l, i))
                    act.copy(br_hi[:, 8 + 4 * m + c, P * t:P * t + P], tr[:, 0, 384:512]).then_inc(attn_hi.sem, 1)
                elif what == "conv":
                    act.wait_ge(*conv_ready(l, i))
                    act.copy(br_hi[:, i, LAT], cy[:, i % 2, 0:T_LAT])
                    act.copy(br_hi[:, i, CTX], cy[:, i % 2, T_LAT + 1:T + 1]).then_inc(conv_hi.sem, 1)
                elif what == "poolsplit":
                    act.wait_ge(*pooled(l, i))
                    n = BASE["pv"] + 8 * (i // 2) + i % 2
                    act.activation(br_hi[:, 4 + i, :], bank[:, (n + 1) % RING, 0:T], ACT.Identity,
                                   scale=vec[:, V_PSC + i:V_PSC + i + 1]).then_inc(pool_hi.sem, 1)

            def norm(l, which, start=None):
                shift = (M_SH1, M_SH2)[which]

                for d in range(DC):
                    if which == 0 and d % 2 == 0:
                        if d and start:
                            start(d // 2)
                        act.wait_ge(*gain_ready(l, d // 2))
                    elif d == 0:
                        act.wait_ge(*gain_ready(l, 4))
                    act.wait_ge(*x_normed(l, 8 * which + d))
                    for c, part in enumerate((LAT, CTX)):
                        ins = act.activation(h_hi[:, d, part], nx[:, d % 4, part], ACT.Identity,
                                             scale=gain[:, which, d, c:c + 1], bias=modc[:, shift + d, c:c + 1])
                    ins.then_inc(h_hi_ready.sem, 1)

            def slot(l, n, it=0, per=0, spi=0):
                if n + LOOKAHEAD >= U:
                    with act.If(l < DEPTH - 1):
                        split(l + 1, n + LOOKAHEAD - U)
                else:
                    split(l, n + LOOKAHEAD, it, per, spi)
                run_hooks(act, l, n, it, hook, ("load_next", "mod_next"))
                post(l, n, it, per)

            for t in range(TT):
                rows = io["x_sample"][0, P * t:P * t + P, :] if t < 2 else io["x_prompt"][0]
                act.dma_start(tok[:, t, :], rows).then_inc(tok_in.sem, 16)
            for k in range(DC):
                if k == 4:
                    act.wait_ge(*turned(0, DC))
                    act.activation(cond_t[:, 0, :], tr[:, 1, 0:2 * DC], ACT.Tanh, scale=0.5).then_inc(cond_tanh.sem, 1)
                    act.copy(cond_t[:, 1, :], tr[:, 1, 0:2 * DC]).then_inc(cond_tanh.sem, 1)
                act.wait_ge(*x_ready(0, k - 8))
                if k >= 2:
                    act.wait_ge(*x_summed(0, k - 2 - 7))
                act.activation(x_sq[:, k % 2, :], x[:, k, :], ACT.Square).then_inc(x_squared.sem, 1)

            def start(j):
                for k in (2 * j, 2 * j + 1):
                    act.wait_ge(*next_sum(0, k - 8))
                    if k >= 2:
                        act.wait_ge(*next_col(0, k - 2 - 8))
                    act.copy(next_row[:, k % 2, :], start_bank[k % 4][:, 0:2 * P]).then_inc(next_row_ready.sem, 1)

            start(0)
            for n in range(LOOKAHEAD):
                split(0, n)
            norm(0, 0, start)

            with act.Fori(0, DEPTH) as l:
                for n in range(0, N_AC):
                    slot(l, n)
                with act.Fori(0, 2) as it:
                    for n in range(N_AC, N_AC + 16):
                        slot(l, n, it, 16, 8)
                for d in range(DC):
                    act.wait_ge(*merge_done(l, 16 + d))
                    act.mul(br_hi[:, d, :], merged[:, d, :], 0.5).then_inc(merged_hi.sem, 1)
                for n in range(N_O, N_F):
                    slot(l, n)
                norm(l, 1)
                for n in range(N_F, N_F + 4):
                    slot(l, n)
                with act.Fori(0, 4) as it:
                    for n in range(N_F + 4, N_F + 12):
                        slot(l, n, it, 8, 4)
                for n in range(N_F + 36, U):
                    slot(l, n)
                with act.If(l < DEPTH - 1):
                    norm(l + 1, 0)

        @block.vector
        def _(dve):
            chain = Steps(dve_step, sizes, "dve")

            def split(l, n, it=0, per=0):
                dve.wait_ge(*hi_ready(l, n + it * per))
                to, src = weights_of(n, w_lo)
                hi, _ = weights_of(n, w_hi)
                dve.tensor_tensor(to, src, hi.bitcast(F32), ALU.subtract).then_inc(lo_ready.sem, 1)

            def lo_part(to, x_, hi, scale=None):
                if scale is None:
                    return dve.tensor_tensor(to, x_, hi.bitcast(F32), ALU.subtract)
                return dve.scalar_tensor_tensor(to, x_, scale, hi.bitcast(F32), ALU.mult, ALU.subtract)

            def residual(l, n, k):
                u = UNITS[n]
                b = (u["i"] % 4) if u["kind"] == "down" else n % RING
                g = (M_G1 if k < 8 else M_G2) + k % 8
                for c, part in enumerate((LAT, CTX)):
                    xs = x[:, k % 8, part]
                    ins = dve.scalar_tensor_tensor(xs, bank[:, b, part], modc[:, g, c:c + 1], xs, ALU.mult, ALU.add)
                ins.then_inc(x_ready.sem, 1)

            def before_split(l, n, it, per):
                u = UNITS[n]
                kind, i = u["kind"], u["i"]
                ps = bank[:, n % RING, 0:T]
                if kind == "out":
                    dve.wait_ge(*unit_done(l, n))
                    residual(l, n, i)
                elif kind == "down" and u["last"]:
                    dve.wait_ge(*unit_done(l, n))
                    residual(l, n, 8 + i)
                elif kind == "b":
                    dve.wait_ge(*unit_done(l, n + it * per))
                    dve.wait_ge(*ff_made[i % 2])
                    dve.tensor_tensor(ff_f[:, i % 2, :], ff_s[:, i % 2, :], ps, ALU.mult).then_inc(ff_prod.sem, 1)
                elif kind == "gc":
                    dve.wait_ge(*unit_done(l, n))
                    dve.wait_ge(*conv_in(l, 4 * (i // 2) + 3))
                    if i == 0:
                        dve.wait_ge(*pads_zeroed(l, 1))
                    dve.tensor_tensor(cz[:, 1:1 + T_LAT], cu[:, i % 2, LAT], ps[:, LAT], ALU.mult)
                    made["z"] = chain.made(dve.tensor_tensor(cz[:, 2 + T_LAT:2 + T], cu[:, i % 2, CTX], ps[:, CTX], ALU.mult))
                elif kind == "proj":
                    b, d = i // 8, i % 8
                    dve.wait_ge(*unit_done(l, n + it * per))
                    dve.wait_ge(*gate_ready(l, i + it * 8))
                    t = gate_t[:, d % 4, :]
                    if b == 0:
                        dve.scalar_tensor_tensor(merged[:, d, :], t, 1.0, ps, ALU.add, ALU.mult).then_inc(merge_begun.sem, 1)
                    else:
                        dve.scalar_tensor_tensor(t, t, 1.0, ps, ALU.add, ALU.mult).then_inc(merge_product.sem, 1)

            def after_split(l, n, it, per):
                u = UNITS[n]
                kind, i = u["kind"], u["i"]
                ps = bank[:, n % RING, 0:T]
                if kind == "a":
                    dve.wait_ge(*ff_tanh(l, i + it * 4))
                    ff_made[i % 2] = chain.made(dve.scalar_tensor_tensor(
                        ff_s[:, i % 2, :], ff_t[:, i % 2, :], 1.0, ps, ALU.add, ALU.mult))
                elif kind == "b":
                    k = i + it * 4
                    dve.wait_ge(*ff_hi(l, k))
                    c = bass.ds(k, 1) if per else slice(i, i + 1)
                    lo_part(f_lo[:, c, :].rearrange("p a t -> p (a t)"), ff_f[:, i % 2, :],
                            f_hi[:, c, :].rearrange("p a t -> p (a t)"), 0.5).then_inc(ff_split.sem, 1)
                elif kind == "gc":
                    y, n1 = cy[:, i % 2, :], ZL - 2
                    tap = [vec[:, V_CONV + 4 * r + i:V_CONV + 4 * r + i + 1] for r in range(3)]
                    dve.wait_ge(*made["z"])
                    if i >= 2:
                        dve.wait_ge(*conv_split(l, i - 2))
                        dve.wait_ge(*conv_hi(l, i - 2))
                    s = chain.made(dve.tensor_scalar(y[:, 0:n1], cz[:, 1:1 + n1], tap[1], None, ALU.mult))
                    dve.wait_ge(*s)
                    s = chain.made(dve.scalar_tensor_tensor(y[:, 0:n1], cz[:, 0:n1], tap[0], y[:, 0:n1], ALU.mult, ALU.add))
                    dve.wait_ge(*s)
                    s = chain.made(dve.scalar_tensor_tensor(y[:, 0:n1], cz[:, 2:2 + n1], tap[2], y[:, 0:n1], ALU.mult, ALU.add))
                    dve.wait_ge(*s)
                    dve.tensor_tensor(y[:, 0:T_LAT], y[:, 0:T_LAT], cgb[:, i % 2, LAT], ALU.mult)
                    dve.tensor_tensor(y[:, T_LAT + 1:T + 1], y[:, T_LAT + 1:T + 1], cgb[:, i % 2, CTX], ALU.mult)\
                        .then_inc(conv_ready.sem, 1)

            def mod_columns(c, src, t, b, summed, done):
                tiles = src[:, 0:2 * P].rearrange("p (y j c) -> p y c j", y=2, j=4)[:, :, 0:2, :]
                dve.reduce_sum(mod_t[:, t, :, :], tiles, AXX).then_inc(summed[0], 1)
                dve.wait_ge(*summed)
                dve.tensor_tensor(modc[:, c, :], mod_t[:, t, :, :], b.unsqueeze(2).broadcast_to([P, 2, 2]), ALU.add)\
                    .then_inc(done, 1)

            def hook(l, what, i, it):
                if what == "sel":
                    dve.wait_ge(*mod_col(l, mod_index(i, it)))
                    c = 16 + 2 * i + it * 12 if i < 12 else 40 + it * 2
                    mod_columns(bass.ds(c, 2), sc[:, i % 2, :], i % 2, vec[:, bass.ds(c, 2)],
                                mod_added(l, mod_index(i, it)), mod_ready.sem)
                elif what == "sel_next":
                    dve.wait_ge(*next_col(l, i + 2 * it))
                    c = bass.ds(2 * next_group(i) + it * 2, 2)
                    b = vec_all[:, bass.ds((l + 1) % DEPTH, 1), c].rearrange("p a v -> p (a v)")
                    mod_columns(c, next_bank[i], 2 + i, b, next_added(l, i + 2 * it), next_ready.sem)
                elif what == "stat":
                    g = i if i < 2 else (i - 2) // 4
                    gi = V_GAIN + (2 * g + 1 if i < 2 else 2 * g)
                    own, other = vec[:, gi:gi + 1], vec[:, gi + 4:gi + 5]
                    dve.wait_ge(*q_stat(l, i))
                    if i >= 2:
                        dve.wait_ge(*q_rs_ready(l, i - 2))
                    ms = tr[:, 1, T_LAT:T_LAT + 6]
                    if i < 2:
                        dve.tensor_scalar(q_ms[i % 2], ms, EPS, None, ALU.add).then_inc(q_ms_ready.sem, 1)
                    else:
                        dve.tensor_scalar(q_ms[i % 2], ms, EPS, SCALE ** -2, ALU.add, ALU.mult).then_inc(q_ms_ready.sem, 1)
                    mix = q_mix[:, i % 2, :] if i < 2 else q[:, i - 2, :]
                    s = chain.made(dve.scalar_tensor_tensor(q_rot[:, :], tr[:, 1, 0:T_LAT], other, const[:, K_SIN:K_SIN + T_LAT],
                                                            ALU.mult, ALU.mult))
                    s2 = chain.made(dve.scalar_tensor_tensor(mix[:, LAT], q_raw[:, i % 3, LAT], own,
                                                             const[:, K_COS:K_COS + T_LAT], ALU.mult, ALU.mult))
                    s2 = chain.made(dve.tensor_scalar(mix[:, CTX], q_raw[:, i % 3, CTX], own, None, ALU.mult))
                    dve.wait_ge(*s2)
                    dve.tensor_tensor(mix[:, LAT], mix[:, LAT], q_rot[:, :], ALU.add).then_inc(q_mixed.sem, 1)
                elif what == "rnorm":
                    to = keys[:, i, PAST:PAST + T]
                    dve.wait_ge(*q_bcast(l, i))
                    dve.wait_ge(*q_mixed(l, i))
                    dve.tensor_tensor(to, q_mix[:, i % 2, :], tr[:, 0, 0:T], ALU.mult).then_inc(k_ready.sem, 1)
                elif what == "vt":
                    dve.wait_ge(*v_turned(l, i))
                    dve.tensor_copy(vals[:, i, 1:1 + TT, :], tr[:, 0, 0:T].rearrange("p (t c) -> p t c", c=P))\
                        .then_inc(v_ready.sem, 1)
                elif what == "scores":
                    m, t = i // 12, i % 3
                    nk = PAST + T_LAT if t < 2 else T_CTX
                    dve.wait_ge(*scores(l, i))
                    if m == 1 and t < 2:
                        at = PAST + P * (1 - t)
                        blk = sc[:, :, at:at + P]
                        mask = const[:, K_MASK + P * t:K_MASK + P * t + P].unsqueeze(1).broadcast_to([P, 2, P])
                        s = chain.made(dve.tensor_tensor(blk, blk, mask, ALU.add))
                        dve.wait_ge(*s)
                    s = chain.made(dve.reduce_max(s_max, sc[:, :, 0:nk], AXX))
                    dve.wait_ge(*s)
                    nm, c = s_nm[i % 2], i % 12 // 3
                    rs = q_rs[:, 2 + 4 * m + c, 2 * t:2 * t + 2]
                    dve.wait_ge(*q_rs_ready(l, 2 + 4 * m + c))
                    top_ = dve.scalar_tensor_tensor(nm, s_max, -1.0, rs, ALU.mult, ALU.mult)
                    if m == 0:
                        top_.then_inc(max_ready.sem, 1)
                    else:
                        two = nsink[:, c:c + 5:4]
                        dve.wait_ge(*chain.made(top_))
                        s = chain.made(dve.tensor_tensor(nm, nm, two, ALU.min))
                        dve.wait_ge(*s)
                        dve.tensor_tensor(s_sd, nm, two, ALU.subtract).then_inc(max_ready.sem, 1)
                elif what == "scale":
                    nk = PAST + T_LAT if i % 3 < 2 else T_CTX
                    dve.wait_ge(*exps(l, i))
                    total = s_sum[i % 2]
                    if i >= 12:
                        dve.wait_ge(*sink_exp(l, i - 12))
                        s = chain.made(dve.tensor_tensor(total, total, s_se, ALU.add))
                        dve.wait_ge(*s)
                    s = chain.made(dve.reciprocal(s_r, total))
                    dve.wait_ge(*s)
                    for g in range(2):
                        v = prob[:, i % 2, g, 0:nk]
                        ins = dve.tensor_scalar(v, v, s_r[:, g:g + 1], None, ALU.mult)
                    ins.then_inc(probs_ready.sem, 1)
                elif what == "attn":
                    m, c, t = i // 12, i % 12 // 3, i % 3
                    part = slice(P * t, P * t + P)
                    dve.wait_ge(*attn_hi(l, i))
                    if i == 0:
                        dve.wait_ge(*kv_stored(l, 0))
                    lo_part(br_lo[:, 8 + 4 * m + c, part], tr[:, 0, 384:512], br_hi[:, 8 + 4 * m + c, part])\
                        .then_inc(attn_ready.sem, 1)
                elif what == "conv":
                    dve.wait_ge(*conv_hi(l, i))
                    lo_part(br_lo[:, i, LAT], cy[:, i % 2, 0:T_LAT], br_hi[:, i, LAT])
                    lo_part(br_lo[:, i, CTX], cy[:, i % 2, T_LAT + 1:T + 1], br_hi[:, i, CTX]).then_inc(conv_split.sem, 1)
                elif what == "pooldiff":
                    p, w = pin[:, i % 2, :], POOL_SIZES[i]
                    src = sums_of(w)
                    dve.wait_ge(*window_sums(l, i))
                    for at, m in ((16, T_LAT), (32 + T_LAT, T_CTX)):
                        ins = dve.scalar_tensor_tensor(p[:, at:at + m], src[:, at:at + m], 1.0 / w, p[:, at:at + m],
                                                       ALU.mult, ALU.subtract)
                    ins.then_inc(pool_ready.sem, 1)
                elif what == "poolsplit":
                    n = BASE["pv"] + 8 * (i // 2) + i % 2
                    dve.wait_ge(*pool_hi(l, i))
                    lo_part(br_lo[:, 4 + i, :], bank[:, (n + 1) % RING, 0:T], br_hi[:, 4 + i, :],
                            vec[:, V_PSC + i:V_PSC + i + 1]).then_inc(pool_split.sem, 1)

            def mean_square(l, which):
                dve.wait_ge(*x_stat(l, which))
                dve.tensor_scalar(x_ms, tr[:, 0, 0:TT], EPS, None, ALU.add).then_inc(x_ms_ready.sem, 1)

            def norm(l, which, start=None):
                sc_, g_ = (M_SC1, M_SC2)[which], (V_GMIX, V_GFFN)[which]
                shift, full = (M_SH1, M_SH2)[which], {}

                def gains(d, n, columns_in, k):
                    dve.wait_ge(*columns_in)
                    dve.scalar_tensor_tensor(gain[:, which, d:d + n, :], modc[:, sc_ + d:sc_ + d + n, :], 1.0,
                                             vec[:, g_ + d:g_ + d + n].unsqueeze(2).broadcast_to([P, n, 2]),
                                             ALU.add, ALU.mult).then_inc(gain_ready.sem, 1)
                    dve.wait_ge(*gain_ready(l, k))

                def normed(d):
                    if d >= 4:
                        dve.wait_ge(*h_hi_ready(l, 8 * which + d - 4))
                    dve.tensor_tensor(nx[:, d % 4, :], x[:, d, :], tr[:, 0, 0:T], ALU.mult).then_inc(x_normed.sem, 1)

                def whole(d):
                    dve.wait_ge(*x_normed(l, 8 * which + d))
                    for c, part in enumerate((LAT, CTX)):
                        ins = dve.tensor_scalar(nf[:, d % 4, part], nx[:, d % 4, part], gain[:, which, d, c:c + 1],
                                                modc[:, shift + d, c:c + 1], ALU.mult, ALU.add)
                    full[d] = chain.made(ins)

                def low(d):
                    dve.wait_ge(*full[d])
                    dve.wait_ge(*h_hi_ready(l, 8 * which + d))
                    lo_part(h_lo[:, d, :], nf[:, d % 4, :], h_hi[:, d, :]).then_inc(h_ready.sem, 1)

                if which:
                    gains(0, DC, mod_ready(l, 11), 4)
                for d in range(DC + 1):
                    if which == 0 and d % 2 == 0 and d < DC:
                        if d:
                            low(d - 1)
                            if start:
                                start(d // 2)
                        gains(d, 2, next_ready(l, d + 1 - 8), d // 2)
                    if d == 0:
                        dve.wait_ge(*x_bcast(l, which))
                    if d < DC:
                        normed(d)
                    if d and (which or d % 2 or d == DC):
                        low(d - 1)
                    if d < DC:
                        whole(d)

            def slot(l, n, it=0, per=0):
                first = UNITS[n]["kind"] in ("out", "down")
                if first:
                    before_split(l, n, it, per)
                if n + LOOKAHEAD >= U:
                    with dve.If(l < DEPTH - 1):
                        split(l + 1, n + LOOKAHEAD - U)
                else:
                    split(l, n + LOOKAHEAD, it, per)
                run_hooks(dve, l, n, it, hook, ("sel_next",))
                if not first:
                    before_split(l, n, it, per)
                after_split(l, n, it, per)

            made, ff_made = {}, {}

            dve.nop().then_inc(lo_ready.sem, 8)
            for k in range(DC):
                dve.wait_ge(*turned(0, k))
                dve.tensor_copy(x[:, k, :], bank[:, k % RING, 0:T]).then_inc(x_ready.sem, 1)
            s = chain.made(dve.memset(cond[:, :, :], 0.0))
            dve.wait_ge(*cond_tanh(0, 1))
            s = chain.made(dve.scalar_tensor_tensor(cond_t[:, 0, :], cond_t[:, 0, :], 1.0, cond_t[:, 1, :], ALU.add, ALU.mult))
            dve.wait_ge(*s)
            for c in range(2):
                dve.tensor_scalar(cond[:, :, c], cond_t[:, 0, DC * c:DC * c + DC], 0.5, None, ALU.mult)\
                    .then_inc(cond_ready.sem, 1)
            for l in range(DEPTH):
                dve.wait_ge(*turned(0, 1 + DC + 2 * l))
                dve.tensor_copy(vec_all[:, l, 0:NV], tr[:, 0, P * l:P * l + NV]).then_inc(evicted.sem, 1)
                dve.wait_ge(*turned(0, 2 + DC + 2 * l))
                dve.tensor_copy(vec_all[:, l, NV:NVX], tr[:, 0, 256 + 4 * l:256 + 4 * l + 4]).then_inc(evicted.sem, 1)
            dve.wait_ge(*evicted(0, 2 * DEPTH - 1))
            dve.wait_ge(*vectors_in(0, 9))
            def vectors(l, at):
                dve.tensor_copy(vec[:, :], vec_all[:, bass.ds(at, 1), :].rearrange("p a v -> p (a v)")).then_inc(vec_ready.sem, 1)
                dve.wait_ge(*vec_ready(l, 0))
                s = chain.made(dve.tensor_scalar(nsink[:, :], sink[:, bass.ds(at, 1), :].rearrange("p a v -> p (a v)"),
                                                 -1.0, None, ALU.mult))
                dve.wait_ge(*s)

            def start(j):
                for k in (2 * j, 2 * j + 1):
                    g = next_group(k)
                    dve.wait_ge(*next_col(0, k - 8))
                    mod_columns(slice(2 * g, 2 * g + 2), start_bank[k % 4], 2 + k % 4, vec_all[:, 0, 2 * g:2 * g + 2],
                                next_added(0, k - 8), next_ready.sem)

            vectors(0, 0)
            start(0)
            mean_square(0, 0)
            for n in range(LOOKAHEAD):
                split(0, n)
            norm(0, 0, start)

            with dve.Fori(0, DEPTH) as l:
                chain.enter("layer", l)
                for n in range(0, N_AC):
                    slot(l, n)
                with dve.Fori(0, 2) as it:
                    chain.enter("branches", it)
                    for n in range(N_AC, N_AC + 16):
                        slot(l, n, it, 16)
                    chain.leave(2)
                for d in range(DC):
                    dve.wait_ge(*merged_hi(l, d))
                    lo_part(br_lo[:, d, :], merged[:, d, :], br_hi[:, d, :], 0.5).then_inc(merged_split.sem, 1)
                for n in range(N_O, N_F):
                    slot(l, n)
                mean_square(l, 1)
                norm(l, 1)
                for n in range(N_F, N_F + 4):
                    slot(l, n)
                with dve.Fori(0, 4) as it:
                    chain.enter("ffn", it)
                    for n in range(N_F + 4, N_F + 12):
                        slot(l, n, it, 8)
                    chain.leave(4)
                for n in range(N_F + 36, U):
                    slot(l, n)
                with dve.If(l < DEPTH - 1):
                    mean_square(l + 1, 0)
                    vectors(l + 1, (l + 1) % DEPTH)
                    norm(l + 1, 0)
                chain.leave(DEPTH)

            for k in range(2 * TT):
                dve.wait_ge(*turned(0, 1 + DC + 2 * DEPTH + k))
                ins = dve.tensor_copy(tok[:, k // 2, 512 * (k % 2):512 * (k % 2) + 512], bank[:, k % RING, :])
                ins.then_inc(evicted.sem, 1)

        @block.gpsimd
        def _(pool):
            chain = Steps(pool_step, sizes, "pool")

            def add_square(l, k):
                if k % 8 in (0, 7):
                    return
                pool.wait_ge(*x_squared(l, k))
                if k % 8 == 1:
                    pool.tensor_tensor(x_acc[:, :], x_sq[:, 0, :], x_sq[:, 1, :], ALU.add).then_inc(x_summed.sem, 2)
                    return
                pool.wait_ge(*x_summed(l, k // 8 * 7 + k % 8 - 1))
                pool.tensor_tensor(x_acc[:, :], x_acc[:, :], x_sq[:, k % 2, :], ALU.add).then_inc(x_summed.sem, 1)

            def window(l, i):
                p, w = pin[:, i % 2, :], POOL_SIZES[i]
                pool.wait_ge(*pool_in(l, i))
                if i:
                    pool.wait_ge(*pool_ready(l, i - 1))
                s = chain.made(pool.tensor_tensor(ps_a[:, 1:PL], p[:, 0:PL - 1], p[:, 1:PL], ALU.add))
                src, dst, size, lo = ps_a, ps_b, 2, 1
                while size < w:
                    hf = size // 2
                    pool.wait_ge(*s)
                    a, b = lo + hf, PL - (size - 1)
                    s = chain.made(pool.tensor_tensor(dst[:, a:b], src[:, a - hf:b - hf], src[:, a + hf:b + hf], ALU.add))
                    src, dst, size, lo = dst, src, 2 * size, a
                pool.wait_ge(*s)
                edge = const[:, K_EDGE + 32 * i:K_EDGE + 32 * i + 32].rearrange("p (s e) -> p s e", e=8)
                for sq_, at, step in ((0, 16, T_LAT - 8), (1, 32 + T_LAT, T_CTX - 8)):
                    for e in range(2):
                        v = src[:, at + e * step:at + e * step + 8]
                        ins = pool.tensor_tensor(v, v, edge[:, 2 * sq_ + e, :], ALU.mult)
                ins.then_inc(window_sums.sem, 1)

            def merge(l, i, it):
                d = i % 8
                pool.wait_ge(*merge_product(l, i + it * 8))
                pool.wait_ge(*merge_begun(l, d))
                if i >= 8:
                    pool.wait_ge(*merge_done(l, i - 8 + it * 8))
                m = merged[:, d, :]
                pool.tensor_tensor(m, m, gate_t[:, d % 4, :], ALU.add).then_inc(merge_done.sem, 1)

            def rms(l, which):
                pool.wait_ge(*x_ms_ready(l, which))
                pool.tensor_tensor(x_rs, x_ms, exponent[:, 0:1].broadcast_to([P, TT]), ALU.pow).then_inc(x_rs_ready.sem, 1)

            pool.wait_ge(*chain.made(pool.memset(exponent[:, :], -0.5)))
            for k in range(DC):
                add_square(0, k - 8)
            rms(0, 0)
            with pool.Fori(0, DEPTH) as l:
                chain.enter("layer", l)
                pool.wait_ge(*next_sum(l, -1))
                for m, name in enumerate(("attn", "win")):
                    pool.dma_start(k_past[:, m, :], io["cache_k_" + name][0, l].rearrange("t h c -> t (h c)"))\
                        .then_inc(past_in.sem, 16)
                for m, name in enumerate(("attn", "win")):
                    pool.dma_start(vals[:, m, 0, :], io["cache_v_" + name][0, l].rearrange("t h c -> t (h c)"))\
                        .then_inc(vals_in.sem, 16)
                pool.dma_start(pw[:, :, :], io["pool_w"][l].rearrange("g c e -> c g e")).then_inc(pw_in.sem, 16)
                for i in range(10):
                    pool.wait_ge(*q_ms_ready(l, i))
                    pool.tensor_tensor(q_rs[:, i, :], q_ms[i % 2], exponent[:, 0:1].broadcast_to([P, 2 * TT]), ALU.pow)\
                        .then_inc(q_rs_ready.sem, 1)
                    if i == 0:
                        pool.memset(cz[:, :], 0.0).then_inc(pads_zeroed.sem, 1)
                        pool.memset(pin[:, :, :], 0.0).then_inc(pads_zeroed.sem, 1)
                for i in range(CC):
                    window(l, i)
                for i in range(8):
                    merge(l, i, 0)
                with pool.Fori(0, 2) as it:
                    for i in range(8, 16):
                        merge(l, i, it)
                for k in range(8):
                    add_square(l, k)
                rms(l, 1)
                for k in range(8, 16):
                    add_square(l, k)
                with pool.If(l < DEPTH - 1):
                    rms(l + 1, 0)
                chain.leave(DEPTH)


SHAPES_OUT = {
    "y_prompt": (1, T_CTX, D), "y_sample": (1, T_LAT, D),
    "k_attn": (1, DEPTH, T_CTX, NKV, HD), "v_attn": (1, DEPTH, T_CTX, NKV, HD),
    "k_win": (1, DEPTH, T_CTX, NKV, HD), "v_win": (1, DEPTH, T_CTX, NKV, HD),
}


def build(make, shapes, sizes):
    nc = make()
    io = {n: nc.dram_tensor(f"in_{n}", s, F32, kind="ExternalInput").ap() for n, s in shapes.items()}
    io |= {n: nc.dram_tensor(f"out_{n}", s, F32, kind="ExternalOutput").ap() for n, s in SHAPES_OUT.items()}
    program(nc, io, sizes)
    return nc


def kernel(**inputs):
    import concourse.bacc as bacc
    from concourse.bass_utils import run_bass_kernel_spmd

    arrays = {n: np.ascontiguousarray(a) for n, a in inputs.items()}
    arrays["const"] = constants()
    shapes = {n: a.shape for n, a in arrays.items()}

    def make():
        return bacc.Bacc("TRN2", target_bir_lowering=False, num_devices=1)

    sizes = {}
    build(make, shapes, sizes)
    nc = build(make, shapes, sizes)
    r = run_bass_kernel_spmd(nc, [{f"in_{n}": a for n, a in arrays.items()}], core_ids=[0])
    return tuple(r.results[0][f"out_{n}"] for n in SHAPES_OUT)
```

```python
from contextlib import ExitStack

import numpy as np

import concourse.bass as bass
import concourse.mybir as mybir

P = 128
F32 = mybir.dt.float32
F32R = mybir.dt.float32r
ALU = mybir.AluOpType
ACT = mybir.ActivationFunctionType
AXX = mybir.AxisListType.X

DEPTH = 2
D = 1024
DC = D // P
T_LAT, T_CTX = 256, 128
T = T_LAT + T_CTX
TT = T // P
PAST = 128
HD = 64
NQ, NKV = 8, 2
QW, KVW = NQ * HD, NKV * HD
GRID_W = 64
N_FREQ = HD // 4
ROPE_THETA = 10000.0
CW = 512
CC = CW // P
POOL_SIZES = (2, 4, 8, 16)
D_FF = -(-(8 * D) // (3 * 256)) * 256
FC = D_FF // P
EPS = 1e-6
NEG = -1e30
SCALE = HD ** -0.5

C_QA, C_KVA = 0, QW
C_QC, C_KVC = QW + 2 * KVW, 2 * QW + 2 * KVW
C_U = 2 * QW + 4 * KVW
C_GB, C_GC, C_PV = C_U + CW, C_U + 2 * CW, C_U + 3 * CW
C_GL = C_U + 4 * CW

LOOKAHEAD = 3
RING = 4
SLAB = 2048
LAT, CTX = slice(0, T_LAT), slice(T_LAT, T)

V_BMOD, V_GMIX, V_GFFN, V_CONV, V_PSC, V_GAIN = 0, 48, 56, 64, 76, 80
NV = 84
NVX = NV + 4
M_SH1, M_SC1, M_G1, M_SH2, M_SC2, M_G2 = range(0, 48, 8)

K_ID, K_PERM, K_HEAD, K_MEAN = 0, 128, 256, 258
NK_FIRST = 260
K_MASK, K_COS, K_SIN, K_EDGE = 260, 516, 772, 1028
NK = 1028 + 128


def constants():
    k = np.zeros((P, NK), np.float32)
    p = np.arange(P)
    k[p, K_ID + p] = 1.0
    k[p, K_PERM + (p ^ N_FREQ)] = 1.0
    a, b = np.meshgrid(p, p, indexing="ij")
    k[:, K_MASK:K_MASK + P] = np.where(b <= a, 0.0, NEG)
    k[:, K_MASK + P:K_MASK + 2 * P] = np.where(a <= b, 0.0, NEG)
    t = np.arange(T_LAT)
    pos = np.stack([t // GRID_W, t % GRID_W]).astype(np.float32)
    inv = (1.0 / (np.float32(ROPE_THETA) ** (np.arange(N_FREQ, dtype=np.float32) / N_FREQ))).astype(np.float32)
    ang = (pos[(p % HD) // 32] * inv[p % N_FREQ][:, None]).astype(np.float32)
    sign = np.where((p // N_FREQ) % 2 == 0, -1.0, 1.0)[:, None]
    k[:, K_COS:K_COS + T_LAT] = np.cos(ang)
    k[:, K_SIN:K_SIN + T_LAT] = np.sin(ang) * sign
    k[p, K_HEAD + p // HD] = 1.0 / HD
    k[:, K_MEAN] = 1.0 / D
    edge = np.ones((4, 4, 8), np.float32)
    for g, w in enumerate(POOL_SIZES):
        for s, n in enumerate((T_LAT, T_CTX)):
            for e, first in enumerate((0, n - 8)):
                i = np.arange(first, first + 8)
                cnt = np.clip(i + w - w // 2, 0, n) - np.clip(i - w // 2, 0, n)
                edge[g, 2 * s + e] = w / cnt
    k[:, K_EDGE:K_EDGE + 128] = edge.reshape(1, 128)
    return k


def plan():
    units, slab_of = [], []

    def add(kind, indices, K, slab):
        slab_of.append(slab)
        for j, i in enumerate(indices):
            units.append(dict(kind=kind[j] if isinstance(kind, tuple) else kind, i=i, K=K,
                              part=j, slab=len(slab_of) - 1, shape=slab[0]))

    for m, c0 in enumerate((C_KVA, C_KVC)):
        add(("norm", "v"), (m, m), DC, ("in", c0))
    for m, c0 in enumerate((C_QA, C_QC)):
        for s in range(2):
            add("norm", (2 + 4 * m + 2 * s, 3 + 4 * m + 2 * s), DC, ("pair", c0 + P * s))
    for s in range(2):
        for kind, c0 in (("u", C_U), ("gb", C_GB), ("gc", C_GC), ("pv", C_PV)):
            add(kind, (2 * s, 2 * s + 1), DC, ("in", c0 + 2 * P * s))
    for b, branch in enumerate((1, 3, 0, 2)):
        for half in range(2):
            for s in (2 * half, 2 * half + 1):
                add("gate", (8 * b + 2 * s, 8 * b + 2 * s + 1), DC, ("in", C_GL + branch * D + 2 * P * s))
            for d in (4 * half, 4 * half + 2):
                add("proj", (8 * b + d, 8 * b + d + 1), 4, ("heads" if b > 1 else "branch", branch, P * d))
    for s in range(4):
        add("out", (2 * s, 2 * s + 1), DC, ("out", s))
    for s in range(FC // 2):
        add("a", (2 * s, 2 * s + 1), DC, ("gu", 2 * P * s))
        add("b", (2 * s, 2 * s + 1), DC, ("gu", D_FF + 2 * P * s))
    for s in range(4):
        k0 = 0
        assert FC == 22
        for q, K in enumerate((6, 6, 5, 5)):
            add("down", (2 * s, 2 * s + 1), K, ("down", s, k0, K))
            for u in units[-2:]:
                u.update(k0=k0, first=q == 0, last=q == 3)
            k0 += K
    base = {}
    for n, u in enumerate(units):
        base.setdefault(u["kind"], n)
    U = len(units)

    hooks = [[] for _ in range(U)]
    for n, u in enumerate(units[:12]):
        if u["kind"] == "norm":
            at = (3, None, 4)[n] if n < 3 else n + 1
            if u["i"] < 2:
                hooks[at + 2].append(("rnorm", u["i"]))
            hooks[at].append(("stat", u["i"]))
        else:
            hooks[(3, 4)[u["i"]]].append(("vt", u["i"]))
    for i, at in reversed(list(enumerate((6, 7, 7, 7, 8, 9, 10, 11, 12, 13)))):
        hooks[at].insert(0, ("split", i))
    hooks[7].insert(0, ("kout", 0))
    hooks[8].insert(0, ("kout", 1))
    hooks[9].insert(0, ("cache", 0))
    hooks[10].insert(0, ("cache", 1))
    P0, G0 = base["u"], base["gate"]
    for n in range(P0, G0):
        if units[n]["kind"] == "gc":
            hooks[n + 1].append(("conv", units[n]["i"]))
        if units[n]["kind"] == "pv":
            hooks[n + 2].append(("pooldiff", units[n]["i"]))
            hooks[n + 3].append(("pool", units[n]["i"]))
            hooks[n + 3].append(("poolsplit", units[n]["i"]))
    steps = []
    for k in range(51):
        now, j = [], k // 2
        if k % 2 == 0:
            now += [("attn", j - 2)] if j >= 2 else []
            now += [("scores", j)] if j < 24 else []
        else:
            now += [("scale", j)] if j < 24 else []
            now += [("probsT", j - 1)] if j >= 1 else []
        steps.append(now)
    n_attn = range(P0, base["gate"] + 32)
    weight = sum(units[n]["K"] for n in n_attn)
    done = k = 0
    mid = [[] for _ in range(U)]
    for n in n_attn:
        for where in (mid, hooks):
            done += units[n]["K"] / 2
            while k < len(steps) and (k + 0.5) * weight / len(steps) <= done:
                where[n].extend(steps[k])
                k += 1
    assert k == len(steps)
    AC = G0 + 32
    for x, at in enumerate((2, 4, 6, 8, 10, 12)):
        hooks[AC + at - 2].insert(0, ("load", x))
        hooks[AC + at].append(("mod", x))
        hooks[AC + at + 1].insert(0, ("sel", x))
    hooks[base["out"]] += [("load", x) for x in range(12, 16)]
    for at, k in ((base["a"] + 4, 0), (base["a"] + 36, 4)):
        hooks[at].append(("load_next", k))
        hooks[at + 3].append(("mod_next", k))
        hooks[at + 4].append(("sel_next", k))
    hooks[base["down"] + 1] += [("load_next", k) for k in (5, 6, 7)]
    last_unit = {}
    for n, u in enumerate(units):
        last_unit[u["slab"]] = n
    return units, slab_of, hooks, mid, base, last_unit


UNITS, SLABS, HOOKS, MID, BASE, LAST_UNIT = plan()
U, S = len(UNITS), len(SLABS)
N_Q, N_P, N_G = 0, BASE["u"], BASE["gate"]
N_AC, N_O = N_G + 32, BASE["out"]
N_F, N_D = BASE["a"], BASE["down"]
assert U % RING == 0 and S % RING == 0


class Signal:

    def __init__(self, sem, per_layer, before=0, step=1):
        self.sem, self.per_layer, self.before, self.step = sem, per_layer, before, step

    def __call__(self, l, k):
        return self.sem, (l * self.per_layer + (k + self.before + 1)) * self.step


class Steps:

    def __init__(self, sem, sizes, name):
        self.sem, self.sizes, self.name = sem, sizes, name
        self.offset, self.n, self.marks = 0, 0, []

    def made(self, instruction):
        instruction.then_inc(self.sem, 1)
        self.n += 1
        return self.sem, self.offset + self.n

    def enter(self, what, i):
        self.marks.append((what, self.n, self.offset))
        self.offset = self.offset + i * self.sizes.get((self.name, what), 1)

    def leave(self, times):
        what, n, offset = self.marks.pop()
        size = self.n - n
        self.sizes[(self.name, what)] = size
        self.offset, self.n = offset, n + size * times


def program(nc, io, sizes):
    with ExitStack() as ctx:
        base = (nc.sbuf_base + 63) // 64 * 64
        top = base

        def place(name, shape, dt=F32, at=None):
            nonlocal top
            size = 4 * int(np.prod(shape[1:]))
            size = (size + 31) // 32 * 32
            if at is None:
                at, top = top, top + size
            place.end = at + size
            return nc.alloc_sbuf_tensor_at(name, shape, dt, offset=at)

        raw = place("raw", [P, RING, SLAB])
        w_hi = place("w_hi", [P, RING, DC * P], F32R)
        w_lo = place("w_lo", [P, RING, DC * P], F32R)
        x = place("x", [P, DC, T])
        h_hi = place("h_hi", [P, DC, T], F32R)
        h_lo = place("h_lo", [P, DC, T], F32R)
        G = top
        f_hi = place("f_hi", [P, FC, T], F32R)
        f_lo = place("f_lo", [P, FC, T], F32R)
        br_hi = place("br_hi", [P, 16, T], F32R, at=G)
        br_lo = place("br_lo", [P, 16, T], F32R, at=G + 16 * T * 4)
        late_w0 = place("late_w0", [P, SLAB], at=G + 8 * T * 4)
        late_w1 = place("late_w1", [P, SLAB], at=G + 24 * T * 4)
        Z = G + 2 * 16 * T * 4
        merged = place("merged", [P, DC, T], at=Z)
        gate_t = place("gate_t", [P, 4, T], at=Z + DC * T * 4)
        assert place.end <= top
        Q1 = G + 8 * T * 4
        q_sq = place("q_sq", [P, 2, T], at=Q1)
        q_raw = place("q_raw", [P, 3, T], at=place.end)
        k_lo0 = place("k_lo0", [P, PAST + T], F32R, at=place.end)
        assert place.end - (PAST + T) * 4 >= Q1 + 4 * T * 4
        pw = place("pw", [P, CC, P], at=place.end)
        assert place.end <= Q1 + 8 * T * 4
        ZL = 1 + T_LAT + 1 + T_CTX + 1
        PL = 16 + T_LAT + 16 + T_CTX + 16
        pin = place("pin", [P, 2, PL], at=Z)
        ps_a = place("ps_a", [P, PL], at=place.end)
        ps_b = place("ps_b", [P, PL], at=place.end)
        cz = place("cz", [P, ZL], at=place.end)
        cy = place("cy", [P, 2, ZL - 1], at=place.end)
        cu = place("cu", [P, 2, T], at=place.end)
        cgb = place("cgb", [P, 2, T], at=place.end)
        assert place.end <= top, (place.end, top)
        nx = place("nx", [P, 4, T], at=Z)
        nf = place("nf", [P, 4, T], at=place.end)
        tok = place("tok", [P, TT, D], at=G)
        vec_raw = place("vec_raw", [NV, DEPTH, P], at=G + TT * D * 4)
        c_raw = place("c_raw", [2 * DC, P], at=place.end)
        start_w = place("start_w", [P, 4, SLAB], at=place.end)
        assert place.end <= Z
        q_at = top
        q_hi = place("q_hi", [P, 8, T], F32R)
        q_lo = br_lo[:, 8:16, :]
        x_sq = place("x_sq", [P, 2, T], at=q_at)
        x_acc = place("x_acc", [P, T], at=place.end)
        k_hi = place("k_hi", [P, 2, PAST + T], F32R)
        vals = place("vals", [P, 2, 1 + TT, KVW])
        A0 = top
        prob = place("prob", [P, 2, 2, PAST + T_LAT])
        prob_t = place("prob_t", [P, 2, 2, 3, P])
        v_t = place("v_t", [P, 2, T], at=A0)
        q_mix = place("q_mix", [P, 4, T], at=place.end)
        k_past = place("k_past", [P, 2, KVW], at=place.end)
        q_rot = place("q_rot", [P, T_LAT], at=place.end)
        k_out = place("k_out", [P, 2, KVW], at=place.end)
        assert place.end <= top
        mod_w = place("mod_w", [P, 2, SLAB], at=q_at + 3 * T * 4)
        next_row = place("next_row", [P, 2, 2 * P], at=place.end)
        ff_at = place.end
        tail_w = place("tail_w", [P, SLAB], at=ff_at)
        assert place.end <= top
        ff_t = place("ff_t", [P, 2, T], at=ff_at)
        ff_s = place("ff_s", [P, 2, T], at=place.end)
        ff_f = place("ff_f", [P, 2, T], at=place.end)
        assert place.end <= top
        const = place("const", [P, NK])
        cond = place("cond", [P, DC, 32])
        cond_t = place("cond_t", [P, 2, 2 * DC], at=A0 + 4096)
        vec_all = place("vec_all", [P, DEPTH, NVX])
        vec = place("vec", [P, NVX])
        modc = place("modc", [P, 48, 2])
        gain = place("gain", [P, 2, DC, 2])
        mod_row = place("mod_row", [P, 2, 2 * P])
        k_lo = [k_lo0, place("k_lo1", [P, PAST + T], F32R, at=top - 2 * 2 * P * 4)]
        assert place.end <= top
        sink = place("sink", [P, DEPTH, NQ])
        nsink = place("nsink", [P, NQ])
        st = place("st", [P, 64])
        exponent = place("exponent", [P, 1])
        mod_t = place("mod_t", [P, 6, 2, 2])
        q_rs = place("q_rs", [P, 10, 2 * TT])
        assert top <= nc.sbuf_usable_end, (top, nc.sbuf_usable_end)
        x_ms, x_rs = st[:, 0:3], st[:, 4:7]
        q_ms = [st[:, 8 + 8 * i:14 + 8 * i] for i in range(2)]
        s_max, s_nm = st[:, 40:42], [st[:, 42 + 2 * i:44 + 2 * i] for i in range(2)]
        s_sum = [st[:, 46 + 2 * i:48 + 2 * i] for i in range(2)]
        s_sd, s_se, s_r = st[:, 50:52], st[:, 52:54], st[:, 54:56]
        ident = const[:, K_ID:K_ID + P]

        def psum(name, shape):
            return ctx.enter_context(nc.psum_tensor(name, shape, F32))

        bank = psum("bank", [P, RING, 512])
        sc = psum("sc", [P, 2, 512])
        tr = psum("tr", [P, 2, 512])

        def signal(name, per_layer, before=0, step=1):
            return Signal(ctx.enter_context(nc.semaphore(name)), per_layer, before, step)

        slab_in = [signal(f"slab_in{s}", S // RING, step=32) for s in range(RING)]
        start_in = [signal(f"start_in{s}", 0, step=32) for s in range(6)]
        mod_in = [signal(f"mod_in{s}", 6, step=32) for s in range(2)]
        late_in = [signal(f"late_in{s}", 1, step=32) for s in range(4)]
        next_in = signal("next_in", 5, step=32)
        tail_in = [signal(f"tail_in{s}", 1, step=32) for s in range(3)]
        unit_done = signal("unit_done", U, before=RING)
        x_stat = signal("x_stat", 2)
        x_bcast = signal("x_bcast", 2)
        q_stat = signal("q_stat", 10)
        q_bcast = signal("q_bcast", 2)
        v_turned = signal("v_turned", 2)
        k_turned = signal("k_turned", 2)
        past_turned = signal("past_turned", 2)
        scores = signal("scores", 24)
        probs_turned = signal("probs_turned", 24)
        attn_out = signal("attn_out", 24)
        mod_sum = signal("mod_sum", 16)
        mod_col = signal("mod_col", 16)
        next_sum = signal("next_sum", 8, before=8)
        next_col = signal("next_col", 8, before=8)
        pooled = signal("pooled", 4)
        turned = signal("turned", 0)
        hi_ready = signal("hi_ready", U)
        h_hi_ready = signal("h_hi_ready", 16)
        q_copied = signal("q_copied", 10)
        v_copied = signal("v_copied", 2)
        k_out_ready = signal("k_out_ready", 2)
        past_hi = signal("past_hi", 2)
        qk_hi = signal("qk_hi", 10)
        exps = signal("exps", 24)
        sink_exp = signal("sink_exp", 12)
        probs_t_ready = signal("probs_t_ready", 24)
        attn_hi = signal("attn_hi", 24)
        mod_row_ready = signal("mod_row_ready", 16)
        next_row_ready = signal("next_row_ready", 8, before=8)
        conv_in = signal("conv_in", 8)
        pool_in = signal("pool_in", 4)
        conv_hi = signal("conv_hi", 4)
        pool_hi = signal("pool_hi", 4)
        gate_ready = signal("gate_ready", 32)
        merged_hi = signal("merged_hi", 8)
        x_squared = signal("x_squared", 16, before=8)
        ff_tanh = signal("ff_tanh", FC)
        ff_hi = signal("ff_hi", FC)
        cond_tanh = signal("cond_tanh", 0)
        lo_ready = signal("lo_ready", U, before=8)
        vec_ready = signal("vec_ready", 1)
        x_ms_ready = signal("x_ms_ready", 2)
        x_normed = signal("x_normed", 16)
        h_ready = signal("h_ready", 16)
        q_ms_ready = signal("q_ms_ready", 10)
        q_mixed = signal("q_mixed", 10)
        k_ready = signal("k_ready", 2)
        past_split = signal("past_split", 2)
        qk_split = signal("qk_split", 10)
        v_ready = signal("v_ready", 2)
        max_ready = signal("max_ready", 24)
        probs_ready = signal("probs_ready", 24)
        attn_ready = signal("attn_ready", 24)
        mod_ready = signal("mod_ready", 16)
        next_ready = signal("next_ready", 8, before=8)
        mod_added = signal("mod_added", 16)
        next_added = signal("next_added", 8, before=8)
        gain_ready = signal("gain_ready", 5)
        conv_ready = signal("conv_ready", 4)
        conv_split = signal("conv_split", 4)
        pool_ready = signal("pool_ready", 4)
        pool_split = signal("pool_split", 4)
        merge_begun = signal("merge_begun", 8)
        merge_product = signal("merge_product", 24)
        merged_split = signal("merged_split", 8)
        x_ready = signal("x_ready", 16, before=8)
        ff_prod = signal("ff_prod", FC)
        ff_split = signal("ff_split", FC)
        evicted = signal("evicted", 0)
        result_out = [signal(f"result_out{s}", 0) for s in range(2)]
        cond_ready = signal("cond_ready", 0)
        dve_step = ctx.enter_context(nc.semaphore("dve_step"))
        x_rs_ready = signal("x_rs_ready", 2)
        q_rs_ready = signal("q_rs_ready", 10)
        x_summed = signal("x_summed", 14, before=7)
        pads_zeroed = signal("pads_zeroed", 2)
        merge_done = signal("merge_done", 24)
        window_sums = signal("window_sums", 4)
        pool_step = ctx.enter_context(nc.semaphore("pool_step"))
        loaded = signal("loaded", 0, step=16)
        loaded_all = signal("loaded_all", 0, step=16)
        vectors_in = signal("vectors_in", 0, step=16)
        tok_in = signal("tok_in", 0, step=16)
        past_in = signal("past_in", 1, step=16 * 2)
        vals_in = signal("vals_in", 1, step=16 * 2)
        pw_in = signal("pw_in", 1, step=16)
        kv_stored = signal("kv_stored", 1, step=16 * 4)
        y_stored = signal("y_stored", 0, step=16)

        block = ctx.enter_context(nc.Block())

        def load_vector(engine, k):
            rows = [
                (V_BMOD, 48, io["b_mod"]), (V_GMIX, 8, io["g_mix"]), (V_GFFN, 8, io["g_ffn"]),
                (V_CONV, 12, io["conv_w"]), (V_PSC, 4, io["pool_scale"]),
            ]
            if k < 5:
                r, n, src = rows[k]
                src = src.rearrange("l a (k p) -> (a k) l p", p=P) if k == 3 else src.rearrange("l (k p) -> k l p", p=P)
                engine.dma_start(vec_raw[r:r + n, :, :], src).then_inc(vectors_in.sem, 16)
            elif k < 9:
                g = k - 5
                src = io[("gq_attn", "gk_attn", "gq_win", "gk_win")[g]].unsqueeze(1).unsqueeze(0)
                engine.dma_start(vec_raw[V_GAIN + g:V_GAIN + g + 1, :, :].rearrange("a l (r c) -> a l r c", r=2),
                                 src.broadcast_to([1, DEPTH, 2, HD])).then_inc(vectors_in.sem, 16)
            else:
                src = io["sink_win"].rearrange("l h -> (l h)").unsqueeze(0)
                engine.dma_start(sink[:, :, :].rearrange("p l h -> p (l h)"), src.broadcast_to([P, DEPTH * NQ]))\
                    .then_inc(vectors_in.sem, 16)

        next_bank = [sc[:, 1, :], sc[:, 0, :], sc[:, 1, :], tr[:, 1, :]]
        next_w = [mod_w[:, 1, :], mod_w[:, 0, :], mod_w[:, 1, :], tail_w[:, :]]
        row_of = [next_row[:, 0, :], next_row[:, 0, :], next_row[:, 1, :], mod_row[:, 0, :]]
        start_bank = [bank[:, 3, :], tr[:, 1, :], sc[:, 0, :], sc[:, 1, :]]

        def start_group(k):
            return k // 2 + 4 * (k % 2)

        def start_slot(k):
            return start_w[:, k % 6, :] if k % 6 < 4 else mod_w[:, k % 6 - 4, :]

        def qk_of(i):
            if i < 2:
                return (k_hi[:, i, PAST:PAST + T], k_lo[i][:, PAST:PAST + T]), q_mix[:, i, :]
            return (q_hi[:, i - 2, :], q_lo[:, i - 2, :]), q_mix[:, 2 + i % 2, :]

        def sums_of(w):
            return (ps_a, ps_b)[(w.bit_length() - 2) % 2]

        def mod_index(i, it):
            return i + it * 6

        late_bank = [sc[:, 0, :], sc[:, 1, :], tr[:, 1, :], bank[:, (N_F + 3) % RING, :]]
        late_w = [mod_w[:, 0, :], mod_w[:, 1, :], late_w0[:, :], late_w1[:, :]]
        late_row = [mod_row[:, 0, :], mod_row[:, 1, :], next_row[:, 0, :], next_row[:, 1, :]]

        def run_hooks(engine, l, n, it, hook, takes, mid):
            hooks = mid + HOOKS[n]
            for what, i in hooks:
                if not what.endswith("_next"):
                    hook(l, what, i, it)
            following = [h for h in hooks if h[0] in takes]
            if following:
                with engine.If(l < DEPTH - 1):
                    for what, i in following:
                        hook(l, what, i, it)

        def load_mod(engine, w, l, columns, done):
            src = io["w_mod"][l].rearrange("(k p) c -> p k c", p=P)
            to = w.rearrange("p (k c) -> p k c", k=DC)
            for k in (slice(4, 8), slice(0, 4)):
                engine.dma_start(to[:, k, :], src[:, k, columns]).then_inc(done, 16)

        def weights_of(n, to):
            u = UNITS[n]
            K, j, slot = u["K"], u["part"], u["slab"] % RING
            if u["shape"] == "pair":
                dst = to[:, n % RING, :].rearrange("p (k g c) -> p k g c", k=DC, g=2)
                return dst, raw[:, slot, :].rearrange("p (k g i c) -> p k g i c", k=DC, g=2, i=2)[:, :, :, j, :]
            dst = to[:, n % RING, 0:K * P].rearrange("p (k c) -> p k c", k=K)
            return dst, raw[:, slot, 0:K * 2 * P].rearrange("p (k c) -> p k c", k=K)[:, :, P * j:P * j + P]

        @block.sync
        def _(sp):
            def slab(l, s, it=0, per=0):
                slot = s % RING
                layer = l % DEPTH if s < 2 and not isinstance(l, int) else l
                before, wrap = (s - RING) % S, U if s < RING else 0
                sp.wait_ge(*lo_ready(l, LAST_UNIT[before] - wrap + it * (2 * per)))
                dst, done = raw[:, slot, :], slab_in[slot].sem

                def load(to, rows):
                    sp.dma_start(to, rows).then_inc(done, 16)

                def rows_of(w, c0, stride=0, K=DC, k0=0):
                    c = bass.ds(c0 + it * stride, 256) if per else slice(c0, c0 + 256)
                    to = dst[:, 0:K * 256].rearrange("p (k c) -> p k c", k=K)
                    rows = w.rearrange("(k p) c -> p k c", p=P)
                    load(to[:, 0:K // 2, :], rows[:, k0:k0 + K // 2, c])
                    load(to[:, K // 2:K, :], rows[:, k0 + K // 2:k0 + K, c])

                what = SLABS[s]
                if what[0] == "in":
                    rows_of(io["w_in"][layer], what[1], 2 * D)
                elif what[0] == "pair":
                    w = io["w_in"][layer].rearrange("(k p) c -> p k c", p=P)
                    to = dst.rearrange("p (k g c) -> p k g c", k=DC, g=2)
                    for g in (1, 0):
                        load(to[:, :, g, :], w[:, :, what[1] + 256 * g:what[1] + 256 * g + P])
                elif what[0] == "branch":
                    rows_of(io["w_branch"][l, what[1]], what[2], K=4)
                elif what[0] == "heads":
                    to = dst[:, 0:4 * 256].rearrange("p (k c) -> p k c", k=4)
                    w = io["w_branch"][l, 2 * it].rearrange("(g i p) c -> g p i c", g=2, i=4)
                    for g in range(2):
                        load(to[64 * g:64 * g + 64, :, :], w[g, :, :, what[2]:what[2] + 256])
                elif what[0] == "out":
                    rows_of(io["w_out"][l], 256 * what[1])
                elif what[0] == "gu":
                    rows_of(io["w_gate_up"][l], what[1], 512)
                else:
                    _, s4, k0, K = what
                    rows_of(io["w_down"][l], 256 * s4, K=K, k0=k0)

            sp.dma_start(const[:, 0:NK_FIRST], io["const"][:, 0:NK_FIRST]).then_inc(loaded.sem, 16)
            sp.dma_start(c_raw[0:DC, :], io["c"].rearrange("a (k p) -> (a k) p", p=P)).then_inc(loaded.sem, 16)
            sp.dma_start(c_raw[DC:2 * DC, :], io["c_ctx"].rearrange("(k p) -> k p", p=P)).then_inc(loaded.sem, 16)
            for k in range(10):
                load_vector(sp, k)
            for k in range(8):
                if k == 2:
                    slab(0, 0)
                    slab(0, 1)
                if k >= 6:
                    sp.wait_ge(*next_sum(0, k - 6 - 8))
                g = start_group(k)
                load_mod(sp, start_slot(k), 0, slice(256 * g, 256 * g + 256), start_in[k % 6].sem)
            sp.dma_start(const[:, NK_FIRST:], io["const"][:, NK_FIRST:]).then_inc(loaded_all.sem, 16)
            a0, a1 = UNITS[N_AC]["slab"], UNITS[N_O]["slab"]
            f1, d0 = UNITS[N_F + 4]["slab"], UNITS[N_D]["slab"]
            assert (a1 - a0) == 16 and (d0 - f1) == 20
            stores = UNITS[N_P + 8]["slab"]
            with sp.Fori(0, DEPTH) as l:
                for s in range(2, a0):
                    if s == stores:
                        for m, name in enumerate(("attn", "win")):
                            sp.wait_ge(*k_out_ready(l, m))
                            sp.dma_start(io["k_" + name][0, l].rearrange("t h c -> t (h c)"), k_out[:, m, :])\
                                .then_inc(kv_stored.sem, 16)
                            sp.wait_ge(*v_ready(l, m))
                            sp.dma_start(io["v_" + name][0, l].rearrange("t h c -> t (h c)"), vals[:, m, TT, :])\
                                .then_inc(kv_stored.sem, 16)
                    slab(l, s)
                with sp.Fori(0, 2) as it:
                    for s in range(a0, a0 + 8):
                        slab(l, s, it, 8)
                for s in range(a1, f1):
                    slab(l, s)
                with sp.Fori(0, 5) as it:
                    for s in range(f1, f1 + 4):
                        slab(l, s, it, 4)
                for s in range(d0, S):
                    slab(l, s)
                with sp.If(l < DEPTH - 1):
                    slab(l + 1, 0)
                    slab(l + 1, 1)
            for k in range(2 * TT):
                t, half = k // 2, slice(D // 2 * (k % 2), D // 2 * (k % 2) + D // 2)
                sp.wait_ge(*result_out[k % 2](0, t))
                to = io["y_sample"][0, P * t:P * t + P, half] if t < 2 else io["y_prompt"][0, :, half]
                sp.dma_start(to, tok[:, t, half]).then_inc(y_stored.sem, 16)
            sp.wait_ge(*kv_stored(DEPTH - 1, 0))
            sp.wait_ge(*y_stored(0, 2 * TT - 1))

        @block.tensor
        def _(pe):
            def parts(n, k):
                K = UNITS[n]["K"]
                a = slice(k * P, k * P + P)
                return w_hi[:, n % RING, a], w_lo[:, n % RING, a]

            def product(out, w, r, start, stop):
                pe.matmul(out, w[1], r[0], start=start, stop=False)
                pe.matmul(out, w[0], r[1], start=False, stop=False)
                return pe.matmul(out, w[0], r[0], start=False, stop=stop)

            def right_operand(n, k, it):
                u = UNITS[n]
                kind = u["kind"]
                if kind == "proj":
                    if n >= N_AC:
                        c = bass.ds(8 + k + it * 4, 1)
                        return [v[:, c, :].rearrange("p a t -> p (a t)") for v in (br_hi, br_lo)]
                    c = (n - N_G) // 16 * 4 + k
                    return br_hi[:, c, :], br_lo[:, c, :]
                if kind == "out":
                    return br_hi[:, k, :], br_lo[:, k, :]
                if kind == "down":
                    return f_hi[:, u["k0"] + k, :], f_lo[:, u["k0"] + k, :]
                return h_hi[:, k, :], h_lo[:, k, :]

            def out_bank(n):
                u = UNITS[n]
                b = (u["i"] % 4) if u["kind"] == "down" else n % RING
                return bank[:, b, 0:T]

            def unit(l, n, it=0, per=0):
                u = UNITS[n]
                pe.wait_ge(*lo_ready(l, n + it * per))
                first, last = u.get("first", True), u.get("last", True)
                for k in range(u["K"]):
                    if k == u["K"] // 2:
                        for what, i in MID[n]:
                            hook(l, what, i, it)
                    ins = product(out_bank(n), parts(n, k), right_operand(n, k, it),
                                  first and k == 0, last and k == u["K"] - 1)
                ins.then_inc(unit_done.sem, 1)

            def three_units(l, n, chunk_ready, chunks=range(DC)):
                if chunks[0] == 0:
                    for m in range(n, n + 3):
                        pe.wait_ge(*lo_ready(l, m))
                for k in chunks:
                    pe.wait_ge(*chunk_ready(k))
                    for m in range(n, n + 3):
                        ins = product(out_bank(m), parts(m, k), right_operand(m, k, 0), k == 0, k == DC - 1)
                        if k == DC - 1:
                            ins.then_inc(unit_done.sem, 1)

            def statistics(l, which):
                pe.wait_ge(*x_summed(l, 7 * which - 1))
                pe.wait_ge(*x_squared(l, 8 * which - 1))
                for t in range(TT):
                    part = slice(P * t, P * t + P)
                    pe.matmul(tr[:, 0, t:t + 1], x_acc[:, part], const[:, K_MEAN:K_MEAN + 1], start=True, stop=False)
                    ins = pe.matmul(tr[:, 0, t:t + 1], x_sq[:, 1, part], const[:, K_MEAN:K_MEAN + 1], start=False, stop=True)
                ins.then_inc(x_stat.sem, 1)

            def broadcast(l, which):
                pe.wait_ge(*x_rs_ready(l, which))
                for t in range(TT):
                    ins = pe.transpose(tr[:, 0, P * t:P * t + P], x_rs[:, t:t + 1].broadcast_to([P, P]), ident)
                ins.then_inc(x_bcast.sem, 1)

            def mod_matmul(out, w, done):
                w = w.rearrange("p (k c) -> p k c", k=DC)
                for k in range(DC):
                    j = k % 4
                    ins = pe.matmul(out[32 * j:32 * j + 32, 0:2 * P], cond[:, k, :], w[:, k, :], start=k < 4, stop=k >= 4)
                ins.then_inc(done, 1)

            def mod_turn(out, row, done):
                for y in range(2):
                    ins = pe.transpose(out[:, P * y:P * y + P], row[:, P * y:P * y + P], ident)
                ins.then_inc(done, 1)

            reader = {}

            def claim(b):
                if reader.get(b):
                    pe.wait_ge(*reader[b])

            def hook(l, what, i, it):
                if what == "mod":
                    f, slot = mod_index(i, it), i % 2
                    pe.wait_ge(*mod_in[slot](l, i // 2 + it * 3))
                    if i >= 2:
                        pe.wait_ge(*mod_ready(l, f - 2))
                    mod_matmul(sc[:, slot, :], mod_w[:, slot, :], mod_sum.sem)
                elif what == "sel":
                    pe.wait_ge(*mod_row_ready(l, mod_index(i, it)))
                    mod_turn(sc[:, i % 2, :], mod_row[:, i % 2, :], mod_col.sem)
                elif what == "mod_next":
                    pe.wait_ge(*next_in(l, i + it))
                    pe.wait_ge(*next_ready(l, i + it - 1))
                    mod_matmul(next_bank[0], next_w[0], next_sum.sem)
                elif what == "sel_next":
                    pe.wait_ge(*next_row_ready(l, i + it))
                    mod_turn(next_bank[0], row_of[0], next_col.sem)
                elif what == "stat":
                    pe.wait_ge(*q_copied(l, i))
                    claim(1)
                    pe.matmul(tr[:, 1, 0:T_LAT], const[:, K_PERM:K_PERM + P], q_raw[:, i % 3, LAT], start=True, stop=True)
                    for t in range(TT):
                        ins = pe.matmul(tr[:, 1, T_LAT + 2 * t:T_LAT + 2 * t + 2], q_sq[:, i % 2, P * t:P * t + P],
                                        const[:, K_HEAD:K_HEAD + 2], start=True, stop=True)
                    ins.then_inc(q_stat.sem, 1)
                    reader[1] = q_mixed(l, i)
                elif what == "rnorm":
                    pe.wait_ge(*q_rs_ready(l, i))
                    claim(0)
                    for t in range(TT):
                        for g in range(2):
                            c = 2 * t + g
                            ins = pe.matmul(tr[64 * g:64 * g + 64, 0, P * t:P * t + P],
                                            q_rs[:, i, c:c + 1].broadcast_to([P, 64]), ident, start=True, stop=True)
                    ins.then_inc(q_bcast.sem, 1)
                    reader[0] = k_ready(l, i)
                elif what == "vt":
                    pe.wait_ge(*v_copied(l, i))
                    claim(0)
                    for t in range(TT):
                        ins = pe.transpose(tr[:, 0, P * t:P * t + P], v_t[:, i, P * t:P * t + P], ident)
                    ins.then_inc(v_turned.sem, 1)
                    reader[0] = v_ready(l, i)
                elif what == "kout":
                    pe.wait_ge(*k_ready(l, i))
                    claim(0)
                    pe.transpose(tr[:, 0, 0:P], q_mix[:, i, CTX], ident).then_inc(k_turned.sem, 1)
                    reader[0] = k_out_ready(l, i)
                elif what == "cache":
                    pe.wait_ge(*past_in(l, 0))
                    claim(0)
                    pe.transpose(tr[:, 0, 0:P], k_past[:, i, :], ident).then_inc(past_turned.sem, 1)
                    reader[0] = past_split(l, i)
                elif what == "scores":
                    m, c, t = i // 12, i % 12 // 3, i % 3
                    pe.wait_ge(*qk_split(l, 2 + 4 * m + c))
                    pe.wait_ge(*past_split(l, m))
                    if i:
                        pe.wait_ge(*exps(l, i - 1))
                    ks = slice(0, PAST + T_LAT) if t < 2 else slice(PAST + T_LAT, PAST + T)
                    for r, (q_, k_) in enumerate(((q_lo, k_hi[:, m, :]), (q_hi, k_lo[m]), (q_hi, k_hi[:, m, :]))):
                        for g in range(2):
                            a = slice(64 * g, 64 * g + 64)
                            ins = pe.matmul(sc[:, g, 0:ks.stop - ks.start], q_[a, 4 * m + c, P * t:P * t + P], k_[a, ks],
                                            start=r == 0, stop=r == 2)
                    ins.then_inc(scores.sem, 1)
                elif what == "probsT":
                    pe.wait_ge(*probs_ready(l, i))
                    claim(0)
                    claim(1)
                    for g in range(2):
                        for b in range(3 if i % 3 < 2 else 1):
                            ins = pe.transpose(tr[:, g, P * b:P * b + P], prob[:, i % 2, g, P * b:P * b + P], ident)
                    ins.then_inc(probs_turned.sem, 1)
                    reader[0] = reader[1] = probs_t_ready(l, i)
                elif what == "attn":
                    m, t = i // 12, i % 3
                    pe.wait_ge(*probs_t_ready(l, i))
                    pe.wait_ge(*v_ready(l, m))
                    pe.wait_ge(*vals_in(l, 0))
                    claim(0)
                    reader[0] = attn_ready(l, i)
                    tiles = (0, 1, 2) if t < 2 else (3,)
                    for b, v in enumerate(tiles):
                        for g in range(2):
                            ins = pe.matmul(tr[64 * g:64 * g + 64, 0, 384:512], vals[:, m, v, 64 * g:64 * g + 64],
                                            prob_t[:, i % 2, g, b, :], start=b == 0, stop=v == tiles[-1])
                    ins.then_inc(attn_out.sem, 1)
                elif what == "pool":
                    pe.wait_ge(*pool_ready(l, i))
                    pe.wait_ge(*pw_in(l, 0))
                    n = BASE["pv"] + 8 * (i // 2) + i % 2 + 1
                    pe.wait_ge(*lo_ready(l, n + 4))
                    for to, at in ((LAT, 16), (CTX, 32 + T_LAT)):
                        ins = pe.matmul(bank[:, n % RING, to], pw[:, i, :], pin[:, i % 2, at:at + to.stop - to.start],
                                        start=True, stop=True)
                    ins.then_inc(pooled.sem, 1)

            def after(l, n, it=0):
                run_hooks(pe, l, n, it, hook, ("mod_next", "sel_next"), [])

            pe.nop().then_inc(unit_done.sem, RING)
            pe.wait_ge(*loaded(0, 2))
            pe.wait_ge(*tok_in(0, TT - 1))
            for k in range(DC):
                if k >= RING:
                    pe.wait_ge(*x_ready(0, k - RING - 8))
                for t in range(TT):
                    ins = pe.transpose(bank[:, k % RING, P * t:P * t + P], tok[:, t, P * k:P * k + P], ident)
                ins.then_inc(turned.sem, 1)
            pe.transpose(tr[:, 1, 0:2 * DC], c_raw[:, :], const[0:2 * DC, K_ID:K_ID + 2 * DC]).then_inc(turned.sem, 1)
            pe.wait_ge(*vectors_in(0, 9))
            for l in range(DEPTH):
                if l:
                    pe.wait_ge(*evicted(0, 2 * l - 1))
                pe.transpose(tr[:, 0, P * l:P * l + NV], vec_raw[:, l, :], const[0:NV, K_ID:K_ID + NV])\
                    .then_inc(turned.sem, 1)
                pe.wait_ge(*evicted(0, 2 * l))
                pe.matmul(tr[:, 0, 256 + 4 * l:256 + 4 * l + 4], const[:, K_PERM:K_PERM + P],
                          vec_all[:, l, V_GAIN:V_GAIN + 4], start=True, stop=True).then_inc(turned.sem, 1)
            pe.wait_ge(*evicted(0, 2 * DEPTH - 1))
            pe.wait_ge(*cond_ready(0, 1))
            for j in range(4):
                for k in (2 * j, 2 * j + 1):
                    pe.wait_ge(*start_in[k % 6](0, k // 6))
                    if k >= 4:
                        pe.wait_ge(*next_ready(0, k - 4 - 8))
                    mod_matmul(start_bank[k % 4], start_slot(k), next_sum.sem)
                for k in (2 * j, 2 * j + 1):
                    pe.wait_ge(*next_row_ready(0, k - 8))
                    mod_turn(start_bank[k % 4], next_row[:, k % 2, :], next_col.sem)
                if j == 0:
                    statistics(0, 0)
                    broadcast(0, 0)
                    three_units(0, N_Q, lambda k: h_ready(0, k), range(2))
                if j > 1:
                    three_units(0, N_Q, lambda k: h_ready(0, k), range(2 * j - 2, 2 * j))
            three_units(0, N_Q, lambda k: h_ready(0, k), range(6, 8))

            with pe.Fori(0, DEPTH) as l:
                reader.clear()
                for n in range(0, 3):
                    after(l, n)
                for n in range(3, N_AC):
                    if n == N_G + 4:
                        pe.wait_ge(*conv_split(l, CC - 1))
                    if n == N_G + 16 + 4:
                        pe.wait_ge(*pool_split(l, CC - 1))
                    if n >= 5 and UNITS[n - 5]["kind"] == "pv":
                        pe.wait_ge(*pool_split(l, UNITS[n - 5]["i"]))
                    unit(l, n)
                    after(l, n)
                with pe.Fori(0, 2) as it:
                    for n in range(N_AC, N_AC + 16):
                        if n == N_AC + 4:
                            pe.wait_ge(*attn_ready(l, 11 + it * 12))
                        unit(l, n, it, 16)
                        after(l, n, it)
                three_units(l, N_O, lambda k: merged_split(l, k))
                for n in range(N_O + 3, N_F):
                    unit(l, n)
                def late(x):
                    pe.wait_ge(*late_in[x](l, 0))
                    if x == 3:
                        pe.wait_ge(*x_ready(l, 7))
                    mod_matmul(late_bank[x], late_w[x], mod_sum.sem)

                late(0)
                late(1)
                statistics(l, 1)
                late(2)
                broadcast(l, 1)
                late(3)
                for j in range(4):
                    pe.wait_ge(*mod_row_ready(l, 12 + j))
                    mod_turn(late_bank[j], late_row[j], mod_col.sem)
                three_units(l, N_F, lambda k: h_ready(l, 8 + k))
                unit(l, N_F + 3)
                with pe.Fori(0, 4) as it:
                    for n in range(N_F + 4, N_F + 12):
                        unit(l, n, it, 8)
                        after(l, n, it)
                for n in range(N_F + 36, N_D):
                    unit(l, n)
                    after(l, n)
                for n in range(N_D, U):
                    if n < N_D + 8 and n % 2 == 0:
                        pe.wait_ge(*ff_split(l, UNITS[n]["k0"] + UNITS[n]["K"] - 1))
                    unit(l, n)
                with pe.If(l < DEPTH - 1):
                    def tail(x):
                        pe.wait_ge(*tail_in[x](l, 0))
                        mod_matmul(next_bank[1 + x], next_w[1 + x], next_sum.sem)

                    pe.wait_ge(*next_ready(l, 4))
                    tail(0)
                    tail(1)
                    statistics(l + 1, 0)
                    tail(2)
                    broadcast(l + 1, 0)
                    for j in range(1, 4):
                        pe.wait_ge(*next_row_ready(l, 4 + j))
                        mod_turn(next_bank[j], row_of[j], next_col.sem)
                    three_units(l + 1, N_Q, lambda k: h_ready(l + 1, k))

            pe.wait_ge(*x_ready(DEPTH - 1, 15))
            for k in range(2 * TT):
                if k >= RING:
                    pe.wait_ge(*result_out[k % 2](0, (k - RING) // 2))
                for c in range(4):
                    ins = pe.transpose(bank[:, k % RING, P * c:P * c + P],
                                       x[:, 4 * (k % 2) + c, P * (k // 2):P * (k // 2) + P], ident)
                ins.then_inc(turned.sem, 1)

        @block.scalar
        def _(act):
            def split(l, n, it=0, per=0):
                u = UNITS[n]
                s = u["slab"]
                act.wait_ge(*slab_in[s % RING](l, s // RING + it * (per // 2 // RING)))
                act.wait_ge(*unit_done(l, n - RING + it * per))
                to, src = weights_of(n, w_hi)
                act.copy(to, src).then_inc(hi_ready.sem, 1)

            def post(l, n, it=0, per=0):
                u = UNITS[n]
                kind, i = u["kind"], u["i"]
                ps = bank[:, n % RING, 0:T]
                if kind in ("out", "proj", "b", "gc"):
                    if kind == "b":
                        k = i + it * 4
                        act.wait_ge(*ff_prod(l, k))
                        c = bass.ds(k, 1) if per else slice(i, i + 1)
                        act.mul(f_hi[:, c, :].rearrange("p a t -> p (a t)"), ff_f[:, i % 2, :], 0.5).then_inc(ff_hi.sem, 1)
                    if kind == "out":
                        square(l, i)
                    return
                if kind == "down":
                    if u["last"]:
                        square(l, 8 + i)
                    return
                act.wait_ge(*unit_done(l, n + it * per))
                if kind == "norm":
                    if i >= 2:
                        act.wait_ge(*q_stat(l, i - 2))
                    act.activation(q_sq[:, i % 2, :], ps, ACT.Square)
                    if i >= 3:
                        act.wait_ge(*q_mixed(l, i - 3))
                    act.copy(q_raw[:, i % 3, :], ps).then_inc(q_copied.sem, 1)
                elif kind == "v":
                    act.copy(v_t[:, i, :], ps).then_inc(v_copied.sem, 1)
                elif kind == "u":
                    act.copy(cu[:, i % 2, :], ps).then_inc(conv_in.sem, 1)
                elif kind == "gb":
                    act.copy(cgb[:, i % 2, :], ps).then_inc(conv_in.sem, 1)
                elif kind == "pv":
                    if i == 0:
                        act.wait_ge(*pads_zeroed(l, 1))
                    if i >= 2:
                        act.wait_ge(*pooled(l, i - 2))
                    act.copy(pin[:, i % 2, 16:16 + T_LAT], ps[:, LAT])
                    act.copy(pin[:, i % 2, 32 + T_LAT:32 + T], ps[:, CTX]).then_inc(pool_in.sem, 1)
                elif kind == "gate":
                    if n == N_G:
                        act.wait_ge(*conv_ready(l, CC - 1))
                    if i >= 12:
                        act.wait_ge(*merge_done(l, i - 12 + it * 8))
                    elif i >= 4:
                        act.wait_ge(*merge_begun(l, i - 4))
                    act.activation(gate_t[:, i % 4, :], ps, ACT.Tanh, scale=0.5).then_inc(gate_ready.sem, 1)
                elif kind == "a":
                    act.activation(ff_t[:, i % 2, :], ps, ACT.Tanh, scale=0.5).then_inc(ff_tanh.sem, 1)

            def square(l, k):
                act.wait_ge(*x_ready(l, k))
                if k % 8 == 1:
                    act.wait_ge(*x_stat(l, k // 8))
                else:
                    act.wait_ge(*x_summed(l, (k - 2) // 8 * 7 + (k - 2) % 8))
                act.activation(x_sq[:, k % 2, :], x[:, k % 8, :], ACT.Square).then_inc(x_squared.sem, 1)

            def hook(l, what, i, it):
                if what == "load" and i >= 12:
                    act.wait_ge(*(mod_sum(l, 11) if i < 14 else unit_done(l, N_O - 1)))
                    load_mod(act, late_w[i - 12], l, slice(256 * (8 + i), 256 * (9 + i)), late_in[i - 12].sem)
                elif what == "load":
                    f, slot = mod_index(i, it), i % 2
                    if i < 2:
                        act.wait_ge(*attn_ready(l, 23))
                    if i >= 2:
                        act.wait_ge(*mod_sum(l, f - 2))
                    load_mod(act, mod_w[:, slot, :], l, bass.ds(256 * (8 + i) + it * (6 * 256), 256), mod_in[slot].sem)
                elif what == "mod":
                    f = mod_index(i, it)
                    act.wait_ge(*mod_sum(l, f))
                    if i >= 2:
                        act.wait_ge(*mod_col(l, f - 2))
                    act.copy(mod_row[:, i % 2, :], sc[:, i % 2, 0:2 * P]).then_inc(mod_row_ready.sem, 1)
                elif what == "load_next" and i < 5:
                    if i or not isinstance(it, int):
                        act.wait_ge(*next_sum(l, i + it - 1))
                    load_mod(act, next_w[0], (l + 1) % DEPTH, bass.ds(256 * i + it * 256, 256), next_in.sem)
                elif what == "load_next":
                    act.wait_ge(*(next_sum(l, 4) if i == 6 else ff_split(l, FC - 1)))
                    load_mod(act, next_w[i - 4], (l + 1) % DEPTH, slice(256 * i, 256 * i + 256), tail_in[i - 5].sem)
                elif what == "mod_next":
                    act.wait_ge(*next_sum(l, i + it))
                    act.wait_ge(*next_col(l, i + it - 1))
                    act.copy(row_of[0], next_bank[0][:, 0:2 * P]).then_inc(next_row_ready.sem, 1)
                elif what == "kout":
                    act.wait_ge(*k_turned(l, i))
                    act.copy(k_out[:, i, :], tr[:, 0, 0:P]).then_inc(k_out_ready.sem, 1)
                elif what == "cache":
                    act.wait_ge(*past_turned(l, i))
                    act.copy(k_hi[:, i, 0:PAST], tr[:, 0, 0:P]).then_inc(past_hi.sem, 1)
                elif what == "split":
                    act.wait_ge(*(k_ready(l, i) if i < 2 else q_mixed(l, i)))
                    to, src = qk_of(i)
                    act.copy(to[0], src).then_inc(qk_hi.sem, 1)
                elif what == "scores":
                    act.wait_ge(*max_ready(l, i))
                    if i >= 2:
                        act.wait_ge(*probs_turned(l, i - 2))
                    nk = PAST + T_LAT if i % 3 < 2 else T_CTX
                    c = 2 + 4 * (i // 12) + i % 12 // 3
                    for g in range(2):
                        r = 2 * (i % 3) + g
                        ins = act.activation(prob[:, i % 2, g, 0:nk], sc[:, g, 0:nk], ACT.Exp, scale=q_rs[:, c, r:r + 1],
                                             bias=s_nm[i % 2][:, g:g + 1], accum_out=s_sum[i % 2][:, g:g + 1])
                    ins.then_inc(exps.sem, 1)
                    if i >= 12:
                        act.activation(s_se, s_sd, ACT.Exp).then_inc(sink_exp.sem, 1)
                elif what == "probsT":
                    act.wait_ge(*probs_turned(l, i))
                    if i == 1:
                        act.wait_ge(*kv_stored(l, 0))
                    if i >= 2:
                        act.wait_ge(*attn_out(l, i - 2))
                    nb = 3 if i % 3 < 2 else 1
                    act.copy(prob_t[:, i % 2, :, 0:nb, :], tr[:, :, 0:P * nb].rearrange("p g (b q) -> p g b q", b=nb))\
                        .then_inc(probs_t_ready.sem, 1)
                elif what == "attn":
                    m, c, t = i // 12, i % 12 // 3, i % 3
                    act.wait_ge(*attn_out(l, i))
                    act.copy(br_hi[:, 8 + 4 * m + c, P * t:P * t + P], tr[:, 0, 384:512]).then_inc(attn_hi.sem, 1)
                elif what == "conv":
                    act.wait_ge(*conv_ready(l, i))
                    act.copy(br_hi[:, i, LAT], cy[:, i % 2, 0:T_LAT])
                    act.copy(br_hi[:, i, CTX], cy[:, i % 2, T_LAT + 1:T + 1]).then_inc(conv_hi.sem, 1)
                elif what == "poolsplit":
                    act.wait_ge(*pooled(l, i))
                    n = BASE["pv"] + 8 * (i // 2) + i % 2
                    act.activation(br_hi[:, 4 + i, :], bank[:, (n + 1) % RING, 0:T], ACT.Identity,
                                   scale=vec[:, V_PSC + i:V_PSC + i + 1]).then_inc(pool_hi.sem, 1)

            def norm(l, which, start=None):
                shift = (M_SH1, M_SH2)[which]
                for d in range(DC):
                    if which == 0 and d % 2 == 0:
                        if d and start:
                            start(d // 2)
                        act.wait_ge(*gain_ready(l, d // 2))
                    elif d == 0:
                        act.wait_ge(*gain_ready(l, 4))
                    act.wait_ge(*x_normed(l, 8 * which + d))
                    for c, part in enumerate((LAT, CTX)):
                        ins = act.activation(h_hi[:, d, part], nx[:, d % 4, part], ACT.Identity,
                                             scale=gain[:, which, d, c:c + 1], bias=modc[:, shift + d, c:c + 1])
                    ins.then_inc(h_hi_ready.sem, 1)

            def slot(l, n, it=0, per=0):
                if n + LOOKAHEAD >= U:
                    with act.If(l < DEPTH - 1):
                        split(l + 1, n + LOOKAHEAD - U)
                else:
                    split(l, n + LOOKAHEAD, it, per)
                run_hooks(act, l, n, it, hook, ("load_next", "mod_next"), MID[n])
                post(l, n, it, per)

            for t in range(TT):
                rows = io["x_sample"][0, P * t:P * t + P, :] if t < 2 else io["x_prompt"][0]
                act.dma_start(tok[:, t, :], rows).then_inc(tok_in.sem, 16)
            for k in range(DC):
                if k == 4:
                    act.wait_ge(*turned(0, DC))
                    act.activation(cond_t[:, 0, :], tr[:, 1, 0:2 * DC], ACT.Tanh, scale=0.5).then_inc(cond_tanh.sem, 1)
                    act.copy(cond_t[:, 1, :], tr[:, 1, 0:2 * DC]).then_inc(cond_tanh.sem, 1)
                act.wait_ge(*x_ready(0, k - 8))
                if k >= 2:
                    act.wait_ge(*x_summed(0, k - 2 - 7))
                act.activation(x_sq[:, k % 2, :], x[:, k, :], ACT.Square).then_inc(x_squared.sem, 1)

            def start(j):
                for k in (2 * j, 2 * j + 1):
                    act.wait_ge(*next_sum(0, k - 8))
                    if k >= 2:
                        act.wait_ge(*next_col(0, k - 2 - 8))
                    act.copy(next_row[:, k % 2, :], start_bank[k % 4][:, 0:2 * P]).then_inc(next_row_ready.sem, 1)

            start(0)
            for n in range(LOOKAHEAD):
                split(0, n)
            norm(0, 0, start)

            with act.Fori(0, DEPTH) as l:
                for n in range(0, N_AC):
                    slot(l, n)
                with act.Fori(0, 2) as it:
                    for n in range(N_AC, N_AC + 16):
                        slot(l, n, it, 16)
                for d in range(DC):
                    act.wait_ge(*merge_done(l, 16 + d))
                    act.mul(br_hi[:, d, :], merged[:, d, :], 0.5).then_inc(merged_hi.sem, 1)
                for n in range(N_O, N_F):
                    slot(l, n)
                for j in range(4):
                    act.wait_ge(*mod_sum(l, 12 + j))
                    act.copy(late_row[j], late_bank[j][:, 0:2 * P]).then_inc(mod_row_ready.sem, 1)
                norm(l, 1)
                for n in range(N_F, N_F + 4):
                    slot(l, n)
                with act.Fori(0, 4) as it:
                    for n in range(N_F + 4, N_F + 12):
                        slot(l, n, it, 8)
                for n in range(N_F + 36, U):
                    slot(l, n)
                with act.If(l < DEPTH - 1):
                    for j in range(1, 4):
                        act.wait_ge(*next_sum(l, 4 + j))
                        if j == 1:
                            act.wait_ge(*next_col(l, 4))
                        act.copy(row_of[j], next_bank[j][:, 0:2 * P]).then_inc(next_row_ready.sem, 1)
                    norm(l + 1, 0)

            for k in range(1, 2 * TT, 2):
                act.wait_ge(*turned(0, 1 + DC + 2 * DEPTH + k))
                act.copy(tok[:, k // 2, D // 2:], bank[:, k % RING, :]).then_inc(result_out[1].sem, 1)

        @block.vector
        def _(dve):
            chain = Steps(dve_step, sizes, "dve")

            def split(l, n, it=0, per=0):
                dve.wait_ge(*hi_ready(l, n + it * per))
                to, src = weights_of(n, w_lo)
                hi, _ = weights_of(n, w_hi)
                dve.tensor_tensor(to, src, hi.bitcast(F32), ALU.subtract).then_inc(lo_ready.sem, 1)

            def lo_part(to, x_, hi, scale=None):
                if scale is None:
                    return dve.tensor_tensor(to, x_, hi.bitcast(F32), ALU.subtract)
                return dve.scalar_tensor_tensor(to, x_, scale, hi.bitcast(F32), ALU.mult, ALU.subtract)

            def residual(l, n, k):
                u = UNITS[n]
                b = (u["i"] % 4) if u["kind"] == "down" else n % RING
                g = (M_G1 if k < 8 else M_G2) + k % 8
                for c, part in enumerate((LAT, CTX)):
                    xs = x[:, k % 8, part]
                    ins = dve.scalar_tensor_tensor(xs, bank[:, b, part], modc[:, g, c:c + 1], xs, ALU.mult, ALU.add)
                ins.then_inc(x_ready.sem, 1)

            def before_split(l, n, it, per):
                u = UNITS[n]
                kind, i = u["kind"], u["i"]
                ps = bank[:, n % RING, 0:T]
                if kind == "out":
                    dve.wait_ge(*unit_done(l, n))
                    residual(l, n, i)
                elif kind == "down" and u["last"]:
                    dve.wait_ge(*unit_done(l, n))
                    residual(l, n, 8 + i)
                elif kind == "b":
                    dve.wait_ge(*unit_done(l, n + it * per))
                    dve.wait_ge(*ff_made[i % 2])
                    dve.tensor_tensor(ff_f[:, i % 2, :], ff_s[:, i % 2, :], ps, ALU.mult).then_inc(ff_prod.sem, 1)
                elif kind == "gc":
                    dve.wait_ge(*unit_done(l, n))
                    dve.wait_ge(*conv_in(l, 4 * (i // 2) + 3))
                    if i == 0:
                        dve.wait_ge(*pads_zeroed(l, 1))
                    dve.tensor_tensor(cz[:, 1:1 + T_LAT], cu[:, i % 2, LAT], ps[:, LAT], ALU.mult)
                    made["z"] = chain.made(dve.tensor_tensor(cz[:, 2 + T_LAT:2 + T], cu[:, i % 2, CTX], ps[:, CTX], ALU.mult))
                elif kind == "proj":
                    b, d = i // 8, i % 8
                    dve.wait_ge(*unit_done(l, n + it * per))
                    dve.wait_ge(*gate_ready(l, i + it * 8))
                    t = gate_t[:, d % 4, :]
                    if b == 0:
                        dve.scalar_tensor_tensor(merged[:, d, :], t, 1.0, ps, ALU.add, ALU.mult).then_inc(merge_begun.sem, 1)
                    else:
                        dve.scalar_tensor_tensor(t, t, 1.0, ps, ALU.add, ALU.mult).then_inc(merge_product.sem, 1)

            def after_split(l, n, it, per):
                u = UNITS[n]
                kind, i = u["kind"], u["i"]
                ps = bank[:, n % RING, 0:T]
                if kind == "a":
                    dve.wait_ge(*ff_tanh(l, i + it * 4))
                    ff_made[i % 2] = chain.made(dve.scalar_tensor_tensor(
                        ff_s[:, i % 2, :], ff_t[:, i % 2, :], 1.0, ps, ALU.add, ALU.mult))
                elif kind == "b":
                    k = i + it * 4
                    dve.wait_ge(*ff_hi(l, k))
                    c = bass.ds(k, 1) if per else slice(i, i + 1)
                    lo_part(f_lo[:, c, :].rearrange("p a t -> p (a t)"), ff_f[:, i % 2, :],
                            f_hi[:, c, :].rearrange("p a t -> p (a t)"), 0.5).then_inc(ff_split.sem, 1)
                elif kind == "gc":
                    y, n1 = cy[:, i % 2, :], ZL - 2
                    tap = [vec[:, V_CONV + 4 * r + i:V_CONV + 4 * r + i + 1] for r in range(3)]
                    dve.wait_ge(*made["z"])
                    if i >= 2:
                        dve.wait_ge(*conv_split(l, i - 2))
                        dve.wait_ge(*conv_hi(l, i - 2))
                    s = chain.made(dve.tensor_scalar(y[:, 0:n1], cz[:, 1:1 + n1], tap[1], None, ALU.mult))
                    dve.wait_ge(*s)
                    s = chain.made(dve.scalar_tensor_tensor(y[:, 0:n1], cz[:, 0:n1], tap[0], y[:, 0:n1], ALU.mult, ALU.add))
                    dve.wait_ge(*s)
                    s = chain.made(dve.scalar_tensor_tensor(y[:, 0:n1], cz[:, 2:2 + n1], tap[2], y[:, 0:n1], ALU.mult, ALU.add))
                    dve.wait_ge(*s)
                    dve.tensor_tensor(y[:, 0:T_LAT], y[:, 0:T_LAT], cgb[:, i % 2, LAT], ALU.mult)
                    dve.tensor_tensor(y[:, T_LAT + 1:T + 1], y[:, T_LAT + 1:T + 1], cgb[:, i % 2, CTX], ALU.mult)\
                        .then_inc(conv_ready.sem, 1)

            def mod_columns(c, src, t, b, summed, done):
                tiles = src[:, 0:2 * P].rearrange("p (y j c) -> p y c j", y=2, j=4)[:, :, 0:2, :]
                dve.reduce_sum(mod_t[:, t, :, :], tiles, AXX).then_inc(summed[0], 1)
                dve.wait_ge(*summed)
                dve.tensor_tensor(modc[:, c, :], mod_t[:, t, :, :], b.unsqueeze(2).broadcast_to([P, 2, 2]), ALU.add)\
                    .then_inc(done, 1)

            def hook(l, what, i, it):
                if what == "sel":
                    dve.wait_ge(*mod_col(l, mod_index(i, it)))
                    c = 16 + 2 * i + it * 12
                    mod_columns(bass.ds(c, 2), sc[:, i % 2, :], i % 2, vec[:, bass.ds(c, 2)],
                                mod_added(l, mod_index(i, it)), mod_ready.sem)
                elif what == "sel_next":
                    dve.wait_ge(*next_col(l, i + it))
                    c = bass.ds(2 * i + it * 2, 2)
                    b = vec_all[:, bass.ds((l + 1) % DEPTH, 1), c].rearrange("p a v -> p (a v)")
                    mod_columns(c, next_bank[0], 5, b, next_added(l, i + it), next_ready.sem)
                elif what == "stat":
                    g = i if i < 2 else (i - 2) // 4
                    gi = V_GAIN + (2 * g + 1 if i < 2 else 2 * g)
                    own, other = vec[:, gi:gi + 1], vec[:, gi + 4:gi + 5]
                    dve.wait_ge(*q_stat(l, i))
                    if i >= 2:
                        dve.wait_ge(*q_rs_ready(l, i - 2))
                    ms = tr[:, 1, T_LAT:T_LAT + 6]
                    if i < 2:
                        dve.tensor_scalar(q_ms[i % 2], ms, EPS, None, ALU.add).then_inc(q_ms_ready.sem, 1)
                    else:
                        dve.tensor_scalar(q_ms[i % 2], ms, EPS, SCALE ** -2, ALU.add, ALU.mult).then_inc(q_ms_ready.sem, 1)
                    _, mix = qk_of(i)
                    if i >= 4:
                        dve.wait_ge(*qk_split(l, i - 2))
                    chain.made(dve.scalar_tensor_tensor(q_rot[:, :], tr[:, 1, 0:T_LAT], other,
                                                        const[:, K_SIN:K_SIN + T_LAT], ALU.mult, ALU.mult))
                    chain.made(dve.scalar_tensor_tensor(mix[:, LAT], q_raw[:, i % 3, LAT], own,
                                                        const[:, K_COS:K_COS + T_LAT], ALU.mult, ALU.mult))
                    s = chain.made(dve.tensor_scalar(mix[:, CTX], q_raw[:, i % 3, CTX], own, None, ALU.mult))
                    dve.wait_ge(*s)
                    dve.tensor_tensor(mix[:, LAT], mix[:, LAT], q_rot[:, :], ALU.add).then_inc(q_mixed.sem, 1)
                elif what == "rnorm":
                    _, mix = qk_of(i)
                    dve.wait_ge(*q_bcast(l, i))
                    dve.wait_ge(*q_mixed(l, i))
                    dve.tensor_tensor(mix, mix, tr[:, 0, 0:T], ALU.mult).then_inc(k_ready.sem, 1)
                elif what == "cache":
                    dve.wait_ge(*past_hi(l, i))
                    lo_part(k_lo[i][:, 0:PAST], tr[:, 0, 0:P], k_hi[:, i, 0:PAST]).then_inc(past_split.sem, 1)
                elif what == "split":
                    dve.wait_ge(*qk_hi(l, i))
                    to, src = qk_of(i)
                    lo_part(to[1], src, to[0]).then_inc(qk_split.sem, 1)
                elif what == "vt":
                    dve.wait_ge(*v_turned(l, i))
                    dve.tensor_copy(vals[:, i, 1:1 + TT, :], tr[:, 0, 0:T].rearrange("p (t c) -> p t c", c=P))\
                        .then_inc(v_ready.sem, 1)
                elif what == "scores":
                    m, t = i // 12, i % 3
                    nk = PAST + T_LAT if t < 2 else T_CTX
                    dve.wait_ge(*scores(l, i))
                    if m == 1 and t < 2:
                        at = PAST + P * (1 - t)
                        blk = sc[:, :, at:at + P]
                        mask = const[:, K_MASK + P * t:K_MASK + P * t + P].unsqueeze(1).broadcast_to([P, 2, P])
                        s = chain.made(dve.tensor_tensor(blk, blk, mask, ALU.add))
                        dve.wait_ge(*s)
                    s = chain.made(dve.reduce_max(s_max, sc[:, :, 0:nk], AXX))
                    dve.wait_ge(*s)
                    nm, c = s_nm[i % 2], i % 12 // 3
                    rs = q_rs[:, 2 + 4 * m + c, 2 * t:2 * t + 2]
                    dve.wait_ge(*q_rs_ready(l, 2 + 4 * m + c))
                    negated = dve.scalar_tensor_tensor(nm, s_max, -1.0, rs, ALU.mult, ALU.mult)
                    if m == 0:
                        negated.then_inc(max_ready.sem, 1)
                    else:
                        two = nsink[:, c:c + 5:4]
                        dve.wait_ge(*chain.made(negated))
                        s = chain.made(dve.tensor_tensor(nm, nm, two, ALU.min))
                        dve.wait_ge(*s)
                        dve.tensor_tensor(s_sd, nm, two, ALU.subtract).then_inc(max_ready.sem, 1)
                elif what == "scale":
                    nk = PAST + T_LAT if i % 3 < 2 else T_CTX
                    dve.wait_ge(*exps(l, i))
                    total = s_sum[i % 2]
                    if i >= 12:
                        dve.wait_ge(*sink_exp(l, i - 12))
                        s = chain.made(dve.tensor_tensor(total, total, s_se, ALU.add))
                        dve.wait_ge(*s)
                    s = chain.made(dve.reciprocal(s_r, total))
                    dve.wait_ge(*s)
                    for g in range(2):
                        v = prob[:, i % 2, g, 0:nk]
                        ins = dve.tensor_scalar(v, v, s_r[:, g:g + 1], None, ALU.mult)
                    ins.then_inc(probs_ready.sem, 1)
                elif what == "attn":
                    m, c, t = i // 12, i % 12 // 3, i % 3
                    part = slice(P * t, P * t + P)
                    dve.wait_ge(*attn_hi(l, i))
                    lo_part(br_lo[:, 8 + 4 * m + c, part], tr[:, 0, 384:512], br_hi[:, 8 + 4 * m + c, part])\
                        .then_inc(attn_ready.sem, 1)
                elif what == "conv":
                    dve.wait_ge(*conv_hi(l, i))
                    lo_part(br_lo[:, i, LAT], cy[:, i % 2, 0:T_LAT], br_hi[:, i, LAT])
                    lo_part(br_lo[:, i, CTX], cy[:, i % 2, T_LAT + 1:T + 1], br_hi[:, i, CTX]).then_inc(conv_split.sem, 1)
                elif what == "pooldiff":
                    p, w = pin[:, i % 2, :], POOL_SIZES[i]
                    src = sums_of(w)
                    dve.wait_ge(*window_sums(l, i))
                    for at, m in ((16, T_LAT), (32 + T_LAT, T_CTX)):
                        ins = dve.scalar_tensor_tensor(p[:, at:at + m], src[:, at:at + m], 1.0 / w, p[:, at:at + m],
                                                       ALU.mult, ALU.subtract)
                    ins.then_inc(pool_ready.sem, 1)
                elif what == "poolsplit":
                    n = BASE["pv"] + 8 * (i // 2) + i % 2
                    dve.wait_ge(*pool_hi(l, i))
                    lo_part(br_lo[:, 4 + i, :], bank[:, (n + 1) % RING, 0:T], br_hi[:, 4 + i, :],
                            vec[:, V_PSC + i:V_PSC + i + 1]).then_inc(pool_split.sem, 1)

            def mean_square(l, which):
                dve.wait_ge(*x_stat(l, which))
                dve.tensor_scalar(x_ms, tr[:, 0, 0:TT], EPS, None, ALU.add).then_inc(x_ms_ready.sem, 1)

            def norm(l, which, start=None, late=0):
                sc_, g_ = (M_SC1, M_SC2)[which], (V_GMIX, V_GFFN)[which]
                shift, full = (M_SH1, M_SH2)[which], {}

                def gains(d, n, columns_in, k):
                    dve.wait_ge(*columns_in)
                    dve.scalar_tensor_tensor(gain[:, which, d:d + n, :], modc[:, sc_ + d:sc_ + d + n, :], 1.0,
                                             vec[:, g_ + d:g_ + d + n].unsqueeze(2).broadcast_to([P, n, 2]),
                                             ALU.add, ALU.mult).then_inc(gain_ready.sem, 1)
                    dve.wait_ge(*gain_ready(l, k))

                def normed(d):
                    if d >= 4:
                        dve.wait_ge(*h_hi_ready(l, 8 * which + d - 4))
                    dve.tensor_tensor(nx[:, d % 4, :], x[:, d, :], tr[:, 0, 0:T], ALU.mult).then_inc(x_normed.sem, 1)

                def whole(d):
                    dve.wait_ge(*x_normed(l, 8 * which + d))
                    for c, part in enumerate((LAT, CTX)):
                        ins = dve.tensor_scalar(nf[:, d % 4, part], nx[:, d % 4, part], gain[:, which, d, c:c + 1],
                                                modc[:, shift + d, c:c + 1], ALU.mult, ALU.add)
                    full[d] = chain.made(ins)

                def low(d):
                    dve.wait_ge(*full[d])
                    dve.wait_ge(*h_hi_ready(l, 8 * which + d))
                    lo_part(h_lo[:, d, :], nf[:, d % 4, :], h_hi[:, d, :]).then_inc(h_ready.sem, 1)

                if which:
                    gains(0, DC, mod_ready(l, 11), 4)
                for d in range(DC + 1):
                    if which == 0 and d % 2 == 0 and d < DC:
                        if d:
                            low(d - 1)
                            if start:
                                start(d // 2)
                        gains(d, 2, next_ready(l, (d // 2 + late if late else d + 1) - 8), d // 2)
                    if d == 0:
                        dve.wait_ge(*x_bcast(l, which))
                    if d < DC:
                        normed(d)
                    if d and (which or d % 2 or d == DC):
                        low(d - 1)
                    if d < DC:
                        whole(d)

            def slot(l, n, it=0, per=0):
                first = UNITS[n]["kind"] == "down" or (UNITS[n]["kind"] == "out" and n != N_O)
                if first:
                    before_split(l, n, it, per)
                if n + LOOKAHEAD >= U:
                    with dve.If(l < DEPTH - 1):
                        split(l + 1, n + LOOKAHEAD - U)
                else:
                    split(l, n + LOOKAHEAD, it, per)
                run_hooks(dve, l, n, it, hook, ("sel_next",), MID[n])
                if not first:
                    before_split(l, n, it, per)
                after_split(l, n, it, per)

            made, ff_made = {}, {}

            dve.nop().then_inc(lo_ready.sem, 8)
            for k in range(DC):
                dve.wait_ge(*turned(0, k))
                dve.tensor_copy(x[:, k, :], bank[:, k % RING, 0:T]).then_inc(x_ready.sem, 1)
            s = chain.made(dve.memset(cond[:, :, :], 0.0))
            dve.wait_ge(*cond_tanh(0, 1))
            s = chain.made(dve.scalar_tensor_tensor(cond_t[:, 0, :], cond_t[:, 0, :], 1.0, cond_t[:, 1, :], ALU.add, ALU.mult))
            dve.wait_ge(*s)
            for c in range(2):
                dve.tensor_scalar(cond[:, :, c], cond_t[:, 0, DC * c:DC * c + DC], 0.5, None, ALU.mult)\
                    .then_inc(cond_ready.sem, 1)
            for l in range(DEPTH):
                dve.wait_ge(*turned(0, 1 + DC + 2 * l))
                dve.tensor_copy(vec_all[:, l, 0:NV], tr[:, 0, P * l:P * l + NV]).then_inc(evicted.sem, 1)
                dve.wait_ge(*turned(0, 2 + DC + 2 * l))
                dve.tensor_copy(vec_all[:, l, NV:NVX], tr[:, 0, 256 + 4 * l:256 + 4 * l + 4]).then_inc(evicted.sem, 1)
            dve.wait_ge(*evicted(0, 2 * DEPTH - 1))
            dve.wait_ge(*vectors_in(0, 9))

            def vectors(l, at):
                dve.tensor_copy(vec[:, :], vec_all[:, bass.ds(at, 1), :].rearrange("p a v -> p (a v)"))\
                    .then_inc(vec_ready.sem, 1)
                dve.wait_ge(*vec_ready(l, 0))
                s = chain.made(dve.tensor_scalar(nsink[:, :], sink[:, bass.ds(at, 1), :].rearrange("p a v -> p (a v)"),
                                                 -1.0, None, ALU.mult))
                dve.wait_ge(*s)

            def start(j):
                for k in (2 * j, 2 * j + 1):
                    g = start_group(k)
                    dve.wait_ge(*next_col(0, k - 8))
                    mod_columns(slice(2 * g, 2 * g + 2), start_bank[k % 4], 2 + k % 4, vec_all[:, 0, 2 * g:2 * g + 2],
                                next_added(0, k - 8), next_ready.sem)

            vectors(0, 0)
            start(0)
            mean_square(0, 0)
            for n in range(LOOKAHEAD):
                split(0, n)
            norm(0, 0, start)

            dve.wait_ge(*loaded_all(0, 0))
            with dve.Fori(0, DEPTH) as l:
                chain.enter("layer", l)
                for n in range(0, N_AC):
                    slot(l, n)
                with dve.Fori(0, 2) as it:
                    chain.enter("branches", it)
                    for n in range(N_AC, N_AC + 16):
                        slot(l, n, it, 16)
                    chain.leave(2)
                for d in range(DC):
                    dve.wait_ge(*merged_hi(l, d))
                    lo_part(br_lo[:, d, :], merged[:, d, :], br_hi[:, d, :], 0.5).then_inc(merged_split.sem, 1)
                for n in range(N_O, N_F):
                    slot(l, n)
                mean_square(l, 1)
                norm(l, 1)
                for j in range(4):
                    dve.wait_ge(*mod_col(l, 12 + j))
                    mod_columns(slice(40 + 2 * j, 42 + 2 * j), late_bank[j], 2 + j, vec[:, 40 + 2 * j:42 + 2 * j],
                                mod_added(l, 12 + j), mod_ready.sem)
                for n in range(N_F, N_F + 4):
                    slot(l, n)
                with dve.Fori(0, 4) as it:
                    chain.enter("ffn", it)
                    for n in range(N_F + 4, N_F + 12):
                        slot(l, n, it, 8)
                    chain.leave(4)
                for n in range(N_F + 36, U):
                    slot(l, n)

                def tail(j):
                    dve.wait_ge(*next_col(l, 4 + j))
                    mod_columns(slice(8 + 2 * j, 10 + 2 * j), next_bank[j], 1 + j, vec[:, 8 + 2 * j:10 + 2 * j],
                                next_added(l, 4 + j), next_ready.sem)

                with dve.If(l < DEPTH - 1):
                    mean_square(l + 1, 0)
                    vectors(l + 1, (l + 1) % DEPTH)
                    norm(l + 1, 0, tail, 4)
                chain.leave(DEPTH)

            for k in range(0, 2 * TT, 2):
                dve.wait_ge(*turned(0, 1 + DC + 2 * DEPTH + k))
                dve.tensor_copy(tok[:, k // 2, 0:D // 2], bank[:, k % RING, :]).then_inc(result_out[0].sem, 1)

        @block.gpsimd
        def _(pool):
            chain = Steps(pool_step, sizes, "pool")

            def add_square(l, k):
                if k % 8 in (0, 7):
                    return
                pool.wait_ge(*x_squared(l, k))
                if k % 8 == 1:
                    pool.tensor_tensor(x_acc[:, :], x_sq[:, 0, :], x_sq[:, 1, :], ALU.add).then_inc(x_summed.sem, 2)
                    return
                pool.wait_ge(*x_summed(l, k // 8 * 7 + k % 8 - 1))
                pool.tensor_tensor(x_acc[:, :], x_acc[:, :], x_sq[:, k % 2, :], ALU.add).then_inc(x_summed.sem, 1)

            def window(l, i):
                p, w = pin[:, i % 2, :], POOL_SIZES[i]
                pool.wait_ge(*pool_in(l, i))
                if i:
                    pool.wait_ge(*pool_ready(l, i - 1))
                s = chain.made(pool.tensor_tensor(ps_a[:, 1:PL], p[:, 0:PL - 1], p[:, 1:PL], ALU.add))
                src, dst, size, lo = ps_a, ps_b, 2, 1
                while size < w:
                    hf = size // 2
                    pool.wait_ge(*s)
                    a, b = lo + hf, PL - (size - 1)
                    s = chain.made(pool.tensor_tensor(dst[:, a:b], src[:, a - hf:b - hf], src[:, a + hf:b + hf], ALU.add))
                    src, dst, size, lo = dst, src, 2 * size, a
                pool.wait_ge(*s)
                edge = const[:, K_EDGE + 32 * i:K_EDGE + 32 * i + 32].rearrange("p (s e) -> p s e", e=8)
                for sq_, at, step in ((0, 16, T_LAT - 8), (1, 32 + T_LAT, T_CTX - 8)):
                    for e in range(2):
                        v = src[:, at + e * step:at + e * step + 8]
                        ins = pool.tensor_tensor(v, v, edge[:, 2 * sq_ + e, :], ALU.mult)
                ins.then_inc(window_sums.sem, 1)

            def merge(l, i, it):
                d = i % 8
                pool.wait_ge(*merge_product(l, i + it * 8))
                pool.wait_ge(*merge_begun(l, d))
                if i >= 8:
                    pool.wait_ge(*merge_done(l, i - 8 + it * 8))
                m = merged[:, d, :]
                pool.tensor_tensor(m, m, gate_t[:, d % 4, :], ALU.add).then_inc(merge_done.sem, 1)

            def rms(l, which):
                pool.wait_ge(*x_ms_ready(l, which))
                pool.tensor_tensor(x_rs, x_ms, exponent[:, 0:1].broadcast_to([P, TT]), ALU.pow).then_inc(x_rs_ready.sem, 1)

            pool.wait_ge(*chain.made(pool.memset(exponent[:, :], -0.5)))
            for k in range(DC):
                add_square(0, k - 8)
            rms(0, 0)
            pool.wait_ge(*loaded_all(0, 0))
            with pool.Fori(0, DEPTH) as l:
                chain.enter("layer", l)
                pool.wait_ge(*next_sum(l, -1))
                for m, name in enumerate(("attn", "win")):
                    pool.dma_start(k_past[:, m, :], io["cache_k_" + name][0, l].rearrange("t h c -> t (h c)"))\
                        .then_inc(past_in.sem, 16)
                for m, name in enumerate(("attn", "win")):
                    pool.dma_start(vals[:, m, 0, :], io["cache_v_" + name][0, l].rearrange("t h c -> t (h c)"))\
                        .then_inc(vals_in.sem, 16)
                pool.dma_start(pw[:, :, :], io["pool_w"][l].rearrange("g c e -> c g e")).then_inc(pw_in.sem, 16)
                for i in range(10):
                    pool.wait_ge(*q_ms_ready(l, i))
                    pool.tensor_tensor(q_rs[:, i, :], q_ms[i % 2], exponent[:, 0:1].broadcast_to([P, 2 * TT]), ALU.pow)\
                        .then_inc(q_rs_ready.sem, 1)
                    if i == 0:
                        pool.memset(cz[:, :], 0.0).then_inc(pads_zeroed.sem, 1)
                        pool.memset(pin[:, :, :], 0.0).then_inc(pads_zeroed.sem, 1)
                for i in range(CC):
                    window(l, i)
                for i in range(8):
                    merge(l, i, 0)
                with pool.Fori(0, 2) as it:
                    for i in range(8, 16):
                        merge(l, i, it)
                for k in range(8):
                    add_square(l, k)
                rms(l, 1)
                for k in range(8, 16):
                    add_square(l, k)
                with pool.If(l < DEPTH - 1):
                    rms(l + 1, 0)
                chain.leave(DEPTH)


SHAPES_OUT = {
    "y_prompt": (1, T_CTX, D), "y_sample": (1, T_LAT, D),
    "k_attn": (1, DEPTH, T_CTX, NKV, HD), "v_attn": (1, DEPTH, T_CTX, NKV, HD),
    "k_win": (1, DEPTH, T_CTX, NKV, HD), "v_win": (1, DEPTH, T_CTX, NKV, HD),
}


def build(make, shapes, sizes):
    nc = make()
    io = {n: nc.dram_tensor(f"in_{n}", s, F32, kind="ExternalInput").ap() for n, s in shapes.items()}
    io |= {n: nc.dram_tensor(f"out_{n}", s, F32, kind="ExternalOutput").ap() for n, s in SHAPES_OUT.items()}
    program(nc, io, sizes)
    return nc


def kernel(**inputs):
    import concourse.bacc as bacc
    from concourse.bass_utils import run_bass_kernel_spmd

    arrays = {n: np.ascontiguousarray(a) for n, a in inputs.items()}
    arrays["const"] = constants()
    shapes = {n: a.shape for n, a in arrays.items()}

    def make():
        return bacc.Bacc("TRN2", target_bir_lowering=False, num_devices=1)

    sizes = {}
    build(make, shapes, sizes)
    nc = build(make, shapes, sizes)
    r = run_bass_kernel_spmd(nc, [{f"in_{n}": a for n, a in arrays.items()}], core_ids=[0])
    return tuple(r.results[0][f"out_{n}"] for n in SHAPES_OUT)
```
